# Optimizing a Trainium2 kernel written in Bass

```python
import jax, jax.numpy as jnp
from jax import lax
import numpy as np

D_MODEL = 1024
BATCH = 1
SEQ = 1024
DEPTH = 1

CHUNK = 64
MEM_LEN = 256
D_MIX = D_MODEL
D_A = D_MIX // 2
A_GROUPS = 4
A_CH = D_A // A_GROUPS
A_BLOCK = 128
D_B = D_MIX - D_A
B_HEADS = 8
B_HEAD_DIM = D_B // B_HEADS
B_LEFT_CHUNKS = 8
B_BAND = (B_LEFT_CHUNKS + 1) * CHUNK
REL_CLIP = 128
X_HEADS = 4
X_HEAD_DIM = D_MODEL // X_HEADS
PEER_HEADS = 8
PEER_KEYS = 128
PEER_EXPERTS = PEER_KEYS * PEER_KEYS
PEER_D_KEY = 256
PEER_HALF = PEER_D_KEY // 2
PEER_TOPK = 16
PEER_TOKEN_BLOCK = 128
N_IN = 2 * D_A + 3 * D_B
DN_ALPHA = (2.0 * DEPTH) ** 0.25
DN_BETA = (8.0 * DEPTH) ** -0.25
LN_EPS = 1e-5

kernel_name = "hybrid_gmlp_chunkattn_peer_deepnorm"

def layer_norm(x, g, b):
    xf = x.astype(jnp.float32)
    mu = xf.mean(-1, keepdims=True)
    var = jnp.square(xf - mu).mean(-1, keepdims=True)
    y = (xf - mu) * lax.rsqrt(var + LN_EPS)
    return (y * g.astype(jnp.float32) + b.astype(jnp.float32)).astype(x.dtype)

def gmlp_chunk_mask():
    c = np.arange(A_BLOCK) // CHUNK
    return jnp.asarray(c[None, :] <= c[:, None])

def spatial_gating_mixer(z, ln_g, ln_b, w_sp, b_sp):
    b_, s_, _ = z.shape
    u, v = jnp.split(z, 2, axis=-1)
    v = layer_norm(v, ln_g, ln_b)
    v = v.reshape(b_, s_ // A_BLOCK, A_BLOCK, A_GROUPS, A_CH)
    w = jnp.where(gmlp_chunk_mask()[None], w_sp, 0)
    s = jnp.einsum('gij,bnjgc->bnigc', w, v) + b_sp.T[None, None, :, :, None]
    return u * s.reshape(b_, s_, D_A)

def chunk_band_attention(q, k, v, rel_bias):
    b_, s_, _ = q.shape
    nc = s_ // CHUNK
    shp = (b_, nc, CHUNK, B_HEADS, B_HEAD_DIM)
    q = q.reshape(shp)
    k = k.reshape(shp)
    v = v.reshape(shp)
    pad = ((0, 0), (B_LEFT_CHUNKS, 0), (0, 0), (0, 0), (0, 0))
    band = jnp.arange(nc)[:, None] + jnp.arange(B_LEFT_CHUNKS + 1)[None, :]
    kb = jnp.pad(k, pad)[:, band].reshape(b_, nc, B_BAND, B_HEADS, B_HEAD_DIM)
    vb = jnp.pad(v, pad)[:, band].reshape(b_, nc, B_BAND, B_HEADS, B_HEAD_DIM)
    scores = jnp.einsum('bcihd,bcmhd->bchim', q, kb).astype(jnp.float32) * (B_HEAD_DIM ** -0.5)
    qi = jnp.arange(CHUNK)[:, None]
    km = jnp.arange(B_BAND)[None, :]
    rel = jnp.clip(qi + B_LEFT_CHUNKS * CHUNK - km, -REL_CLIP, REL_CLIP) + REL_CLIP
    bias = rel_bias.astype(jnp.float32)[:, rel]
    key_pos = (jnp.arange(nc)[:, None] - B_LEFT_CHUNKS) * CHUNK + jnp.arange(B_BAND)[None, :]
    valid = key_pos >= 0
    scores = jnp.where(valid[None, :, None, None, :], scores + bias[None, None], -1e30)
    p = jax.nn.softmax(scores, axis=-1).astype(v.dtype)
    o = jnp.einsum('bchim,bcmhd->bcihd', p, vb)
    return o.reshape(b_, s_, D_B)

def memory_cross_attention(h, mem, w_q, w_k, w_v, w_o):
    b_, s_, _ = h.shape
    m_ = mem.shape[1]
    q = (h @ w_q).reshape(b_, s_, X_HEADS, X_HEAD_DIM)
    k = (mem @ w_k).reshape(b_, m_, X_HEADS, X_HEAD_DIM)
    v = (mem @ w_v).reshape(b_, m_, X_HEADS, X_HEAD_DIM)
    scores = jnp.einsum('bshd,bmhd->bhsm', q, k).astype(jnp.float32) * (X_HEAD_DIM ** -0.5)
    p = jax.nn.softmax(scores, axis=-1).astype(v.dtype)
    o = jnp.einsum('bhsm,bmhd->bshd', p, v).reshape(b_, s_, D_MODEL)
    return o @ w_o

def peer_ffn(h, w_pq, sub_keys, expert_u, expert_v):
    b_, s_, d = h.shape
    t = b_ * s_
    xf = h.reshape(t, d)
    q = (xf @ w_pq).reshape(t, PEER_HEADS, 2, PEER_HALF)
    s = jnp.einsum('thpd,hpkd->thpk', q, sub_keys).astype(jnp.float32)
    sv, si = lax.top_k(s, PEER_TOPK)
    comb = (sv[:, :, 0, :, None] + sv[:, :, 1, None, :]).reshape(t, PEER_HEADS, PEER_TOPK * PEER_TOPK)
    gv, gp = lax.top_k(comb, PEER_TOPK)
    i1 = jnp.take_along_axis(si[:, :, 0], gp // PEER_TOPK, axis=-1)
    i2 = jnp.take_along_axis(si[:, :, 1], gp % PEER_TOPK, axis=-1)
    n_blk = t // PEER_TOKEN_BLOCK
    idx = (i1 * PEER_KEYS + i2).reshape(n_blk, PEER_TOKEN_BLOCK, PEER_HEADS * PEER_TOPK)
    g = jax.nn.softmax(gv, axis=-1).astype(h.dtype).reshape(n_blk, PEER_TOKEN_BLOCK, PEER_HEADS * PEER_TOPK)
    xb = xf.reshape(n_blk, PEER_TOKEN_BLOCK, d)

    def block(args):
        x_blk, idx_blk, g_blk = args
        u = expert_u[idx_blk]
        a = g_blk * jax.nn.gelu(jnp.einsum('tkd,td->tk', u, x_blk), approximate=False)
        return jnp.einsum('tk,tkd->td', a, expert_v[idx_blk])

    out = lax.map(block, (xb, idx, g))
    return out.reshape(b_, s_, d)

def setup_inputs(seed: int = 0) -> dict:
    key = jax.random.key(seed)
    ks = jax.random.split(key, 32)
    f32 = jnp.float32
    nrm = lambda k, shp, sc: jax.random.normal(k, shp, f32) * sc
    gain = lambda k, shp: 1.0 + 0.05 * jax.random.normal(k, shp, f32)
    L = DEPTH
    return {
        "x": nrm(ks[0], (BATCH, SEQ, D_MODEL), 1.0),
        "mem": nrm(ks[1], (BATCH, MEM_LEN, D_MODEL), 1.0),
        "ln_in_g": gain(ks[2], (D_MODEL,)),
        "ln_in_b": nrm(ks[3], (D_MODEL,), 0.05),
        "w_in": nrm(ks[4], (L, D_MODEL, N_IN), D_MODEL ** -0.5),
        "gate_ln_g": gain(ks[5], (L, D_A)),
        "gate_ln_b": nrm(ks[6], (L, D_A), 0.05),
        "w_sp": nrm(ks[7], (L, A_GROUPS, A_BLOCK, A_BLOCK), A_BLOCK ** -0.5),
        "b_sp": gain(ks[8], (L, A_GROUPS, A_BLOCK)),
        "rel_bias": nrm(ks[9], (L, B_HEADS, 2 * REL_CLIP + 1), 0.1),
        "w_out": nrm(ks[10], (L, D_MIX, D_MODEL), DN_BETA * D_MIX ** -0.5),
        "ln1_g": gain(ks[11], (L, D_MODEL)),
        "ln1_b": nrm(ks[12], (L, D_MODEL), 0.05),
        "w_xq": nrm(ks[13], (L, D_MODEL, D_MODEL), D_MODEL ** -0.5),
        "w_xk": nrm(ks[14], (L, D_MODEL, D_MODEL), D_MODEL ** -0.5),
        "w_xv": nrm(ks[15], (L, D_MODEL, D_MODEL), DN_BETA * D_MODEL ** -0.5),
        "w_xo": nrm(ks[16], (L, D_MODEL, D_MODEL), DN_BETA * D_MODEL ** -0.5),
        "ln2_g": gain(ks[17], (L, D_MODEL)),
        "ln2_b": nrm(ks[18], (L, D_MODEL), 0.05),
        "w_pq": nrm(ks[19], (L, D_MODEL, PEER_HEADS * PEER_D_KEY), D_MODEL ** -0.5),
        "sub_keys": nrm(ks[20], (L, PEER_HEADS, 2, PEER_KEYS, PEER_HALF), PEER_HALF ** -0.5),
        "expert_u": nrm(ks[21], (L, PEER_EXPERTS, D_MODEL), D_MODEL ** -0.5),
        "expert_v": nrm(ks[22], (L, PEER_EXPERTS, D_MODEL), DN_BETA),
        "ln3_g": gain(ks[23], (L, D_MODEL)),
        "ln3_b": nrm(ks[24], (L, D_MODEL), 0.05),
    }

def reference(x, mem, ln_in_g, ln_in_b, w_in, gate_ln_g, gate_ln_b, w_sp, b_sp, rel_bias,
              w_out, ln1_g, ln1_b, w_xq, w_xk, w_xv, w_xo, ln2_g, ln2_b,
              w_pq, sub_keys, expert_u, expert_v, ln3_g, ln3_b):
    h = layer_norm(x, ln_in_g, ln_in_b)
    split_at = [2 * D_A, 2 * D_A + D_B, 2 * D_A + 2 * D_B]
    for l in range(DEPTH):
        proj = h @ w_in[l]
        z_a, q_b, k_b, v_b = jnp.split(proj, split_at, axis=-1)
        y_a = spatial_gating_mixer(jax.nn.gelu(z_a, approximate=False),
                                   gate_ln_g[l], gate_ln_b[l], w_sp[l], b_sp[l])
        y_b = chunk_band_attention(q_b, k_b, v_b, rel_bias[l])
        mix = jnp.concatenate([y_a, y_b], axis=-1) @ w_out[l]
        h = layer_norm(DN_ALPHA * h + mix, ln1_g[l], ln1_b[l])
        xa = memory_cross_attention(h, mem, w_xq[l], w_xk[l], w_xv[l], w_xo[l])
        h = layer_norm(DN_ALPHA * h + xa, ln2_g[l], ln2_b[l])
        ff = peer_ffn(h, w_pq[l], sub_keys[l], expert_u[l], expert_v[l])
        h = layer_norm(DN_ALPHA * h + ff, ln3_g[l], ln3_b[l])
    return h


_drawn_inputs = setup_inputs


def setup_inputs(seed=0):
    import zlib

    import numpy as np

    out = dict(_drawn_inputs(seed))
    spreads = {}
    factors = {'rel_bias': 4.103}
    for name, (base, spread) in spreads.items():
        noise = np.random.default_rng([zlib.crc32(name.encode()), seed]).standard_normal(out[name].shape)
        drawn = base * np.exp(spread * noise) if base else spread * noise
        out[name] = __import__('jax').numpy.asarray(drawn.astype(out[name].dtype))
    for name, factor in factors.items():
        out[name] = (out[name] * factor).astype(out[name].dtype)
    return out
```

```python
from contextlib import ExitStack

import concourse.bass as bass
from concourse import mybir

F32 = mybir.dt.float32
F32R = mybir.dt.float32r
U32 = mybir.dt.uint32
ACT = mybir.ActivationFunctionType
ALU = mybir.AluOpType
AX = mybir.AxisListType

P = 128
D = 1024
T = 1024
KT = D // P
TT = T // P
HALF = 512
D_A = D // 2
D_B = D - D_A
A_GROUPS = 4
CHUNK = 64
B_HEADS = 8
B_HD = D_B // B_HEADS
BAND = 8 * CHUNK
SPAN = BAND + P
REL = 128
EXT = SPAN + P
MEM = 256
MT = MEM // P
X_HEADS = 4
X_HD = D // X_HEADS
PH = 8
KEYS = 128
TOPK = 16
UNITS = TT * PH
GBLK = 32
ALPHA = 2.0 ** 0.25
EPS = 1e-5
MASKED = -1e30
LOWEST = -3.4e38


def layer_program(nc, x, mem, ln_in_g, ln_in_b, w_in, gate_ln_g, gate_ln_b, w_sp, b_sp, rel_bias, w_out,
                  ln1_g, ln1_b, w_xq, w_xk, w_xv, w_xo, ln2_g, ln2_b, w_pq, sub_keys, expert_u,
                  expert_v, ln3_g, ln3_b, out):
    top = ExitStack()

    def dram(name, shape):
        return nc.dram_tensor(name, shape, F32, kind="Internal").ap()

    h0_d = dram("h0_d", [T, D])
    h1_d = dram("h1_d", [T, D])
    h2_d = dram("h2_d", [T, D])
    u_d = dram("u_d", [T, D_A])
    v_d = dram("v_d", [T, D_A])
    vb_d = dram("vb_d", [T, D_B])
    qb_d = dram("qb_d", [D_B, T])
    kb_d = dram("kb_d", [D_B, T])
    ext_d = dram("ext_d", [B_HEADS, EXT])
    xq_d = dram("xq_d", [D, T])
    s_d = dram("s_d", [UNITS, P, 2 * KEYS])
    route_d = dram("route_d", [UNITS, TOPK * 3, P])
    act_d = dram("act_d", [P, P, T])
    gate_d = dram("gate_d", [T // GBLK, P, P, GBLK])

    stage_sems = []

    def sem(name):
        stage_sems.append(nc.alloc_semaphore(name=name))
        return stage_sems[-1]

    def free_sems():
        nc.clear_and_free_semaphores(stage_sems)
        nc.all_engine_barrier()
        stage_sems.clear()

    def local(stage):
        def sb(name, shape, dt=F32):
            return stage.enter_context(nc.sbuf_tensor(name, shape, dt))

        def pb(name, cols):
            return stage.enter_context(nc.psum_tensor(name, [P, cols], F32))
        return sb, pb

    def spread(vec):
        return bass.AP(vec.tensor, vec.offset, [[0, P], [1, vec.shape[-1]]])

    def three(pe, ps, l_hi, l_lo, r_hi, r_lo, first, last):
        pe.matmul(ps, l_hi, r_hi, start=first, stop=False)
        pe.matmul(ps, l_hi, r_lo, start=False, stop=False)
        return pe.matmul(ps, l_lo, r_hi, start=False, stop=last)

    with top:
        act_stack = ExitStack()
        asb, _ = local(act_stack)
        ident = asb("ident", [P, P])
        aT_hi = asb("aT_hi", [P, KT, T], F32R)
        aT_lo = asb("aT_lo", [P, KT, T], F32R)

        ident_done, ext_in, ext_built, ext_out = sem("ident_done"), sem("ext_in"), sem("ext_built"), sem("ext_out")
        with ExitStack() as stage:
            sb, pb = local(stage)
            ext = sb("ext", [B_HEADS, EXT])
            rel = sb("rel", [B_HEADS, 2 * REL + 1])
            with nc.Block() as block:
                @block.gpsimd
                def _(pool):
                    pool.memset(ident[:], 0.0).then_inc(ident_done, 1)
                    pool.wait_ge(ident_done, 1)
                    pool.affine_select(out=ident[:], in_=ident[:], compare_op=ALU.not_equal, fill=1.0, base=0,
                                       pattern=[[-1, P]], channel_multiplier=1).then_inc(ident_done, 1)

                @block.sync
                def _(sp):
                    sp.dma_start(rel[:], rel_bias).then_inc(ext_in, 16)
                    sp.wait_ge(ext_built, 2)
                    sp.dma_start(ext_d, ext[:]).then_inc(ext_out, 16)
                    sp.wait_ge(ext_out, 16)

                @block.vector
                def _(dve):
                    near = EXT - BAND - 1
                    dve.wait_ge(ext_in, 16)
                    dve.tensor_copy(ext[:, 0:near], rel[:, 2 * REL - near:2 * REL]).then_inc(ext_built, 1)
                    dve.tensor_copy(ext[:, near:EXT], rel[:, 2 * REL:2 * REL + 1].broadcast_to([B_HEADS, EXT - near])).then_inc(ext_built, 1)

        def norm_stage(tag, gain, bias, resid, dest, weight=None, acc=None, transposed=True):
            w_raw_in = [sem(f"{tag}_w_raw_in{i}") for i in range(2)]
            w_hi_done, w_lo_done = sem(f"{tag}_w_hi"), sem(f"{tag}_w_lo")
            gb_in = sem(f"{tag}_gb_in")
            row_in = [sem(f"{tag}_row_in{i}") for i in range(2)]
            stored = [sem(f"{tag}_stored{i}") for i in range(2)]
            mm_done, chain, var_done = sem(f"{tag}_mm"), sem(f"{tag}_chain"), sem(f"{tag}_var")
            sum_done, root_done, ln_done = sem(f"{tag}_sum"), sem(f"{tag}_root"), sem(f"{tag}_ln")
            tr_done, hi_done, lo_done = sem(f"{tag}_tr"), sem(f"{tag}_hi"), sem(f"{tag}_lo")
            with ExitStack() as stage:
                sb, pb = local(stage)
                g_sb, b_sb = sb(f"{tag}_g", [P, D]), sb(f"{tag}_b", [P, D])
                row = sb(f"{tag}_row", [P, 2, D])
                stats = sb(f"{tag}_stats", [P, 2, 2, 6])
                mv = sb(f"{tag}_mv", [P, 2, 2])
                var = sb(f"{tag}_var_sb", [P, 2])
                root = sb(f"{tag}_root_sb", [P, 2])
                rstd = sb(f"{tag}_rstd", [P, 2])
                if weight is not None:
                    w_raw = sb(f"{tag}_w_raw", [P, 2, D])
                    w_hi, w_lo = sb(f"{tag}_whi", [P, KT, D], F32R), sb(f"{tag}_wlo", [P, KT, D], F32R)
                    ps_mm = [pb(f"{tag}_ps_mm{i}", D) for i in range(2)]
                if transposed:
                    ps_tr = [pb(f"{tag}_ps_tr{i}", D) for i in range(2)]
                with nc.Block() as block:
                    @block.sync
                    def _(sp):
                        def load_row(j):
                            sp.dma_start(row[:, j % 2, :], resid[j * P:(j + 1) * P, :]).then_inc(row_in[j % 2], 16)

                        load_row(0)
                        load_row(1)
                        sp.dma_start(g_sb[:], spread(gain)).then_inc(gb_in, 16)
                        sp.dma_start(b_sb[:], spread(bias)).then_inc(gb_in, 16)
                        if weight is not None:
                            for k in range(KT):
                                if k >= 2:
                                    sp.wait_ge(w_lo_done, k - 1)
                                sp.dma_start(w_raw[:, k % 2, :], weight[k * P:(k + 1) * P, :]).then_inc(w_raw_in[k % 2], 16)
                        for j in range(TT):
                            sp.wait_ge(ln_done, j + 1)
                            sp.dma_start(dest[j * P:(j + 1) * P, :], row[:, j % 2, :]).then_inc(stored[j % 2], 16)
                            if j + 2 < TT:
                                sp.wait_ge(stored[j % 2], 16 * (j // 2 + 1))
                                if transposed:
                                    sp.wait_ge(tr_done, j + 1)
                                load_row(j + 2)
                        for i in range(2):
                            sp.wait_ge(stored[i], 16 * (TT // 2))

                    @block.gpsimd
                    def _(pool):
                        if weight is not None:
                            for k in range(KT):
                                pool.wait_ge(w_hi_done, k + 1)
                                pool.tensor_tensor(w_lo[:, k, :], w_raw[:, k % 2, :], w_hi[:, k, :], ALU.subtract).then_inc(w_lo_done, 1)

                    @block.scalar
                    def _(act):
                        if weight is not None:
                            for k in range(KT):
                                act.wait_ge(w_raw_in[k % 2], 16 * (k // 2 + 1))
                                act.activation(w_hi[:, k, :], w_raw[:, k % 2, :], ACT.Copy).then_inc(w_hi_done, 1)

                        def transposed_hi(j):
                            act.wait_ge(tr_done, j + 1)
                            act.activation(aT_hi[:, :, j * P:(j + 1) * P], ps_tr[j % 2][:].rearrange("p (k t) -> p k t", k=KT),
                                           ACT.Copy).then_inc(hi_done, 1)

                        for j in range(TT):
                            if transposed and j >= 1:
                                transposed_hi(j - 1)
                            act.wait_ge(var_done, j + 1)
                            act.activation(root[:, j % 2:j % 2 + 1], var[:, j % 2:j % 2 + 1], ACT.Sqrt).then_inc(root_done, 1)
                        if transposed:
                            transposed_hi(TT - 1)

                    @block.vector
                    def _(dve):
                        links = [0]

                        def link(ins):
                            links[0] += 1
                            ins.then_inc(chain, 1)
                            dve.wait_ge(chain, links[0])

                        def transposed_lo(j):
                            dve.wait_ge(hi_done, j + 1)
                            dve.tensor_tensor(aT_lo[:, :, j * P:(j + 1) * P], ps_tr[j % 2][:].rearrange("p (k t) -> p k t", k=KT),
                                              aT_hi[:, :, j * P:(j + 1) * P], ALU.subtract).then_inc(lo_done, 1)

                        for j in range(TT):
                            i = j % 2
                            dve.wait_ge(row_in[i], 16 * (j // 2 + 1))
                            if weight is not None:
                                dve.wait_ge(mm_done, j + 1)
                                dve.scalar_tensor_tensor(row[:, i, :], row[:, i, :], ALPHA, ps_mm[i][:], ALU.mult, ALU.add).then_inc(sum_done, 1)
                                dve.wait_ge(sum_done, j + 1)
                            if acc is not None:
                                dve.scalar_tensor_tensor(row[:, i, :], row[:, i, :], ALPHA, acc[:, j, :], ALU.mult, ALU.add).then_inc(sum_done, 1)
                                dve.wait_ge(sum_done, j + 1)
                            for c in range(2):
                                link(dve.bn_stats(stats[:, i, c, :], row[:, i, c * HALF:(c + 1) * HALF]))
                            link(dve.bn_aggr(mv[:, i, :], stats[:, i, :, :].rearrange("p a b -> p (a b)")))
                            dve.tensor_scalar(var[:, i:i + 1], mv[:, i, 1:2], EPS, None, ALU.add).then_inc(var_done, 1)
                            if transposed and j >= 1:
                                transposed_lo(j - 1)
                            dve.wait_ge(root_done, j + 1)
                            link(dve.reciprocal(rstd[:, i:i + 1], root[:, i:i + 1]))
                            link(dve.tensor_scalar(row[:, i, :], row[:, i, :], mv[:, i, 0:1], rstd[:, i:i + 1], ALU.subtract, ALU.mult))
                            if j == 0:
                                dve.wait_ge(gb_in, 32)
                            link(dve.tensor_tensor(row[:, i, :], row[:, i, :], g_sb[:], ALU.mult))
                            dve.tensor_tensor(row[:, i, :], row[:, i, :], b_sb[:], ALU.add).then_inc(ln_done, 1)
                        if transposed:
                            transposed_lo(TT - 1)

                    @block.tensor
                    def _(pe):
                        def transposes(j):
                            pe.wait_ge(ln_done, j + 1)
                            if j >= 2:
                                pe.wait_ge(lo_done, j - 1)
                            for k in range(KT):
                                last = pe.transpose(ps_tr[j % 2][:, k * P:(k + 1) * P], row[:, j % 2, k * P:(k + 1) * P], ident[:])
                            last.then_inc(tr_done, 1)

                        for j in range(TT):
                            if weight is not None:
                                if j >= 2:
                                    pe.wait_ge(sum_done, j - 1)
                                tok = slice(j * P, (j + 1) * P)
                                for k in range(KT):
                                    if j == 0:
                                        pe.wait_ge(w_lo_done, k + 1)
                                    for c in range(2):
                                        col = slice(c * HALF, (c + 1) * HALF)
                                        last = three(pe, ps_mm[j % 2][:, col], aT_hi[:, k, tok], aT_lo[:, k, tok],
                                                     w_hi[:, k, col], w_lo[:, k, col], k == 0, k == KT - 1)
                                last.then_inc(mm_done, 1)
                            if transposed and j >= 1:
                                transposes(j - 1)
                        if transposed:
                            transposes(TT - 1)

        def project_stage(tag, weight, blocks):
            raw_in = [sem(f"{tag}_raw_in{i}") for i in range(4)]
            hi_done, lo_done, mm_done = sem(f"{tag}_hi"), sem(f"{tag}_lo"), sem(f"{tag}_mm")
            act_out, dve_out = sem(f"{tag}_act_out"), sem(f"{tag}_dve_out")
            stored = [sem(f"{tag}_stored{i}") for i in range(4)]
            NB, PIECES, PER = len(blocks), 4, 8
            units = [(b, i) for b in range(NB) for i in range(PER)]

            def by_act(u):
                return blocks[units[u][0]][1] == "gelu"

            def count(u):
                return sum(by_act(n) == by_act(u) for n in range(u + 1))

            def out_of_psum(eng, u):
                eng.wait_ge(act_out if by_act(u) else dve_out, count(u))

            with ExitStack() as stage:
                sb, pb = local(stage)
                raw = sb(f"{tag}_raw", [P, 4, 2, HALF])
                w_hi, w_lo = sb(f"{tag}_whi", [P, 2, KT, HALF], F32R), sb(f"{tag}_wlo", [P, 2, KT, HALF], F32R)
                res = sb(f"{tag}_res", [P, 4, HALF])
                ps = [pb(f"{tag}_ps{i}", HALF) for i in range(8)]
                with nc.Block() as block:
                    @block.sync
                    def _(sp):
                        def load(n):
                            b, q = divmod(n, PIECES)
                            if n >= 4:
                                sp.wait_ge(lo_done, n - 3)
                            src = weight[2 * q * P:2 * (q + 1) * P, b * HALF:(b + 1) * HALF].rearrange("(a p) n -> p a n", p=P)
                            sp.dma_start(raw[:, n % 4, :, :], src).then_inc(raw_in[n % 4], 16)

                        for n in range(PIECES):
                            load(n)
                        for u, (b, i) in enumerate(units):
                            if b + 1 < NB and i % 2 == 0:
                                load((b + 1) * PIECES + i // 2)
                            dest, kind, _ = blocks[b]
                            if kind == "feat":
                                f, th = divmod(i, 2)
                                to = dest[f * P:(f + 1) * P, th * HALF:(th + 1) * HALF]
                            else:
                                to = dest[i * P:(i + 1) * P, :]
                            out_of_psum(sp, u)
                            sp.dma_start(to, res[:, u % 4, :]).then_inc(stored[u % 4], 16)
                        for i in range(4):
                            sp.wait_ge(stored[i], 16 * (len(units) // 4))

                    @block.gpsimd
                    def _(pool):
                        for n in range(NB * PIECES):
                            b, q = divmod(n, PIECES)
                            pool.wait_ge(hi_done, n + 1)
                            pool.tensor_tensor(w_lo[:, b % 2, 2 * q:2 * q + 2, :], raw[:, n % 4, :, :],
                                               w_hi[:, b % 2, 2 * q:2 * q + 2, :], ALU.subtract).then_inc(lo_done, 1)

                    @block.scalar
                    def _(act):
                        def split(n):
                            b, q = divmod(n, PIECES)
                            act.wait_ge(raw_in[n % 4], 16 * (n // 4 + 1))
                            if b >= 2:
                                act.wait_ge(mm_done, (b - 1) * PER)
                            act.activation(w_hi[:, b % 2, 2 * q:2 * q + 2, :], raw[:, n % 4, :, :], ACT.Copy).then_inc(hi_done, 1)

                        for n in range(PIECES):
                            split(n)
                        for u, (b, i) in enumerate(units):
                            if b + 1 < NB and i % 2 == 0:
                                split((b + 1) * PIECES + i // 2)
                            if by_act(u):
                                act.wait_ge(mm_done, u + 1)
                                if u >= 4:
                                    act.wait_ge(stored[u % 4], 16 * (u // 4))
                                act.activation(res[:, u % 4, :], ps[u % 8][:], ACT.Gelu).then_inc(act_out, 1)

                    @block.vector
                    def _(dve):
                        for u, (b, i) in enumerate(units):
                            if not by_act(u):
                                dve.wait_ge(mm_done, u + 1)
                                if u >= 4:
                                    dve.wait_ge(stored[u % 4], 16 * (u // 4))
                                dve.tensor_scalar(res[:, u % 4, :], ps[u % 8][:], blocks[b][2], None, ALU.mult).then_inc(dve_out, 1)

                    @block.tensor
                    def _(pe):
                        for u, (b, i) in enumerate(units):
                            if u >= 8:
                                out_of_psum(pe, u - 8)
                            for k in range(KT):
                                if i == 0 and k % 2 == 0:
                                    pe.wait_ge(lo_done, b * PIECES + k // 2 + 1)
                                if blocks[b][1] == "feat":
                                    f, th = divmod(i, 2)
                                    col, tok = slice(f * P, (f + 1) * P), slice(th * HALF, (th + 1) * HALF)
                                    last = three(pe, ps[u % 8][:], w_hi[:, b % 2, k, col], w_lo[:, b % 2, k, col],
                                                 aT_hi[:, k, tok], aT_lo[:, k, tok], k == 0, k == KT - 1)
                                else:
                                    tok = slice(i * P, (i + 1) * P)
                                    last = three(pe, ps[u % 8][:], aT_hi[:, k, tok], aT_lo[:, k, tok],
                                                 w_hi[:, b % 2, k, :], w_lo[:, b % 2, k, :], k == 0, k == KT - 1)
                            last.then_inc(mm_done, 1)

        def gate_stage():
            consts_in, wt_tr, wt_hi, wt_lo = sem("ga_consts"), sem("ga_wt_tr"), sem("ga_wt_hi"), sem("ga_wt_lo")
            masked = sem("ga_masked")
            v_in = [sem(f"ga_v_in{i}") for i in range(2)]
            u_in = [sem(f"ga_u_in{i}") for i in range(2)]
            chain, var_done, root_done, vn_done = sem("ga_chain"), sem("ga_var"), sem("ga_root"), sem("ga_vn")
            vhi_done, vlo_done, mix_done, y_done = sem("ga_vhi"), sem("ga_vlo"), sem("ga_mix"), sem("ga_y")
            tr_done, hi_done, lo_done = sem("ga_tr"), sem("ga_hi"), sem("ga_lo")
            with ExitStack() as stage:
                sb, pb = local(stage)
                wraw = sb("ga_wraw", [P, A_GROUPS, P])
                wT_hi, wT_lo = sb("ga_wT_hi", [P, A_GROUPS, P], F32R), sb("ga_wT_lo", [P, A_GROUPS, P], F32R)
                bsp = sb("ga_bsp", [P, A_GROUPS])
                g_sb, b_sb = sb("ga_g", [P, D_A]), sb("ga_b", [P, D_A])
                v_sb, u_sb = sb("ga_v", [P, 2, D_A]), sb("ga_u", [P, 2, D_A])
                v_hi, v_lo = sb("ga_v_hi", [P, 2, D_A], F32R), sb("ga_v_lo", [P, 2, D_A], F32R)
                y_sb = sb("ga_y_sb", [P, 2, D_A])
                stats, mv = sb("ga_stats", [P, 2, 6]), sb("ga_mv", [P, 2, 2])
                var, root, rstd = sb("ga_var_sb", [P, 2]), sb("ga_root_sb", [P, 2]), sb("ga_rstd", [P, 2])
                ps_w = pb("ga_ps_w", HALF)
                ps_s = [pb(f"ga_ps_s{i}", HALF) for i in range(2)]
                ps_y = [pb(f"ga_ps_y{i}", HALF) for i in range(2)]
                GA = D_A // P

                with nc.Block() as block:
                    @block.sync
                    def _(sp):
                        sp.dma_start(wraw[:], w_sp.rearrange("g i j -> i g j")).then_inc(consts_in, 16)
                        sp.dma_start(bsp[:], b_sp.rearrange("g i -> i g"), allow_slow_non_contiguous=True).then_inc(consts_in, 16)
                        sp.dma_start(g_sb[:], spread(gate_ln_g)).then_inc(consts_in, 16)
                        sp.dma_start(b_sb[:], spread(gate_ln_b)).then_inc(consts_in, 16)
                        for j in range(TT):
                            if j >= 2:
                                sp.wait_ge(vlo_done, j - 1)
                            sp.dma_start(v_sb[:, j % 2, :], v_d[j * P:(j + 1) * P, :]).then_inc(v_in[j % 2], 16)
                            if j >= 2:
                                sp.wait_ge(y_done, A_GROUPS * (j - 1))
                            sp.dma_start(u_sb[:, j % 2, :], u_d[j * P:(j + 1) * P, :]).then_inc(u_in[j % 2], 16)

                    @block.scalar
                    def _(act):
                        act.wait_ge(wt_tr, 1)
                        act.activation(wT_hi[:], ps_w[:].rearrange("p (g i) -> p g i", g=A_GROUPS), ACT.Copy).then_inc(wt_hi, 1)

                        def y_hi(j):
                            act.wait_ge(tr_done, j + 1)
                            act.activation(aT_hi[:, 0:GA, j * P:(j + 1) * P], ps_y[j % 2][:].rearrange("p (k t) -> p k t", k=GA),
                                           ACT.Copy).then_inc(hi_done, 1)

                        for j in range(TT):
                            act.wait_ge(var_done, j + 1)
                            act.activation(root[:, j % 2:j % 2 + 1], var[:, j % 2:j % 2 + 1], ACT.Sqrt).then_inc(root_done, 1)
                            act.wait_ge(vn_done, j + 1)
                            if j >= 2:
                                act.wait_ge(mix_done, j - 1)
                            act.activation(v_hi[:, j % 2, :], v_sb[:, j % 2, :], ACT.Copy).then_inc(vhi_done, 1)
                            if j >= 1:
                                y_hi(j - 1)
                        y_hi(TT - 1)

                    @block.vector
                    def _(dve):
                        links = [0]

                        def link(ins):
                            links[0] += 1
                            ins.then_inc(chain, 1)
                            dve.wait_ge(chain, links[0])

                        dve.wait_ge(wt_hi, 1)
                        dve.tensor_tensor(wT_lo[:], ps_w[:].rearrange("p (g i) -> p g i", g=A_GROUPS), wT_hi[:], ALU.subtract).then_inc(wt_lo, 1)
                        dve.wait_ge(wt_lo, 1)
                        dve.memset(wT_hi[CHUNK:P, :, 0:CHUNK].bitcast(F32), 0.0).then_inc(masked, 1)
                        dve.memset(wT_lo[CHUNK:P, :, 0:CHUNK].bitcast(F32), 0.0).then_inc(masked, 1)
                        dve.wait_ge(consts_in, 64)

                        def gate(j):
                            dve.wait_ge(mix_done, j + 1)
                            dve.wait_ge(u_in[j % 2], 16 * (j // 2 + 1))
                            if j >= 2:
                                dve.wait_ge(tr_done, j - 1)
                            for g in range(A_GROUPS):
                                col = slice(g * P, (g + 1) * P)
                                dve.scalar_tensor_tensor(y_sb[:, j % 2, col], ps_s[j % 2][:, col], bsp[:, g:g + 1],
                                                         u_sb[:, j % 2, col], ALU.add, ALU.mult).then_inc(y_done, 1)

                        def y_lo(j):
                            dve.wait_ge(hi_done, j + 1)
                            dve.tensor_tensor(aT_lo[:, 0:GA, j * P:(j + 1) * P], ps_y[j % 2][:].rearrange("p (k t) -> p k t", k=GA),
                                              aT_hi[:, 0:GA, j * P:(j + 1) * P], ALU.subtract).then_inc(lo_done, 1)

                        for j in range(TT):
                            i = j % 2
                            dve.wait_ge(v_in[i], 16 * (j // 2 + 1))
                            link(dve.bn_stats(stats[:, i, :], v_sb[:, i, :]))
                            link(dve.bn_aggr(mv[:, i, :], stats[:, i, :]))
                            dve.tensor_scalar(var[:, i:i + 1], mv[:, i, 1:2], EPS, None, ALU.add).then_inc(var_done, 1)
                            dve.wait_ge(root_done, j + 1)
                            link(dve.reciprocal(rstd[:, i:i + 1], root[:, i:i + 1]))
                            link(dve.tensor_scalar(v_sb[:, i, :], v_sb[:, i, :], mv[:, i, 0:1], rstd[:, i:i + 1], ALU.subtract, ALU.mult))
                            link(dve.tensor_tensor(v_sb[:, i, :], v_sb[:, i, :], g_sb[:], ALU.mult))
                            dve.tensor_tensor(v_sb[:, i, :], v_sb[:, i, :], b_sb[:], ALU.add).then_inc(vn_done, 1)
                            if j >= 1:
                                gate(j - 1)
                            dve.wait_ge(vhi_done, j + 1)
                            dve.tensor_tensor(v_lo[:, i, :], v_sb[:, i, :], v_hi[:, i, :], ALU.subtract).then_inc(vlo_done, 1)
                            if j >= 1:
                                y_lo(j - 1)
                        gate(TT - 1)
                        y_lo(TT - 1)

                    @block.tensor
                    def _(pe):
                        pe.wait_ge(consts_in, 64)
                        for g in range(A_GROUPS):
                            last = pe.transpose(ps_w[:, g * P:(g + 1) * P], wraw[:, g, :], ident[:])
                        last.then_inc(wt_tr, 1)
                        pe.wait_ge(masked, 2)

                        def y_transposes(j):
                            pe.wait_ge(y_done, A_GROUPS * (j + 1))
                            if j >= 2:
                                pe.wait_ge(lo_done, j - 1)
                            for k in range(GA):
                                last = pe.transpose(ps_y[j % 2][:, k * P:(k + 1) * P], y_sb[:, j % 2, k * P:(k + 1) * P], ident[:])
                            last.then_inc(tr_done, 1)

                        for j in range(TT):
                            if j >= 1:
                                y_transposes(j - 1)
                            pe.wait_ge(vlo_done, j + 1)
                            if j >= 2:
                                pe.wait_ge(y_done, A_GROUPS * (j - 1))
                            for g in range(A_GROUPS):
                                col = slice(g * P, (g + 1) * P)
                                last = three(pe, ps_s[j % 2][:, col], wT_hi[:, g, :], wT_lo[:, g, :],
                                             v_hi[:, j % 2, col], v_lo[:, j % 2, col], True, True)
                            last.then_inc(mix_done, 1)
                        y_transposes(TT - 1)

        def attention_stage():
            bias_in, masked = sem("at_bias_in"), sem("at_masked")
            raw_in = [sem(f"at_raw_in{i}") for i in range(2)]
            sp_hi, sp_lo = sem("at_split_hi"), sem("at_split_lo")
            s_done, max_done, neg_done, exp_done = sem("at_s"), sem("at_max"), sem("at_neg"), sem("at_exp")
            tr_done, p_hi_done, p_lo_done, pv_done = sem("at_tr"), sem("at_p_hi"), sem("at_p_lo"), sem("at_pv")
            rec_done, y_done, yt_done, y_hi_done, y_lo_done = sem("at_rec"), sem("at_y"), sem("at_yt"), sem("at_y_hi"), sem("at_y_lo")
            QF = D_B // P
            NU = TT * B_HEADS
            units = [divmod(u, B_HEADS) for u in range(NU)]
            G0 = D_A // P

            def keys(n):
                nk = min(SPAN, (n + 1) * P)
                return (n + 1) * P - nk, nk

            def backwards(row):
                (step, count), (one, n) = row.ap
                return bass.AP(row.tensor, row.offset + (n - 1) * one, [[step, count], [-one, n]])

            with ExitStack() as stage:
                sb, pb = local(stage)
                bias = sb("at_bias", [P, B_HEADS, SPAN])
                raw = sb("at_raw", [P, 2, D])
                q_hi, q_lo = sb("at_q_hi", [P, QF, T], F32R), sb("at_q_lo", [P, QF, T], F32R)
                k_hi, k_lo = sb("at_k_hi", [P, QF, T], F32R), sb("at_k_lo", [P, QF, T], F32R)
                v_hi, v_lo = sb("at_v_hi", [P, TT, D_B], F32R), sb("at_v_lo", [P, TT, D_B], F32R)
                prob = sb("at_prob", [P, 2, SPAN])
                pT_hi, pT_lo = sb("at_pT_hi", [P, 2, SPAN], F32R), sb("at_pT_lo", [P, 2, SPAN], F32R)
                top_s, neg, rsum, rinv = sb("at_top", [P, 2]), sb("at_neg_sb", [P, 2]), sb("at_rsum", [P, 4]), sb("at_rinv", [P, 2])
                y_sb = sb("at_y_sb", [P, 2, D_B])
                ps_s = [pb(f"at_ps_s{i}", D) for i in range(2)]
                ps_t = pb("at_ps_t", D)
                ps_o = pb("at_ps_o", HALF)
                ps_y = pb("at_ps_y", HALF)
                pieces = []
                for f in range(QF):
                    pieces.append((qb_d[f * P:(f + 1) * P, :], q_hi[:, f, :], q_lo[:, f, :]))
                    pieces.append((kb_d[f * P:(f + 1) * P, :], k_hi[:, f, :], k_lo[:, f, :]))
                for f in range(TT // 2):
                    pieces.append((vb_d[2 * f * P:2 * (f + 1) * P, :].rearrange("(a p) n -> p a n", p=P),
                                   v_hi[:, 2 * f:2 * f + 2, :], v_lo[:, 2 * f:2 * f + 2, :]))

                def raw_of(n):
                    r = raw[:, n % 2, :]
                    return r if n < 2 * QF else r.rearrange("p (a n) -> p a n", a=2)

                with nc.Block() as block:
                    @block.sync
                    def _(sp):
                        for n, (src, _, _) in enumerate(pieces):
                            if n >= 2:
                                sp.wait_ge(sp_lo, n - 1)
                            sp.dma_start(raw_of(n), src).then_inc(raw_in[n % 2], 16)
                            if n == 1:
                                sp.dma_start(bias[:], bass.AP(ext_d.tensor, ext_d.offset,
                                                              [[1, P], [EXT, B_HEADS], [1, SPAN]])).then_inc(bias_in, 16)

                    @block.gpsimd
                    def _(pool):
                        pool.wait_ge(bias_in, 16)
                        pool.memset(bias[0:CHUNK, :, 0:CHUNK], MASKED).then_inc(masked, 1)
                        pool.memset(bias[CHUNK:P, :, SPAN - CHUNK:SPAN], MASKED).then_inc(masked, 1)

                    @block.scalar
                    def _(act):
                        for n, (_, hi, _) in enumerate(pieces):
                            act.wait_ge(raw_in[n % 2], 16 * (n // 2 + 1))
                            act.activation(hi, raw_of(n), ACT.Copy).then_inc(sp_hi, 1)

                        def prob_hi(u):
                            nk = keys(units[u][0])[1]
                            act.wait_ge(tr_done, u + 1)
                            if u >= 2:
                                act.wait_ge(pv_done, u - 1)
                            act.activation(pT_hi[:, u % 2, 0:nk], ps_t[:, 0:nk], ACT.Copy).then_inc(p_hi_done, 1)

                        def y_hi(n):
                            act.wait_ge(yt_done, n + 1)
                            act.activation(aT_hi[:, G0:KT, n * P:(n + 1) * P], ps_y[:].rearrange("p (k t) -> p k t", k=QF),
                                           ACT.Copy).then_inc(y_hi_done, 1)

                        for u, (n, hd) in enumerate(units):
                            if u >= 1:
                                prob_hi(u - 1)
                            if hd == 3 and n >= 1:
                                y_hi(n - 1)
                            nk = keys(n)[1]
                            act.wait_ge(neg_done, u + 1)
                            if u >= 4:
                                act.wait_ge(rec_done, u - 3)
                            act.activation(prob[:, u % 2, 0:nk], prob[:, u % 2, 0:nk], ACT.Exp, bias=neg[:, u % 2:u % 2 + 1],
                                           accum_out=rsum[:, u % 4:u % 4 + 1]).then_inc(exp_done, 1)
                        prob_hi(NU - 1)
                        y_hi(TT - 1)

                    @block.vector
                    def _(dve):
                        for n, (_, hi, lo) in enumerate(pieces):
                            dve.wait_ge(sp_hi, n + 1)
                            dve.tensor_tensor(lo, raw_of(n), hi, ALU.subtract).then_inc(sp_lo, 1)
                        dve.wait_ge(masked, 2)

                        def prob_lo(u):
                            nk = keys(units[u][0])[1]
                            dve.wait_ge(p_hi_done, u + 1)
                            dve.tensor_tensor(pT_lo[:, u % 2, 0:nk], ps_t[:, 0:nk], pT_hi[:, u % 2, 0:nk], ALU.subtract).then_inc(p_lo_done, 1)

                        def out_of(u):
                            n, hd = units[u]
                            dve.wait_ge(exp_done, u + 1)
                            dve.reciprocal(rinv[:, u % 2:u % 2 + 1], rsum[:, u % 4:u % 4 + 1]).then_inc(rec_done, 1)
                            dve.wait_ge(rec_done, u + 1)
                            dve.wait_ge(pv_done, u + 1)
                            if hd == 0 and n >= 2:
                                dve.wait_ge(yt_done, n - 1)
                            dve.tensor_scalar(y_sb[:, n % 2, hd * B_HD:(hd + 1) * B_HD], ps_o[:, 0:B_HD],
                                              rinv[:, u % 2:u % 2 + 1], None, ALU.mult).then_inc(y_done, 1)

                        def y_lo(n):
                            dve.wait_ge(y_hi_done, n + 1)
                            dve.tensor_tensor(aT_lo[:, G0:KT, n * P:(n + 1) * P], ps_y[:].rearrange("p (k t) -> p k t", k=QF),
                                              aT_hi[:, G0:KT, n * P:(n + 1) * P], ALU.subtract).then_inc(y_lo_done, 1)

                        for u, (n, hd) in enumerate(units):
                            nk = keys(n)[1]
                            dve.wait_ge(s_done, u + 1)
                            if u >= 2:
                                dve.wait_ge(tr_done, u - 1)
                            dve.tensor_tensor_reduce(out=prob[:, u % 2, 0:nk], in0=ps_s[u % 2][:, 0:nk], in1=backwards(bias[:, hd, 0:nk]),
                                                     scale=1.0, scalar=LOWEST, op0=ALU.add, op1=ALU.max,
                                                     accum_out=top_s[:, u % 2:u % 2 + 1]).then_inc(max_done, 1)
                            dve.wait_ge(max_done, u + 1)
                            dve.tensor_scalar(neg[:, u % 2:u % 2 + 1], top_s[:, u % 2:u % 2 + 1], -1.0, None, ALU.mult).then_inc(neg_done, 1)
                            if u >= 2:
                                out_of(u - 2)
                            if u >= 1:
                                prob_lo(u - 1)
                            if hd == 3 and n >= 1:
                                y_lo(n - 1)
                        out_of(NU - 2)
                        prob_lo(NU - 1)
                        out_of(NU - 1)
                        y_lo(TT - 1)

                    @block.tensor
                    def _(pe):
                        def scores(u):
                            n, hd = units[u]
                            k0, nk = keys(n)
                            if n == 0 and hd % 2 == 0:
                                pe.wait_ge(sp_lo, 2 * (hd // 2) + 2)
                            if u >= 2:
                                pe.wait_ge(max_done, u - 1)
                            rows, f, tok = slice((hd % 2) * B_HD, (hd % 2 + 1) * B_HD), hd // 2, slice(n * P, (n + 1) * P)
                            for c in range(0, nk, HALF):
                                w = min(HALF, nk - c)
                                last = three(pe, ps_s[u % 2][:, c:c + w], q_hi[rows, f, tok], q_lo[rows, f, tok],
                                             k_hi[rows, f, k0 + c:k0 + c + w], k_lo[rows, f, k0 + c:k0 + c + w], True, True)
                            last.then_inc(s_done, 1)

                        def transposes(u):
                            nk = keys(units[u][0])[1]
                            pe.wait_ge(exp_done, u + 1)
                            if u >= 1:
                                pe.wait_ge(p_lo_done, u)
                            for c in range(0, nk, P):
                                last = pe.transpose(ps_t[:, c:c + P], prob[:, u % 2, c:c + P], ident[:])
                            last.then_inc(tr_done, 1)

                        def values(u):
                            n, hd = units[u]
                            k0, nk = keys(n)
                            pe.wait_ge(p_lo_done, u + 1)
                            if u >= 1:
                                pe.wait_ge(y_done, u)
                            if hd == 0:
                                pe.wait_ge(sp_lo, 2 * QF + n // 2 + 1)
                            col = slice(hd * B_HD, (hd + 1) * B_HD)
                            for c in range(0, nk, P):
                                kt = (k0 + c) // P
                                last = three(pe, ps_o[:, 0:B_HD], pT_hi[:, u % 2, c:c + P], pT_lo[:, u % 2, c:c + P],
                                             v_hi[:, kt, col], v_lo[:, kt, col], c == 0, c + P == nk)
                            last.then_inc(pv_done, 1)

                        def y_transposes(n):
                            pe.wait_ge(y_done, B_HEADS * (n + 1))
                            if n >= 1:
                                pe.wait_ge(y_lo_done, n)
                            for k in range(QF):
                                last = pe.transpose(ps_y[:, k * P:(k + 1) * P], y_sb[:, n % 2, k * P:(k + 1) * P], ident[:])
                            last.then_inc(yt_done, 1)

                        scores(0)
                        for u, (n, hd) in enumerate(units):
                            if u + 1 < NU:
                                scores(u + 1)
                            transposes(u)
                            if u >= 1:
                                values(u - 1)
                            if hd == 2 and n >= 1:
                                y_transposes(n - 1)
                        values(NU - 1)
                        y_transposes(TT - 1)

        def memory_stage(mk_hi, mk_lo, mv_hi, mv_lo):
            mem_in, mt_tr, mt_hi, mt_lo = sem("me_in"), sem("me_tr"), sem("me_thi"), sem("me_tlo")
            raw_in = [sem(f"me_raw_in{i}") for i in range(4)]
            hi_done, lo_done, mm_done, out_hi, out_lo = sem("me_hi"), sem("me_lo"), sem("me_mm"), sem("me_out_hi"), sem("me_out_lo")
            PIECES = 4
            weights = [(w_xk, 0), (w_xk, 1), (w_xv, 0), (w_xv, 1)]
            units = [(b, i) for b in range(4) for i in range(4 if b < 2 else MT)]
            ends = [4, 8, 8 + MT, 8 + 2 * MT]
            with ExitStack() as stage:
                sb, pb = local(stage)
                mraw = sb("me_mraw", [P, MT, D])
                mT_hi, mT_lo = sb("me_mT_hi", [P, KT, MEM], F32R), sb("me_mT_lo", [P, KT, MEM], F32R)
                raw = sb("me_raw", [P, 4, 2, HALF])
                w_hi, w_lo = sb("me_whi", [P, 2, KT, HALF], F32R), sb("me_wlo", [P, 2, KT, HALF], F32R)
                ps_t = pb("me_ps_t", MT * D)
                ps = [pb(f"me_ps{i}", HALF) for i in range(4)]

                def target(u, mk, mv):
                    b, i = units[u]
                    if b < 2:
                        return mk[:, b * 4 + i, :], ps[u % 4][:, 0:MEM]
                    return mv[:, i, (b - 2) * HALF:(b - 1) * HALF], ps[u % 4][:]

                with nc.Block() as block:
                    @block.sync
                    def _(sp):
                        sp.dma_start(mraw[:], mem.rearrange("(a p) d -> p a d", p=P)).then_inc(mem_in, 16)
                        for n in range(4 * PIECES):
                            b, q = divmod(n, PIECES)
                            w, c = weights[b]
                            if n >= 4:
                                sp.wait_ge(lo_done, n - 3)
                            src = w[2 * q * P:2 * (q + 1) * P, c * HALF:(c + 1) * HALF].rearrange("(a p) n -> p a n", p=P)
                            sp.dma_start(raw[:, n % 4, :, :], src).then_inc(raw_in[n % 4], 16)

                    @block.gpsimd
                    def _(pool):
                        for n in range(4 * PIECES):
                            b, q = divmod(n, PIECES)
                            pool.wait_ge(hi_done, n + 1)
                            pool.tensor_tensor(w_lo[:, b % 2, 2 * q:2 * q + 2, :], raw[:, n % 4, :, :],
                                               w_hi[:, b % 2, 2 * q:2 * q + 2, :], ALU.subtract).then_inc(lo_done, 1)

                    @block.scalar
                    def _(act):
                        act.wait_ge(mt_tr, 1)
                        for a in range(MT):
                            act.activation(mT_hi[:, :, a * P:(a + 1) * P], ps_t[:, a * D:(a + 1) * D].rearrange("p (k m) -> p k m", k=KT),
                                           ACT.Copy).then_inc(mt_hi, 1)
                        n = 0
                        for u, (b, i) in enumerate(units):
                            while n < min(4 * PIECES, (b + 2) * PIECES):
                                nb, q = divmod(n, PIECES)
                                act.wait_ge(raw_in[n % 4], 16 * (n // 4 + 1))
                                if nb >= 2:
                                    act.wait_ge(mm_done, ends[nb - 2])
                                act.activation(w_hi[:, nb % 2, 2 * q:2 * q + 2, :], raw[:, n % 4, :, :], ACT.Copy).then_inc(hi_done, 1)
                                n += 1
                            act.wait_ge(mm_done, u + 1)
                            to, src = target(u, mk_hi, mv_hi)
                            act.activation(to, src, ACT.Copy).then_inc(out_hi, 1)

                    @block.vector
                    def _(dve):
                        for a in range(MT):
                            dve.wait_ge(mt_hi, a + 1)
                            dve.tensor_tensor(mT_lo[:, :, a * P:(a + 1) * P], ps_t[:, a * D:(a + 1) * D].rearrange("p (k m) -> p k m", k=KT),
                                              mT_hi[:, :, a * P:(a + 1) * P], ALU.subtract).then_inc(mt_lo, 1)
                        for u in range(len(units)):
                            dve.wait_ge(out_hi, u + 1)
                            hi, src = target(u, mk_hi, mv_hi)
                            lo, _ = target(u, mk_lo, mv_lo)
                            dve.tensor_tensor(lo, src, hi, ALU.subtract).then_inc(out_lo, 1)

                    @block.tensor
                    def _(pe):
                        pe.wait_ge(mem_in, 16)
                        for a in range(MT):
                            for k in range(KT):
                                last = pe.transpose(ps_t[:, a * D + k * P:a * D + (k + 1) * P], mraw[:, a, k * P:(k + 1) * P], ident[:])
                        last.then_inc(mt_tr, 1)
                        pe.wait_ge(mt_lo, MT)
                        for u, (b, i) in enumerate(units):
                            if u >= 4:
                                pe.wait_ge(out_lo, u - 3)
                            for k in range(KT):
                                if i == 0 and k % 2 == 0:
                                    pe.wait_ge(lo_done, b * PIECES + k // 2 + 1)
                                at = slice(i * P, (i + 1) * P)
                                if b < 2:
                                    last = three(pe, ps[u % 4][:, 0:MEM], w_hi[:, b % 2, k, at], w_lo[:, b % 2, k, at],
                                                 mT_hi[:, k, :], mT_lo[:, k, :], k == 0, k == KT - 1)
                                else:
                                    last = three(pe, ps[u % 4][:], mT_hi[:, k, at], mT_lo[:, k, at],
                                                 w_hi[:, b % 2, k, :], w_lo[:, b % 2, k, :], k == 0, k == KT - 1)
                            last.then_inc(mm_done, 1)

        def cross_stage(mk_hi, mk_lo, mv_hi, mv_lo):
            q_in = [sem(f"xa_q_in{i}") for i in range(2)]
            q_hi_done, q_lo_done, s_done = sem("xa_q_hi"), sem("xa_q_lo"), sem("xa_s")
            max_done, neg_done, exp_done = sem("xa_max"), sem("xa_neg"), sem("xa_exp")
            tr_done, p_hi_done, p_lo_done, pv_done = sem("xa_tr"), sem("xa_p_hi"), sem("xa_p_lo"), sem("xa_pv")
            rec_done, o_done, ot_done, o_hi_done, o_lo_done = sem("xa_rec"), sem("xa_o"), sem("xa_ot"), sem("xa_o_hi"), sem("xa_o_lo")
            SCALE = float(X_HD) ** -0.5
            HC = X_HD // P
            with ExitStack() as stage:
                sb, pb = local(stage)
                q_raw = sb("xa_q_raw", [P, 2, KT, P])
                q_hi, q_lo = sb("xa_q_hi_sb", [P, 2, KT, P], F32R), sb("xa_q_lo_sb", [P, 2, KT, P], F32R)
                prob = sb("xa_prob", [P, 2, X_HEADS, MEM])
                pT_hi, pT_lo = sb("xa_pT_hi", [P, 2, X_HEADS * MT, P], F32R), sb("xa_pT_lo", [P, 2, X_HEADS * MT, P], F32R)
                topm, neg = sb("xa_top", [P, 2, X_HEADS]), sb("xa_neg_sb", [P, 2, X_HEADS])
                rsum, rinv = sb("xa_rsum", [P, 2, X_HEADS]), sb("xa_rinv", [P, 2, X_HEADS])
                o_sb = sb("xa_o_sb", [P, 2, X_HEADS, X_HD])
                ps_s, ps_t, ps_o, ps_ot = pb("xa_ps_s", D), pb("xa_ps_t", D), pb("xa_ps_o", D), pb("xa_ps_ot", D)

                with nc.Block() as block:
                    @block.sync
                    def _(sp):
                        for j in range(TT):
                            if j >= 2:
                                sp.wait_ge(q_lo_done, j - 1)
                            sp.dma_start(q_raw[:, j % 2, :, :], xq_d[:, j * P:(j + 1) * P].rearrange("(k p) t -> p k t", p=P)).then_inc(q_in[j % 2], 16)

                    @block.scalar
                    def _(act):
                        def query_hi(j):
                            act.wait_ge(q_in[j % 2], 16 * (j // 2 + 1))
                            if j >= 2:
                                act.wait_ge(s_done, j - 1)
                            act.activation(q_hi[:, j % 2, :, :], q_raw[:, j % 2, :, :], ACT.Copy).then_inc(q_hi_done, 1)

                        def prob_hi(j):
                            act.wait_ge(tr_done, j + 1)
                            if j >= 2:
                                act.wait_ge(pv_done, j - 1)
                            act.activation(pT_hi[:, j % 2, :, :], ps_t[:].rearrange("p (k t) -> p k t", t=P), ACT.Copy).then_inc(p_hi_done, 1)

                        def out_hi(j):
                            act.wait_ge(ot_done, j + 1)
                            act.activation(aT_hi[:, :, j * P:(j + 1) * P], ps_ot[:].rearrange("p (k t) -> p k t", t=P), ACT.Copy).then_inc(o_hi_done, 1)

                        query_hi(0)
                        for j in range(TT):
                            if j + 1 < TT:
                                query_hi(j + 1)
                            act.wait_ge(neg_done, j + 1)
                            if j >= 2:
                                act.wait_ge(tr_done, j - 1)
                                act.wait_ge(rec_done, j - 1)
                            for hd in range(X_HEADS):
                                act.activation(prob[:, j % 2, hd, :], ps_s[:, hd * MEM:(hd + 1) * MEM], ACT.Exp, scale=SCALE,
                                               bias=neg[:, j % 2, hd:hd + 1], accum_out=rsum[:, j % 2, hd:hd + 1]).then_inc(exp_done, 1)
                            prob_hi(j)
                            if j >= 1:
                                out_hi(j - 1)
                        out_hi(TT - 1)

                    @block.vector
                    def _(dve):
                        def query_lo(j):
                            dve.wait_ge(q_hi_done, j + 1)
                            dve.tensor_tensor(q_lo[:, j % 2, :, :], q_raw[:, j % 2, :, :], q_hi[:, j % 2, :, :], ALU.subtract).then_inc(q_lo_done, 1)

                        def out_lo(j):
                            dve.wait_ge(o_hi_done, j + 1)
                            dve.tensor_tensor(aT_lo[:, :, j * P:(j + 1) * P], ps_ot[:].rearrange("p (k t) -> p k t", t=P),
                                              aT_hi[:, :, j * P:(j + 1) * P], ALU.subtract).then_inc(o_lo_done, 1)

                        query_lo(0)
                        for j in range(TT):
                            i = j % 2
                            if j + 1 < TT:
                                query_lo(j + 1)
                            dve.wait_ge(s_done, j + 1)
                            dve.tensor_reduce(topm[:, i, :], ps_s[:].rearrange("p (h m) -> p h m", h=X_HEADS), AX.X, ALU.max).then_inc(max_done, 1)
                            dve.wait_ge(max_done, j + 1)
                            dve.tensor_scalar(neg[:, i, :], topm[:, i, :], -SCALE, None, ALU.mult).then_inc(neg_done, 1)
                            dve.wait_ge(p_hi_done, j + 1)
                            dve.tensor_tensor(pT_lo[:, i, :, :], ps_t[:].rearrange("p (k t) -> p k t", t=P), pT_hi[:, i, :, :], ALU.subtract).then_inc(p_lo_done, 1)
                            if j >= 1:
                                out_lo(j - 1)
                            dve.reciprocal(rinv[:, i, :], rsum[:, i, :]).then_inc(rec_done, 1)
                            dve.wait_ge(rec_done, j + 1)
                            dve.wait_ge(pv_done, j + 1)
                            dve.tensor_tensor(o_sb[:, i, :, :], ps_o[:].rearrange("p (h d) -> p h d", h=X_HEADS),
                                              rinv[:, i, :].unsqueeze(2).broadcast_to([P, X_HEADS, X_HD]), ALU.mult).then_inc(o_done, 1)
                        out_lo(TT - 1)

                    @block.tensor
                    def _(pe):
                        def scores(j):
                            pe.wait_ge(q_lo_done, j + 1)
                            if j >= 1:
                                pe.wait_ge(exp_done, X_HEADS * j)
                            for hd in range(X_HEADS):
                                for c in range(HC):
                                    f = hd * HC + c
                                    last = three(pe, ps_s[:, hd * MEM:(hd + 1) * MEM], q_hi[:, j % 2, f, :], q_lo[:, j % 2, f, :],
                                                 mk_hi[:, f, :], mk_lo[:, f, :], c == 0, c == HC - 1)
                            last.then_inc(s_done, 1)

                        def out_transposes(j):
                            pe.wait_ge(o_done, j + 1)
                            if j >= 1:
                                pe.wait_ge(o_lo_done, j)
                            o = o_sb[:, j % 2, :, :].rearrange("p h d -> p (h d)")
                            for k in range(KT):
                                last = pe.transpose(ps_ot[:, k * P:(k + 1) * P], o[:, k * P:(k + 1) * P], ident[:])
                            last.then_inc(ot_done, 1)

                        scores(0)
                        for j in range(TT):
                            pe.wait_ge(exp_done, X_HEADS * (j + 1))
                            if j >= 1:
                                pe.wait_ge(p_lo_done, j)
                            for hd in range(X_HEADS):
                                for c in range(MT):
                                    at = (hd * MT + c) * P
                                    last = pe.transpose(ps_t[:, at:at + P], prob[:, j % 2, hd, c * P:(c + 1) * P], ident[:])
                            last.then_inc(tr_done, 1)
                            if j + 1 < TT:
                                scores(j + 1)
                            if j >= 1:
                                out_transposes(j - 1)
                            pe.wait_ge(p_lo_done, j + 1)
                            if j >= 1:
                                pe.wait_ge(o_done, j)
                            for hd in range(X_HEADS):
                                for c in range(MT):
                                    last = three(pe, ps_o[:, hd * X_HD:(hd + 1) * X_HD], pT_hi[:, j % 2, hd * MT + c, :], pT_lo[:, j % 2, hd * MT + c, :],
                                                 mv_hi[:, c, hd * X_HD:(hd + 1) * X_HD], mv_lo[:, c, hd * X_HD:(hd + 1) * X_HD], c == 0, c == MT - 1)
                            last.then_inc(pv_done, 1)
                        out_transposes(TT - 1)

        def key_score_stage():
            sk_in, sk_tr, sk_hi, sk_lo = sem("ks_sk_in"), sem("ks_sk_tr"), sem("ks_sk_hi"), sem("ks_sk_lo")
            raw_in = [sem(f"ks_raw_in{i}") for i in range(4)]
            hi_done, lo_done = sem("ks_hi"), sem("ks_lo")
            q_done, q_hi_done, q_lo_done = sem("ks_q"), sem("ks_q_hi"), sem("ks_q_lo")
            s_done, s_out = sem("ks_s"), sem("ks_s_out")
            stored = [sem(f"ks_stored{i}") for i in range(2)]
            HP, PIECES, NB = 2 * PH, 4, 4
            s_view = s_d.rearrange("(j h) t (q k) -> h q t j k", h=PH, q=2)
            with ExitStack() as stage:
                sb, pb = local(stage)
                sraw = sb("ks_sraw", [P, HP, P])
                sk_hi_sb, sk_lo_sb = sb("ks_skT_hi", [P, HP, P], F32R), sb("ks_skT_lo", [P, HP, P], F32R)
                raw = sb("ks_raw", [P, 4, 2, HALF])
                w_hi, w_lo = sb("ks_whi", [P, 2, KT, HALF], F32R), sb("ks_wlo", [P, 2, KT, HALF], F32R)
                q_hi, q_lo = sb("ks_qhi", [P, 2, T], F32R), sb("ks_qlo", [P, 2, T], F32R)
                res = sb("ks_res", [P, 2, TT, KEYS])
                ps_q = [pb(f"ks_ps_q{i}", HALF) for i in range(4)]
                ps_s = [pb(f"ks_ps_s{i}", D) for i in range(2)]
                with nc.Block() as block:
                    @block.sync
                    def _(sp):
                        def load(n):
                            b, q = divmod(n, PIECES)
                            if n >= 4:
                                sp.wait_ge(lo_done, n - 3)
                            src = w_pq[2 * q * P:2 * (q + 1) * P, b * HALF:(b + 1) * HALF].rearrange("(a p) n -> p a n", p=P)
                            sp.dma_start(raw[:, n % 4, :, :], src).then_inc(raw_in[n % 4], 16)

                        for n in range(PIECES):
                            load(n)
                        sp.dma_start(sraw[:], sub_keys.rearrange("h q k d -> k (h q) d")).then_inc(sk_in, 16)
                        for hp in range(HP + 1):
                            if hp // 4 + 1 < NB:
                                load(PIECES + hp)
                            if hp >= 1:
                                sp.wait_ge(s_out, hp)
                                sp.dma_start(s_view[(hp - 1) // 2, (hp - 1) % 2], res[:, (hp - 1) % 2, :, :]).then_inc(stored[(hp - 1) % 2], 16)
                        for i in range(2):
                            sp.wait_ge(stored[i], 16 * (HP // 2))

                    @block.gpsimd
                    def _(pool):
                        for n in range(NB * PIECES):
                            b, q = divmod(n, PIECES)
                            pool.wait_ge(hi_done, n + 1)
                            pool.tensor_tensor(w_lo[:, b % 2, 2 * q:2 * q + 2, :], raw[:, n % 4, :, :],
                                               w_hi[:, b % 2, 2 * q:2 * q + 2, :], ALU.subtract).then_inc(lo_done, 1)

                    @block.scalar
                    def _(act):
                        def split(n):
                            b, q = divmod(n, PIECES)
                            act.wait_ge(raw_in[n % 4], 16 * (n // 4 + 1))
                            if b >= 2:
                                act.wait_ge(q_done, 8 * (b - 1))
                            act.activation(w_hi[:, b % 2, 2 * q:2 * q + 2, :], raw[:, n % 4, :, :], ACT.Copy).then_inc(hi_done, 1)

                        for n in range(PIECES):
                            split(n)
                        for c in range(2):
                            act.wait_ge(sk_tr, c + 1)
                            act.activation(sk_hi_sb[:, 8 * c:8 * c + 8, :], ps_s[c][:].rearrange("p (k t) -> p k t", t=P), ACT.Copy).then_inc(sk_hi, 1)
                        for hp in range(HP):
                            if hp // 4 + 1 < NB:
                                split(PIECES + hp)
                            for th in range(2):
                                act.wait_ge(q_done, 2 * hp + th + 1)
                                if hp >= 2:
                                    act.wait_ge(s_done, hp - 1)
                                act.activation(q_hi[:, hp % 2, th * HALF:(th + 1) * HALF], ps_q[(2 * hp + th) % 4][:], ACT.Copy).then_inc(q_hi_done, 1)

                    @block.vector
                    def _(dve):
                        for c in range(2):
                            dve.wait_ge(sk_hi, c + 1)
                            dve.tensor_tensor(sk_lo_sb[:, 8 * c:8 * c + 8, :], ps_s[c][:].rearrange("p (k t) -> p k t", t=P),
                                              sk_hi_sb[:, 8 * c:8 * c + 8, :], ALU.subtract).then_inc(sk_lo, 1)

                        def scores_out(hp):
                            dve.wait_ge(s_done, hp + 1)
                            if hp >= 2:
                                dve.wait_ge(stored[hp % 2], 16 * (hp // 2))
                            dve.tensor_copy(res[:, hp % 2, :, :], ps_s[hp % 2][:].rearrange("p (k t) -> p k t", t=P)).then_inc(s_out, 1)

                        for hp in range(HP):
                            for th in range(2):
                                dve.wait_ge(q_hi_done, 2 * hp + th + 1)
                                dve.tensor_tensor(q_lo[:, hp % 2, th * HALF:(th + 1) * HALF], ps_q[(2 * hp + th) % 4][:],
                                                  q_hi[:, hp % 2, th * HALF:(th + 1) * HALF], ALU.subtract).then_inc(q_lo_done, 1)
                            if hp >= 1:
                                scores_out(hp - 1)
                        scores_out(HP - 1)

                    @block.tensor
                    def _(pe):
                        pe.wait_ge(sk_in, 16)
                        for hp in range(HP):
                            last = pe.transpose(ps_s[hp // 8][:, (hp % 8) * P:(hp % 8 + 1) * P], sraw[:, hp, :], ident[:])
                            if hp % 8 == 7:
                                last.then_inc(sk_tr, 1)

                        def scores(hp):
                            pe.wait_ge(q_lo_done, 2 * hp + 2)
                            if hp < 2:
                                pe.wait_ge(sk_lo, 2)
                            else:
                                pe.wait_ge(s_out, hp - 1)
                            for j in range(TT):
                                tok = slice(j * P, (j + 1) * P)
                                last = three(pe, ps_s[hp % 2][:, tok], q_hi[:, hp % 2, tok], q_lo[:, hp % 2, tok],
                                             sk_hi_sb[:, hp, :], sk_lo_sb[:, hp, :], True, True)
                            last.then_inc(s_done, 1)

                        for hp in range(HP):
                            b, f = divmod(hp, 4)
                            for th in range(2):
                                u = 2 * hp + th
                                if u >= 4:
                                    pe.wait_ge(q_lo_done, u - 3)
                                for k in range(KT):
                                    if f == 0 and th == 0 and k % 2 == 0:
                                        pe.wait_ge(lo_done, b * PIECES + k // 2 + 1)
                                    col, tok = slice(f * P, (f + 1) * P), slice(th * HALF, (th + 1) * HALF)
                                    last = three(pe, ps_q[u % 4][:], w_hi[:, b % 2, k, col], w_lo[:, b % 2, k, col],
                                                 aT_hi[:, k, tok], aT_lo[:, k, tok], k == 0, k == KT - 1)
                                last.then_inc(q_done, 1)
                            if hp >= 1:
                                scores(hp - 1)
                        scores(HP - 1)

        def expert_in_stage():
            ROUTE_STEPS, ROUTE_E = 32, 2
            GATE_STEPS, GATE_E = 16, 4
            HALF_E = ROUTE_STEPS * ROUTE_E
            ETILES = HALF_E + GATE_STEPS * GATE_E
            u_rows = expert_u.rearrange("(p e) d -> e p d", e=P)

            raw_in = [sem(f"ei_raw_in{i}") for i in range(2)]
            tr_done, uT_hi_done, uT_lo_done = sem("ei_tr"), sem("ei_uT_hi"), sem("ei_uT_lo")
            mm_done = sem("ei_mm")
            gelu_done = [sem(f"ei_gelu{i}") for i in range(2)]
            act_stored = [sem(f"ei_act_stored{i}") for i in range(2)]
            iota_done, rank = sem("ei_iota"), sem("ei_rank")
            s_in = [sem(f"ei_s_in{i}") for i in range(2)]
            top_done, exp_done = sem("ei_top"), sem("ei_exp")
            route_done, rt_done, rt_out = sem("ei_route"), sem("ei_rt"), sem("ei_rt_out")
            rt_stored = [sem(f"ei_rt_stored{i}") for i in range(2)]
            col_in = [sem(f"ei_col_in{i}") for i in range(2)]
            hot = sem("ei_hot")
            hot_done = [sem(f"ei_hot_done{i}") for i in range(2)]
            g_done = [[sem(f"ei_g_done{i}{g}") for g in range(2)] for i in range(2)]
            g_out = [sem(f"ei_g_out{i}") for i in range(2)]
            g_stored = [sem(f"ei_g_stored{i}") for i in range(2)]
            BATCH, GROUP = 8, 4
            BATCHES = GBLK // BATCH

            def route_step(it, s):
                return it * ROUTE_E + s, s, it + 0, s

            def gate_step(it, s):
                return it * GATE_E + (HALF_E + s), s % 2, it * (GATE_E // 2) + (HALF_E // 2 + s // 2), s

            with ExitStack() as stage:
                sb, pb = local(stage)
                u_raw = sb("ei_u_raw", [P, 2, D])
                uT_hi, uT_lo = sb("ei_uT_hi_sb", [P, 2, KT, P], F32R), sb("ei_uT_lo_sb", [P, 2, KT, P], F32R)
                act_sb = sb("ei_act", [P, 2, T])
                iota = sb("ei_iota_sb", [P, P])
                s_sb = sb("ei_s", [P, 2, 2, KEYS])
                s_left = sb("ei_s_left", [P, 2, KEYS])
                kv = sb("ei_kv", [P, 2, TOPK])
                ki = sb("ei_ki", [P, 2, TOPK], U32)
                kf = sb("ei_kf", [P, 2, TOPK])
                pair, pair_left = sb("ei_pair", [P, TOPK, TOPK]), sb("ei_pair_left", [P, TOPK, TOPK])
                gv, gi = sb("ei_gv", [P, 2, TOPK]), sb("ei_gi", [P, TOPK], U32)
                gpos, gpf = sb("ei_gpos", [P, 2, TOPK], U32), sb("ei_gpf", [P, 2, TOPK])
                pick = sb("ei_pick", [P, 2, TOPK, TOPK])
                gneg, gexp = sb("ei_gneg", [P, 2]), sb("ei_gexp", [P, 2, TOPK])
                gsum, ginv = sb("ei_gsum", [P, 2]), sb("ei_ginv", [P, 2])
                route = sb("ei_route_sb", [P, 2, TOPK, 3])
                routeT = sb("ei_routeT", [3 * TOPK, 2, P])
                col = sb("ei_col", [P, 2, 3, GBLK])
                w_hi, w_lo = sb("ei_w_hi", [P, 2, GBLK], F32R), sb("ei_w_lo", [P, 2, GBLK], F32R)
                hot1 = sb("ei_hot1", [P, 2, BATCH, P], F32R)
                hot2 = sb("ei_hot2", [P, 2, BATCH, P])
                hw_hi, hw_lo = sb("ei_hw_hi", [P, 2, BATCH, P], F32R), sb("ei_hw_lo", [P, 2, BATCH, P], F32R)
                gate_sb = sb("ei_gate", [P, 2, P, GBLK])
                ps_t = pb("ei_ps_t", D)
                ps_h = [pb(f"ei_ps_h{i}", T) for i in range(2)]
                ps_x = [pb(f"ei_ps_x{i}", HALF) for i in range(2)]
                route_cols = route_d.rearrange("(j h) (k q) t -> j (h k) q t", h=PH, q=3)
                RANKS = 24
                HOTS = 2 + 3 * BATCHES

                with nc.Block() as block:
                    @block.sync
                    def _(sp):
                        def load_expert(step):
                            e, i, _, _ = step
                            sp.wait_ge(tr_done, e + 1)
                            sp.dma_start(u_raw[:, i, :], u_rows[e + 2, :, :]).then_inc(raw_in[i], 16)

                        def store_act(step):
                            e, i, n, _ = step
                            sp.wait_ge(gelu_done[i], n + 1)
                            sp.dma_start(act_d[e, :, :], act_sb[:, i, :]).then_inc(act_stored[i], 16)

                        def load_scores(u, i):
                            sp.dma_start(s_sb[:, i, :, :], s_d[u].rearrange("t (q k) -> t q k", q=2)).then_inc(s_in[i], 16)

                        def store_route(u, i):
                            sp.wait_ge(rt_out, u + 1)
                            sp.dma_start(route_d[u, :, :], routeT[:, i, :]).then_inc(rt_stored[i], 16)

                        def load_col(tile, off, b):
                            src = route_cols[tile][:, :, bass.ds(off, GBLK)]
                            sp.dma_start(col[:, b, :, :], src).then_inc(col_in[b], 16)

                        def store_gate(it, b):
                            sp.wait_ge(g_out[1], (it * 2 + (b + 1)) * BATCHES)
                            sp.dma_start(gate_d[it * 2 + b], gate_sb[:, b, :, :]).then_inc(g_stored[b], 16)

                        for i in range(2):
                            sp.dma_start(u_raw[:, i, :], u_rows[i, :, :]).then_inc(raw_in[i], 16)
                            load_scores(i, i)

                        def route_body(it, more):
                            for s in range(ROUTE_E):
                                step = route_step(it, s)
                                load_expert(step)
                                if more:
                                    sp.wait_ge(rank, (step[0] + 1) * RANKS)
                                    load_scores(step[0] + 2, s)
                                store_route(step[0], s)
                                store_act(step)

                        with sp.Fori(0, ROUTE_STEPS - 1) as it:
                            route_body(it, True)
                        route_body(ROUTE_STEPS - 1, False)
                        for i in range(2):
                            sp.wait_ge(rt_stored[i], 16 * (UNITS // 2))
                        load_col(0, 0, 0)
                        load_col(0, GBLK, 1)

                        def gate_body(it, more):
                            for s in range(GATE_E):
                                step = gate_step(it, s)
                                if more or s < GATE_E - 2:
                                    load_expert(step)
                                if s % 2 == 1:
                                    store_gate(it, s // 2)
                                    if more:
                                        load_col((it + 1) // 2, ((it + 1) % 2) * (2 * GBLK) + s // 2 * GBLK, s // 2)
                                store_act(step)

                        with sp.Fori(0, GATE_STEPS - 1) as it:
                            gate_body(it, True)
                        gate_body(GATE_STEPS - 1, False)
                        for i in range(2):
                            sp.wait_ge(act_stored[i], 16 * (ETILES // 2))
                            sp.wait_ge(g_stored[i], 16 * GATE_STEPS)

                    @block.gpsimd
                    def _(pool):
                        pool.iota(iota[:], [[1, P]], base=0, channel_multiplier=0,
                                  allow_small_or_imprecise_dtypes=True).then_inc(iota_done, 1)

                    @block.scalar
                    def _(act):
                        def next_hi(step):
                            e, i, _, _ = step
                            act.wait_ge(tr_done, e + 2)
                            act.wait_ge(mm_done, e)
                            act.activation(uT_hi[:, 1 - i, :, :], ps_t[:].rearrange("p (k t) -> p k t", t=P), ACT.Copy).then_inc(uT_hi_done, 1)

                        def gelu(step):
                            e, i, n, _ = step
                            act.wait_ge(mm_done, e + 1)
                            act.wait_ge(act_stored[i], n * 16)
                            act.activation(act_sb[:, i, :], ps_h[i][:], ACT.Gelu).then_inc(gelu_done[i], 1)

                        act.wait_ge(tr_done, 1)
                        act.activation(uT_hi[:, 0, :, :], ps_t[:].rearrange("p (k t) -> p k t", t=P), ACT.Copy).then_inc(uT_hi_done, 1)

                        with act.Fori(0, ROUTE_STEPS) as it:
                            for s in range(ROUTE_E):
                                step = route_step(it, s)
                                u, i, n, _ = step
                                next_hi(step)
                                act.wait_ge(top_done, u + 1)
                                act.activation(gexp[:, i, :], gv[:, i, :], ACT.Exp, bias=gneg[:, i:i + 1],
                                               accum_out=gsum[:, i:i + 1]).then_inc(exp_done, 1)
                                gelu(step)
                                act.wait_ge(rt_done, u + 1)
                                act.wait_ge(rt_stored[i], n * 16)
                                act.activation(routeT[:, i, :], ps_x[i][0:3 * TOPK, 0:P], ACT.Copy).then_inc(rt_out, 1)

                        def gates_out(it, s, m, gh):
                            b = s // 2
                            act.wait_ge(g_done[m % 2][gh], it * BATCHES + (b * (BATCHES // 2) + m // 2 + 1))
                            if m == 0 and gh == 0:
                                act.wait_ge(g_stored[b], it * 16)
                            t0 = m * BATCH + gh * GROUP
                            act.activation(gate_sb[:, b, :, t0:t0 + GROUP].rearrange("p i t -> p t i"),
                                           ps_x[gh][:].rearrange("p (t i) -> p t i", i=P), ACT.Copy).then_inc(g_out[gh], 1)

                        def gate_body(it, more):
                            for s in range(GATE_E):
                                step = gate_step(it, s)
                                if more or s < GATE_E - 1:
                                    next_hi(step)
                                for q in range(4):
                                    gates_out(it, s, 2 * (s % 2) + q // 2, q % 2)
                                gelu(step)

                        with act.Fori(0, GATE_STEPS - 1) as it:
                            gate_body(it, True)
                        gate_body(GATE_STEPS - 1, False)

                    @block.vector
                    def _(dve):
                        def next_lo(step):
                            e, i, _, _ = step
                            dve.wait_ge(uT_hi_done, e + 2)
                            dve.tensor_tensor(uT_lo[:, 1 - i, :, :], ps_t[:].rearrange("p (k t) -> p k t", t=P), uT_hi[:, 1 - i, :, :],
                                              ALU.subtract).then_inc(uT_lo_done, 1)

                        count_reg = dve.alloc_register("ei_count")

                        def wait_apart(signal, count):
                            dve.reg_mov(count_reg, count)
                            dve.wait_ge(iota_done, 1)
                            dve.wait_ge(signal, count_reg)

                        def rank_unit(step):
                            u, i, n, _ = step
                            links = [0]

                            def link(ins, wait=True):
                                links[0] += 1
                                ins.then_inc(rank, 1)
                                if wait:
                                    wait_apart(rank, u * RANKS + links[0])

                            wait_apart(s_in[i], n * 16 + 16)
                            for q in range(2):
                                src = s_sb[:, i, q, :]
                                link(dve.max(kv[:, q, 0:8], src))
                                link(dve.match_replace(out=s_left[:, q, :], in_to_replace=kv[:, q, 0:8], in_values=src, imm_value=LOWEST), False)
                                link(dve.max_index(ki[:, q, 0:8], kv[:, q, 0:8], src))
                                link(dve.max(kv[:, q, 8:16], s_left[:, q, :]))
                                link(dve.max_index(ki[:, q, 8:16], kv[:, q, 8:16], s_left[:, q, :]), q == 1)
                            link(dve.tensor_copy(kf[:], ki[:]), False)
                            link(dve.tensor_tensor(pair[:], kv[:, 0, :].unsqueeze(2).broadcast_to([P, TOPK, TOPK]),
                                                   kv[:, 1, :].unsqueeze(1).broadcast_to([P, TOPK, TOPK]), ALU.add))
                            flat, left = pair[:].rearrange("p a b -> p (a b)"), pair_left[:].rearrange("p a b -> p (a b)")
                            link(dve.max(gv[:, i, 0:8], flat))
                            link(dve.match_replace(out=left, in_to_replace=gv[:, i, 0:8], in_values=flat, imm_value=LOWEST), False)
                            link(dve.max_index(gi[:, 0:8], gv[:, i, 0:8], flat))
                            link(dve.max(gv[:, i, 8:16], left))
                            link(dve.max_index(gi[:, 8:16], gv[:, i, 8:16], left))
                            dve.tensor_scalar(gneg[:, i:i + 1], gv[:, i, 0:1], -1.0, None, ALU.mult).then_inc(top_done, 1)
                            link(dve.tensor_scalar(gpos[:, 0, :], gi[:], 4, None, ALU.logical_shift_right), False)
                            link(dve.tensor_scalar(gpos[:, 1, :], gi[:], TOPK - 1, None, ALU.bitwise_and))
                            link(dve.tensor_copy(gpf[:], gpos[:]))
                            link(dve.tensor_tensor(pick[:], gpf[:].unsqueeze(3).broadcast_to([P, 2, TOPK, TOPK]),
                                                   iota[:, 0:TOPK].unsqueeze(1).unsqueeze(1).broadcast_to([P, 2, TOPK, TOPK]), ALU.is_equal))
                            link(dve.tensor_tensor(pick[:], pick[:], kf[:].unsqueeze(2).broadcast_to([P, 2, TOPK, TOPK]), ALU.mult))
                            dve.wait_ge(rt_done, it_floor(u, i))
                            link(dve.tensor_reduce(route[:, i, :, 1:3].rearrange("p k q -> p q k"), pick[:], AX.X, ALU.add), False)
                            return link

                        def it_floor(u, i):
                            return u - i

                        def weigh_unit(step, link):
                            u, i, _, _ = step
                            dve.wait_ge(exp_done, u + 1)
                            link(dve.reciprocal(ginv[:, i:i + 1], gsum[:, i:i + 1]))
                            dve.tensor_scalar(route[:, i, :, 0], gexp[:, i, :], ginv[:, i:i + 1], None, ALU.mult).then_inc(route_done, 1)

                        dve.wait_ge(uT_hi_done, 1)
                        dve.tensor_tensor(uT_lo[:, 0, :, :], ps_t[:].rearrange("p (k t) -> p k t", t=P), uT_hi[:, 0, :, :],
                                          ALU.subtract).then_inc(uT_lo_done, 1)
                        dve.wait_ge(iota_done, 1)
                        with dve.Fori(0, ROUTE_STEPS) as it:
                            for s in range(ROUTE_E):
                                step = route_step(it, s)
                                link = rank_unit(step)
                                next_lo(step)
                                weigh_unit(step, link)

                        def batch(it, b, m):
                            i, t0 = m % 2, m * BATCH
                            before = it * BATCHES + (b * (BATCHES // 2) + m // 2)
                            base = it * (2 * HOTS) + (b * HOTS + 2 + 3 * m)
                            keys = iota[:].unsqueeze(1).broadcast_to([P, BATCH, P])

                            def per_token(t):
                                return t.unsqueeze(2).broadcast_to([P, BATCH, P])

                            dve.wait_ge(g_done[i][1], before)
                            dve.tensor_tensor(hot2[:, i, :, :], keys, per_token(col[:, b, 2, t0:t0 + BATCH]), ALU.is_equal).then_inc(hot, 1)
                            dve.tensor_tensor(hot1[:, i, :, :], keys, per_token(col[:, b, 1, t0:t0 + BATCH]), ALU.is_equal).then_inc(hot, 1)
                            dve.wait_ge(hot, base + 1)
                            dve.tensor_tensor(hw_hi[:, i, :, :], hot2[:, i, :, :], per_token(w_hi[:, b, t0:t0 + BATCH].bitcast(F32)), ALU.mult).then_inc(hot, 1)
                            dve.tensor_tensor(hw_lo[:, i, :, :], hot2[:, i, :, :], per_token(w_lo[:, b, t0:t0 + BATCH].bitcast(F32)), ALU.mult).then_inc(hot_done[i], 1)

                        def gate_body(it, more):
                            for s in range(GATE_E):
                                step = gate_step(it, s)
                                b = s // 2
                                if s % 2 == 0:
                                    dve.wait_ge(col_in[b], it * 16 + 16)
                                    dve.tensor_copy(w_hi[:, b, :], col[:, b, 0, :]).then_inc(hot, 1)
                                    dve.wait_ge(hot, it * (2 * HOTS) + (b * HOTS + 1))
                                    dve.tensor_tensor(w_lo[:, b, :], col[:, b, 0, :], w_hi[:, b, :].bitcast(F32), ALU.subtract).then_inc(hot, 1)
                                    dve.wait_ge(hot, it * (2 * HOTS) + (b * HOTS + 2))
                                batch(it, b, 2 * (s % 2))
                                if more or s < GATE_E - 1:
                                    next_lo(step)
                                batch(it, b, 2 * (s % 2) + 1)

                        with dve.Fori(0, GATE_STEPS - 1) as it:
                            gate_body(it, True)
                        gate_body(GATE_STEPS - 1, False)

                    @block.tensor
                    def _(pe):
                        def transposes(i):
                            for k in range(KT):
                                last = pe.transpose(ps_t[:, k * P:(k + 1) * P], u_raw[:, i, k * P:(k + 1) * P], ident[:])
                            last.then_inc(tr_done, 1)

                        def next_transposes(step):
                            e, i, n, _ = step
                            pe.wait_ge(raw_in[1 - i], (n + i) * 16 + 16)
                            pe.wait_ge(uT_lo_done, e + 1)
                            transposes(1 - i)

                        def product(step, between):
                            e, i, n, _ = step
                            pe.wait_ge(uT_lo_done, e + 1)
                            pe.wait_ge(gelu_done[i], n)
                            q = 0
                            for c in range(2):
                                tok = slice(c * HALF, (c + 1) * HALF)
                                for k in range(KT):
                                    last = three(pe, ps_h[i][:, tok], uT_hi[:, i, k, :], uT_lo[:, i, k, :],
                                                 aT_hi[:, k, tok], aT_lo[:, k, tok], k == 0, k == KT - 1)
                                    if k == KT - 1 and c == 1:
                                        last.then_inc(mm_done, 1)
                                    if k % (KT // 2) == KT // 2 - 1:
                                        between(q)
                                        q += 1

                        pe.wait_ge(raw_in[0], 16)
                        transposes(0)

                        with pe.Fori(0, ROUTE_STEPS) as it:
                            for s in range(ROUTE_E):
                                step = route_step(it, s)
                                u, i, _, _ = step
                                next_transposes(step)
                                product(step, lambda q: None)
                                pe.wait_ge(raw_in[0], 16)
                                pe.wait_ge(route_done, u + 1)
                                pe.wait_ge(rt_out, u - i)
                                pe.transpose(ps_x[i][0:3 * TOPK, 0:P], route[:, i, :, :].rearrange("p k q -> p (k q)"), ident[:]).then_inc(rt_done, 1)
                        pe.wait_ge(rt_out, UNITS)

                        def gates(it, s, m, gh):
                            b, i = s // 2, m % 2
                            pe.wait_ge(hot_done[i], it * BATCHES + (b * (BATCHES // 2) + m // 2 + 1))
                            pe.wait_ge(g_out[gh], it * (2 * BATCHES) + (b * BATCHES + m))
                            for t in range(GROUP):
                                at, tk = slice(t * P, (t + 1) * P), gh * GROUP + t
                                pe.matmul(ps_x[gh][:, at], hot1[:, i, tk, :], hw_hi[:, i, tk, :], start=True, stop=False)
                                last = pe.matmul(ps_x[gh][:, at], hot1[:, i, tk, :], hw_lo[:, i, tk, :], start=False, stop=True)
                            last.then_inc(g_done[i][gh], 1)

                        def gate_body(it, more):
                            for s in range(GATE_E):
                                step = gate_step(it, s)
                                if more or s < GATE_E - 1:
                                    next_transposes(step)
                                product(step, lambda q: gates(it, s, 2 * (s % 2) + q // 2, q % 2))

                        with pe.Fori(0, GATE_STEPS - 1) as it:
                            gate_body(it, True)
                        gate_body(GATE_STEPS - 1, False)

        def expert_out_stage(acc):
            GE = 4
            GROUPS = P // GE
            v_rows = expert_v.rearrange("(p e) d -> e p d", e=P)
            a_in = [sem(f"eo_a_in{i}") for i in range(2)]
            v_in = [sem(f"eo_v_in{i}") for i in range(2)]
            g_in = sem("eo_g_in")
            prod, a_hi_done, a_lo_done = sem("eo_prod"), sem("eo_a_hi"), sem("eo_a_lo")
            v_hi_done, v_lo_done = sem("eo_v_hi"), sem("eo_v_lo")
            cleared = sem("eo_cleared")
            mm_done = [sem(f"eo_mm{i}") for i in range(4)]
            added = [sem(f"eo_added{i}") for i in range(4)]
            with ExitStack() as stage:
                sb, pb = local(stage)
                a_raw, v_raw = sb("eo_a_raw", [P, 2, T]), sb("eo_v_raw", [P, 2, D])
                g_raw = sb("eo_g_raw", [P, T // GBLK, GE, GBLK])
                a_hi, a_lo = sb("eo_a_hi_sb", [P, 2, GE, T], F32R), sb("eo_a_lo_sb", [P, 2, GE, T], F32R)
                v_hi, v_lo = sb("eo_v_hi_sb", [P, 2, GE, D], F32R), sb("eo_v_lo_sb", [P, 2, GE, D], F32R)
                ps = [pb(f"eo_ps{i}", D) for i in range(4)]

                with nc.Block() as block:
                    @block.sync
                    def _(sp):
                        def load_gates(q):
                            sp.wait_ge(prod, q * GE)
                            sp.dma_start(g_raw[:], gate_d[:, :, bass.ds(q * GE, GE), :].rearrange("n p e t -> p n e t")).then_inc(g_in, 16)

                        def load_group(q, b):
                            for j in range(GE):
                                e, i = q * GE + j, j % 2
                                if j == 2:
                                    load_gates(q)
                                if j >= 2:
                                    sp.wait_ge(a_lo_done, e - 1)
                                    sp.wait_ge(v_lo_done, e - 1)
                                else:
                                    sp.wait_ge(a_lo_done, e - j)
                                    sp.wait_ge(v_lo_done, e - j)
                                sp.dma_start(a_raw[:, i, :], act_d[e, :, :]).then_inc(a_in[i], 16)
                                sp.dma_start(v_raw[:, i, :], v_rows[e, :, :]).then_inc(v_in[i], 16)

                        with sp.Fori(0, GROUPS // 2) as it:
                            for b in range(2):
                                load_group(it * 2 + b, b)

                    @block.gpsimd
                    def _(pool):
                        pool.memset(acc[:], 0.0).then_inc(cleared, 1)

                        with pool.Fori(0, GROUPS // 2) as it:
                            for b in range(2):
                                for j in range(GE):
                                    pool.wait_ge(v_hi_done, it * (2 * GE) + (b * GE + j + 1))
                                    pool.tensor_tensor(v_lo[:, b, j, :], v_raw[:, j % 2, :], v_hi[:, b, j, :], ALU.subtract).then_inc(v_lo_done, 1)

                    @block.scalar
                    def _(act):
                        def split_group(it, b):
                            for j in range(GE):
                                e = it * (2 * GE) + (b * GE + j)
                                act.wait_ge(v_in[j % 2], it * (GE * 16) + (b * (GE // 2) + j // 2 + 1) * 16)
                                act.activation(v_hi[:, b, j, :], v_raw[:, j % 2, :], ACT.Copy).then_inc(v_hi_done, 1)
                                act.wait_ge(prod, e + 1)
                                act.activation(a_hi[:, b, j, :], a_raw[:, j % 2, :], ACT.Copy).then_inc(a_hi_done, 1)

                        split_group(0, 0)
                        with act.Fori(0, GROUPS // 2 - 1) as it:
                            act.wait_ge(mm_done[3], it * 4)
                            split_group(it, 1)
                            act.wait_ge(mm_done[3], it * 4 + 2)
                            split_group(it + 1, 0)
                        act.wait_ge(mm_done[3], (GROUPS // 2 - 1) * 4)
                        split_group(GROUPS // 2 - 1, 1)

                    @block.vector
                    def _(dve):
                        def multiply(it, b, j):
                            dve.wait_ge(a_in[j % 2], it * (GE * 16) + (b * (GE // 2) + j // 2 + 1) * 16)
                            if j == 0:
                                dve.wait_ge(g_in, it * 32 + (b + 1) * 16)
                            a = a_raw[:, j % 2, :].rearrange("p (n t) -> p n t", t=GBLK)
                            dve.tensor_tensor(a, a, g_raw[:, :, j, :], ALU.mult).then_inc(prod, 1)

                        def product_lo(it, b, j):
                            dve.wait_ge(a_hi_done, it * (2 * GE) + (b * GE + j + 1))
                            dve.tensor_tensor(a_lo[:, b, j, :], a_raw[:, j % 2, :], a_hi[:, b, j, :], ALU.subtract).then_inc(a_lo_done, 1)

                        def add(it, b, t):
                            n = it * 4 + (b * 2 + t // 4)
                            dve.wait_ge(mm_done[t % 4], n + 1)
                            dve.tensor_tensor(acc[:, t, :], acc[:, t, :], ps[t % 4][:], ALU.add).then_inc(added[t % 4], 1)

                        dve.wait_ge(cleared, 1)
                        for j in range(GE):
                            multiply(0, 0, j)
                            product_lo(0, 0, j)

                        def group_step(it, b):
                            ni, nb = (it, 1) if b == 0 else (it + 1, 0)
                            for j in range(GE):
                                multiply(ni, nb, j)
                                add(it, b, 2 * j)
                                product_lo(ni, nb, j)
                                add(it, b, 2 * j + 1)

                        with dve.Fori(0, GROUPS // 2 - 1) as it:
                            group_step(it, 0)
                            group_step(it, 1)
                        group_step(GROUPS // 2 - 1, 0)
                        for t in range(TT):
                            add(GROUPS // 2 - 1, 1, t)

                    @block.tensor
                    def _(pe):
                        with pe.Fori(0, GROUPS // 2) as it:
                            for b in range(2):
                                for t in range(TT):
                                    if t == 0:
                                        pe.wait_ge(a_lo_done, it * (2 * GE) + (b + 1) * GE)
                                        pe.wait_ge(v_lo_done, it * (2 * GE) + (b + 1) * GE)
                                    pe.wait_ge(added[t % 4], it * 4 + (b * 2 + t // 4))
                                    tok = slice(t * P, (t + 1) * P)
                                    for c in range(2):
                                        colc = slice(c * HALF, (c + 1) * HALF)
                                        for j in range(GE):
                                            last = three(pe, ps[t % 4][:, colc], a_hi[:, b, j, tok], a_lo[:, b, j, tok],
                                                         v_hi[:, b, j, colc], v_lo[:, b, j, colc], j == 0, j == GE - 1)
                                    last.then_inc(mm_done[t % 4], 1)

        norm_stage("n0", ln_in_g, ln_in_b, x, h0_d)
        free_sems()
        project_stage("pin", w_in, [(u_d, "gelu", 1.0), (v_d, "gelu", 1.0), (qb_d, "feat", float(B_HD) ** -0.5),
                                    (kb_d, "feat", 1.0), (vb_d, "tok", 1.0)])
        gate_stage()
        free_sems()
        attention_stage()
        free_sems()
        norm_stage("n1", ln1_g, ln1_b, h0_d, h1_d, weight=w_out)
        with ExitStack() as memory:
            msb, _ = local(memory)
            mk_hi, mk_lo = msb("mk_hi", [P, KT, MEM], F32R), msb("mk_lo", [P, KT, MEM], F32R)
            mv_hi, mv_lo = msb("mv_hi", [P, MT, D], F32R), msb("mv_lo", [P, MT, D], F32R)
            memory_stage(mk_hi, mk_lo, mv_hi, mv_lo)
            free_sems()
            project_stage("pxq", w_xq, [(xq_d[0:HALF, :], "feat", 1.0), (xq_d[HALF:D, :], "feat", 1.0)])
            cross_stage(mk_hi, mk_lo, mv_hi, mv_lo)
        free_sems()
        norm_stage("n2", ln2_g, ln2_b, h1_d, h2_d, weight=w_xo)
        free_sems()
        key_score_stage()
        free_sems()
        expert_in_stage()
        act_stack.close()
        with ExitStack() as result:
            rsb, _ = local(result)
            acc = rsb("acc", [P, TT, D])
            free_sems()
            expert_out_stage(acc)
            norm_stage("n3", ln3_g, ln3_b, h2_d, out, acc=acc, transposed=False)


_INS = ["x", "mem", "ln_in_g", "ln_in_b", "w_in", "gate_ln_g", "gate_ln_b", "w_sp", "b_sp", "rel_bias", "w_out",
        "ln1_g", "ln1_b", "w_xq", "w_xk", "w_xv", "w_xo", "ln2_g", "ln2_b", "w_pq", "sub_keys", "expert_u",
        "expert_v", "ln3_g", "ln3_b"]


def kernel(**inputs):
    import numpy as _np
    import concourse.bacc as _bacc
    from concourse import mybir as _mybir
    from concourse.bass_utils import run_bass_kernel_spmd as _run

    nc = _bacc.Bacc("TRN2", target_bir_lowering=False, num_devices=1)
    arrays, args = {}, []
    for name in _INS:
        a = _np.asarray(inputs[name])
        if name != "ln_in_g" and name != "ln_in_b":
            a = a[0]
        a = _np.ascontiguousarray(a)
        arrays[f"in_{name}"] = a
        args.append(nc.dram_tensor(f"in_{name}", a.shape, _mybir.dt.from_np(a.dtype), kind="ExternalInput").ap())
    out = nc.dram_tensor("out_0", (T, D), F32, kind="ExternalOutput").ap()
    layer_program(nc, *args, out)
    r = _run(nc, [arrays], core_ids=[0])
    return r.results[0]["out_0"].reshape(1, T, D)
```

```python
from contextlib import ExitStack

import concourse.bass as bass
from concourse import mybir

F32 = mybir.dt.float32
F32R = mybir.dt.float32r
BF16 = mybir.dt.bfloat16
U32 = mybir.dt.uint32
ACT = mybir.ActivationFunctionType
ALU = mybir.AluOpType
AX = mybir.AxisListType

P = 128
D = 1024
T = 1024
KT = D // P
TT = T // P
HALF = 512
D_A = D // 2
D_B = D - D_A
A_GROUPS = 4
CHUNK = 64
B_HEADS = 8
B_HD = D_B // B_HEADS
BAND = 8 * CHUNK
SPAN = BAND + P
REL = 128
EXT = SPAN + P
MEM = 256
MT = MEM // P
X_HEADS = 4
X_HD = D // X_HEADS
PH = 8
KEYS = 128
TOPK = 16
UNITS = TT * PH
GBLK = 32
ALPHA = 2.0 ** 0.25
EPS = 1e-5
MASKED = -1e30
LOWEST = -3.4e38


def layer_program(nc, x, mem, ln_in_g, ln_in_b, w_in, gate_ln_g, gate_ln_b, w_sp, b_sp, rel_bias, w_out,
                  ln1_g, ln1_b, w_xq, w_xk, w_xv, w_xo, ln2_g, ln2_b, w_pq, sub_keys, expert_u,
                  expert_v, ln3_g, ln3_b, out):
    top = ExitStack()

    def dram(name, shape):
        return nc.dram_tensor(name, shape, F32, kind="Internal").ap()

    h0_d = dram("h0_d", [T, D])
    h1_d = dram("h1_d", [T, D])
    h2_d = dram("h2_d", [T, D])
    u_d = dram("u_d", [T, D_A])
    v_d = dram("v_d", [T, D_A])
    vb_d = dram("vb_d", [T, D_B])
    qb_d = dram("qb_d", [D_B, T])
    kb_d = dram("kb_d", [D_B, T])
    ext_d = dram("ext_d", [B_HEADS, EXT])
    xq_d = dram("xq_d", [D, T])
    s_d = dram("s_d", [UNITS, P, 2 * KEYS])
    route_d = dram("route_d", [UNITS, TOPK * 3, P])
    act_d = dram("act_d", [P, P, T])
    gate_d = dram("gate_d", [T // GBLK, P, P, GBLK])

    stage_sems = []

    def sem(name):
        stage_sems.append(nc.alloc_semaphore(name=name))
        return stage_sems[-1]

    def free_sems():
        nc.clear_and_free_semaphores(stage_sems)
        nc.all_engine_barrier()
        stage_sems.clear()

    def local(stage):
        def sb(name, shape, dt=F32):
            return stage.enter_context(nc.sbuf_tensor(name, shape, dt))

        def pb(name, cols):
            return stage.enter_context(nc.psum_tensor(name, [P, cols], F32))
        return sb, pb

    def spread(vec):
        return bass.AP(vec.tensor, vec.offset, [[0, P], [1, vec.shape[-1]]])

    def three(pe, ps, l_hi, l_lo, r_hi, r_lo, first, last):
        pe.matmul(ps, l_hi, r_hi, start=first, stop=False)
        pe.matmul(ps, l_hi, r_lo, start=False, stop=False)
        return pe.matmul(ps, l_lo, r_hi, start=False, stop=last)

    with top:
        act_stack = ExitStack()
        asb, _ = local(act_stack)
        ident = asb("ident", [P, P])
        aT_hi = asb("aT_hi", [P, KT, T], F32R)
        aT_lo = asb("aT_lo", [P, KT, T], F32R)

        ident_done, ext_in, ext_built, ext_out = sem("ident_done"), sem("ext_in"), sem("ext_built"), sem("ext_out")
        with ExitStack() as stage:
            sb, pb = local(stage)
            ext = sb("ext", [B_HEADS, EXT])
            rel = sb("rel", [B_HEADS, 2 * REL + 1])
            with nc.Block() as block:
                @block.gpsimd
                def _(pool):
                    pool.memset(ident[:], 0.0).then_inc(ident_done, 1)
                    pool.wait_ge(ident_done, 1)
                    pool.affine_select(out=ident[:], in_=ident[:], compare_op=ALU.not_equal, fill=1.0, base=0,
                                       pattern=[[-1, P]], channel_multiplier=1).then_inc(ident_done, 1)

                @block.sync
                def _(sp):
                    sp.dma_start(rel[:], rel_bias).then_inc(ext_in, 16)
                    sp.wait_ge(ext_built, 2)
                    sp.dma_start(ext_d, ext[:]).then_inc(ext_out, 16)
                    sp.wait_ge(ext_out, 16)

                @block.vector
                def _(dve):
                    near = EXT - BAND - 1
                    dve.wait_ge(ext_in, 16)
                    dve.tensor_copy(ext[:, 0:near], rel[:, 2 * REL - near:2 * REL]).then_inc(ext_built, 1)
                    dve.tensor_copy(ext[:, near:EXT], rel[:, 2 * REL:2 * REL + 1].broadcast_to([B_HEADS, EXT - near])).then_inc(ext_built, 1)

        class RowNorm:

            def __init__(self, tag, sb, gain, bias):
                self.gain, self.bias = gain, bias
                self.gb_in, self.chain, self.var_done = sem(f"{tag}_gb_in"), sem(f"{tag}_chain"), sem(f"{tag}_var")
                self.root_done, self.scale_done = sem(f"{tag}_root"), sem(f"{tag}_scale")
                self.unit_done, self.gain_done, self.ln_done = sem(f"{tag}_unit"), sem(f"{tag}_gain"), sem(f"{tag}_ln")
                self.g_sb, self.b_sb = sb(f"{tag}_g", [P, D]), sb(f"{tag}_b", [P, D])
                self.stats, self.mv = sb(f"{tag}_stats", [P, 2, 2, 6]), sb(f"{tag}_mv", [P, 2, 2])
                self.var, self.root = sb(f"{tag}_var_sb", [P, 2]), sb(f"{tag}_root_sb", [P, 2])
                self.rstd, self.shift = sb(f"{tag}_rstd", [P, 2]), sb(f"{tag}_shift", [P, 2])
                self.links = 0

            def load(self, sp):
                sp.dma_start(self.g_sb[:], spread(self.gain)).then_inc(self.gb_in, 16)
                sp.dma_start(self.b_sb[:], spread(self.bias)).then_inc(self.gb_in, 16)

            def link(self, dve, ins):
                self.links += 1
                ins.then_inc(self.chain, 1)
                dve.wait_ge(self.chain, self.links)

            def statistics(self, dve, j, x):
                i = j % 2
                for c in range(2):
                    self.link(dve, dve.bn_stats(self.stats[:, i, c, :], x[:, c * HALF:(c + 1) * HALF]))
                self.link(dve, dve.bn_aggr(self.mv[:, i, :], self.stats[:, i, :, :].rearrange("p a b -> p (a b)")))
                dve.tensor_scalar(self.var[:, i:i + 1], self.mv[:, i, 1:2], EPS, None, ALU.add).then_inc(self.var_done, 1)

            def square_root(self, act, j):
                i = j % 2
                act.wait_ge(self.var_done, j + 1)
                act.activation(self.root[:, i:i + 1], self.var[:, i:i + 1], ACT.Sqrt).then_inc(self.root_done, 1)

            def scale(self, dve, j):
                i = j % 2
                dve.wait_ge(self.root_done, j + 1)
                if j >= 2:
                    dve.wait_ge(self.unit_done, j - 1)
                self.link(dve, dve.reciprocal(self.rstd[:, i:i + 1], self.root[:, i:i + 1]))
                dve.tensor_scalar(self.shift[:, i:i + 1], self.mv[:, i, 0:1], self.rstd[:, i:i + 1], -1.0,
                                  ALU.mult, ALU.mult).then_inc(self.scale_done, 1)

            def normalise(self, act, j, x):
                i = j % 2
                act.wait_ge(self.scale_done, j + 1)
                act.activation(x, x, ACT.Identity, scale=self.rstd[:, i:i + 1], bias=self.shift[:, i:i + 1]).then_inc(self.unit_done, 1)

            def times_gain(self, dve, j, x):
                if j == 0:
                    dve.wait_ge(self.gb_in, 32)
                dve.wait_ge(self.unit_done, j + 1)
                dve.tensor_tensor(x, x, self.g_sb[:], ALU.mult).then_inc(self.gain_done, 1)

            def plus_bias(self, pool, j, x):
                if j == 0:
                    pool.wait_ge(self.gb_in, 32)
                pool.wait_ge(self.gain_done, j + 1)
                pool.tensor_tensor(x, x, self.b_sb[:], ALU.add).then_inc(self.ln_done, 1)

        def norm_stage(tag, gain, bias, resid, dest, weight=None):
            ROWS = 4
            w_raw_in = [sem(f"{tag}_w_raw_in{i}") for i in range(4)]
            w_hi_done = sem(f"{tag}_w_hi")
            w_lo_done = [sem(f"{tag}_w_lo{i}") for i in range(2)]
            row_in = [sem(f"{tag}_row_in{i}") for i in range(ROWS)]
            stored = [sem(f"{tag}_stored{i}") for i in range(ROWS)]
            mm_done, sum_done = sem(f"{tag}_mm"), sem(f"{tag}_sum")
            tr_done, hi_done, lo_done = sem(f"{tag}_tr"), sem(f"{tag}_hi"), sem(f"{tag}_lo")
            with ExitStack() as stage:
                sb, pb = local(stage)
                ln = RowNorm(tag, sb, gain, bias)
                row = sb(f"{tag}_row", [P, ROWS, D])
                if weight is not None:
                    w_raw = sb(f"{tag}_w_raw", [P, 4, D])
                    w_hi, w_lo = sb(f"{tag}_whi", [P, KT, D], F32R), sb(f"{tag}_wlo", [P, KT, D], F32R)
                    ps_mm = [pb(f"{tag}_ps_mm{i}", D) for i in range(2)]
                ps_tr = [pb(f"{tag}_ps_tr{i}", D) for i in range(2)]

                def x(j):
                    return row[:, j % ROWS, :]

                with nc.Block() as block:
                    @block.sync
                    def _(sp):
                        def load_row(j):
                            sp.dma_start(x(j), resid[j * P:(j + 1) * P, :]).then_inc(row_in[j % ROWS], 16)

                        if weight is not None:
                            for k in range(KT):
                                if k >= 4:
                                    sp.wait_ge(w_lo_done[k % 2], k // 2 - 1)
                                sp.dma_start(w_raw[:, k % 4, :], weight[k * P:(k + 1) * P, :]).then_inc(w_raw_in[k % 4], 16)
                        for j in range(ROWS):
                            load_row(j)
                            if j == 1:
                                ln.load(sp)
                        for j in range(TT):
                            sp.wait_ge(ln.ln_done, j + 1)
                            sp.dma_start(dest[j * P:(j + 1) * P, :], x(j)).then_inc(stored[j % ROWS], 16)
                            if 1 <= j and j - 1 + ROWS < TT:
                                sp.wait_ge(stored[(j - 1) % ROWS], 16 * ((j - 1) // ROWS + 1))
                                sp.wait_ge(tr_done, j)
                                load_row(j - 1 + ROWS)
                        for i in range(ROWS):
                            sp.wait_ge(stored[i], 16 * (TT // ROWS))

                    @block.gpsimd
                    def _(pool):
                        if weight is not None:
                            for k in range(1, KT, 2):
                                pool.wait_ge(w_hi_done, k + 1)
                                pool.tensor_tensor(w_lo[:, k, :], w_raw[:, k % 4, :], w_hi[:, k, :], ALU.subtract).then_inc(w_lo_done[1], 1)
                        for j in range(TT):
                            ln.plus_bias(pool, j, x(j))

                    @block.scalar
                    def _(act):
                        if weight is not None:
                            for k in range(KT):
                                act.wait_ge(w_raw_in[k % 4], 16 * (k // 4 + 1))
                                act.activation(w_hi[:, k, :], w_raw[:, k % 4, :], ACT.Copy).then_inc(w_hi_done, 1)

                        def transposed_hi(j):
                            act.wait_ge(tr_done, j + 1)
                            act.activation(aT_hi[:, :, j * P:(j + 1) * P], ps_tr[j % 2][:].rearrange("p (k t) -> p k t", k=KT),
                                           ACT.Copy).then_inc(hi_done, 1)

                        for j in range(TT):
                            ln.square_root(act, j)
                            ln.normalise(act, j, x(j))
                            if j >= 2:
                                transposed_hi(j - 2)
                        transposed_hi(TT - 2)
                        transposed_hi(TT - 1)

                    @block.vector
                    def _(dve):
                        def transposed_lo(j):
                            dve.wait_ge(hi_done, j + 1)
                            dve.tensor_tensor(aT_lo[:, :, j * P:(j + 1) * P], ps_tr[j % 2][:].rearrange("p (k t) -> p k t", k=KT),
                                              aT_hi[:, :, j * P:(j + 1) * P], ALU.subtract).then_inc(lo_done, 1)

                        if weight is not None:
                            for k in range(0, KT, 2):
                                dve.wait_ge(w_hi_done, k + 1)
                                dve.tensor_tensor(w_lo[:, k, :], w_raw[:, k % 4, :], w_hi[:, k, :], ALU.subtract).then_inc(w_lo_done[0], 1)
                        for j in range(TT):
                            dve.wait_ge(row_in[j % ROWS], 16 * (j // ROWS + 1))
                            if weight is not None:
                                dve.wait_ge(mm_done, j + 1)
                                dve.scalar_tensor_tensor(x(j), x(j), ALPHA, ps_mm[j % 2][:], ALU.mult, ALU.add).then_inc(sum_done, 1)
                                dve.wait_ge(sum_done, j + 1)
                            ln.statistics(dve, j, x(j))
                            if j >= 1 and weight is None:
                                ln.times_gain(dve, j - 1, x(j - 1))
                            ln.scale(dve, j)
                            if weight is not None:
                                ln.times_gain(dve, j, x(j))
                            if j >= 2:
                                transposed_lo(j - 2)
                        if weight is None:
                            ln.times_gain(dve, TT - 1, x(TT - 1))
                        transposed_lo(TT - 2)
                        transposed_lo(TT - 1)

                    @block.tensor
                    def _(pe):
                        def transposes(j):
                            pe.wait_ge(ln.ln_done, j + 1)
                            if j >= 2:
                                pe.wait_ge(lo_done, j - 1)
                            for k in range(KT):
                                last = pe.transpose(ps_tr[j % 2][:, k * P:(k + 1) * P], x(j)[:, k * P:(k + 1) * P], ident[:])
                            last.then_inc(tr_done, 1)

                        for j in range(TT):
                            if weight is not None:
                                if j >= 2:
                                    pe.wait_ge(sum_done, j - 1)
                                tok = slice(j * P, (j + 1) * P)
                                for k in range(KT):
                                    if j == 0:
                                        pe.wait_ge(w_lo_done[k % 2], k // 2 + 1)
                                    for c in range(2):
                                        col = slice(c * HALF, (c + 1) * HALF)
                                        last = three(pe, ps_mm[j % 2][:, col], aT_hi[:, k, tok], aT_lo[:, k, tok],
                                                     w_hi[:, k, col], w_lo[:, k, col], k == 0, k == KT - 1)
                                last.then_inc(mm_done, 1)
                            if j >= 1:
                                transposes(j - 1)
                        transposes(TT - 1)

        def project_stage(tag, weight, blocks):
            raw_in = [sem(f"{tag}_raw_in{i}") for i in range(4)]
            hi_done, lo_done, mm_done = sem(f"{tag}_hi"), sem(f"{tag}_lo"), sem(f"{tag}_mm")
            act_out, dve_out = sem(f"{tag}_act_out"), sem(f"{tag}_dve_out")
            stored = [sem(f"{tag}_stored{i}") for i in range(4)]
            NB, PIECES, PER = len(blocks), 4, 8
            units = [(b, i) for b in range(NB) for i in range(PER)]

            def by_act(u):
                return blocks[units[u][0]][1] == "gelu"

            def count(u):
                return sum(by_act(n) == by_act(u) for n in range(u + 1))

            def out_of_psum(eng, u):
                eng.wait_ge(act_out if by_act(u) else dve_out, count(u))

            with ExitStack() as stage:
                sb, pb = local(stage)
                raw = sb(f"{tag}_raw", [P, 4, 2, HALF])
                w_hi, w_lo = sb(f"{tag}_whi", [P, 2, KT, HALF], F32R), sb(f"{tag}_wlo", [P, 2, KT, HALF], F32R)
                res = sb(f"{tag}_res", [P, 4, HALF])
                ps = [pb(f"{tag}_ps{i}", HALF) for i in range(8)]
                with nc.Block() as block:
                    @block.sync
                    def _(sp):
                        def load(n):
                            b, q = divmod(n, PIECES)
                            if n >= 4:
                                sp.wait_ge(lo_done, n - 3)
                            src = weight[2 * q * P:2 * (q + 1) * P, b * HALF:(b + 1) * HALF].rearrange("(a p) n -> p a n", p=P)
                            sp.dma_start(raw[:, n % 4, :, :], src).then_inc(raw_in[n % 4], 16)

                        for n in range(PIECES):
                            load(n)
                        for u, (b, i) in enumerate(units):
                            if b + 1 < NB and i % 2 == 0:
                                load((b + 1) * PIECES + i // 2)
                            dest, kind, _ = blocks[b]
                            if kind == "feat":
                                f, th = divmod(i, 2)
                                to = dest[f * P:(f + 1) * P, th * HALF:(th + 1) * HALF]
                            else:
                                to = dest[i * P:(i + 1) * P, :]
                            out_of_psum(sp, u)
                            sp.dma_start(to, res[:, u % 4, :]).then_inc(stored[u % 4], 16)
                        for i in range(4):
                            sp.wait_ge(stored[i], 16 * (len(units) // 4))

                    @block.gpsimd
                    def _(pool):
                        for n in range(NB * PIECES):
                            b, q = divmod(n, PIECES)
                            pool.wait_ge(hi_done, n + 1)
                            pool.tensor_tensor(w_lo[:, b % 2, 2 * q:2 * q + 2, :], raw[:, n % 4, :, :],
                                               w_hi[:, b % 2, 2 * q:2 * q + 2, :], ALU.subtract).then_inc(lo_done, 1)

                    @block.scalar
                    def _(act):
                        def split(n):
                            b, q = divmod(n, PIECES)
                            act.wait_ge(raw_in[n % 4], 16 * (n // 4 + 1))
                            if b >= 2:
                                act.wait_ge(mm_done, (b - 1) * PER)
                            act.activation(w_hi[:, b % 2, 2 * q:2 * q + 2, :], raw[:, n % 4, :, :], ACT.Copy).then_inc(hi_done, 1)

                        for n in range(PIECES):
                            split(n)
                        for u, (b, i) in enumerate(units):
                            if b + 1 < NB and i % 2 == 0:
                                split((b + 1) * PIECES + i // 2)
                            if by_act(u):
                                act.wait_ge(mm_done, u + 1)
                                if u >= 4:
                                    act.wait_ge(stored[u % 4], 16 * (u // 4))
                                act.activation(res[:, u % 4, :], ps[u % 8][:], ACT.Gelu).then_inc(act_out, 1)

                    @block.vector
                    def _(dve):
                        for u, (b, i) in enumerate(units):
                            if not by_act(u):
                                dve.wait_ge(mm_done, u + 1)
                                if u >= 4:
                                    dve.wait_ge(stored[u % 4], 16 * (u // 4))
                                dve.tensor_scalar(res[:, u % 4, :], ps[u % 8][:], blocks[b][2], None, ALU.mult).then_inc(dve_out, 1)

                    @block.tensor
                    def _(pe):
                        for u, (b, i) in enumerate(units):
                            if u >= 8:
                                out_of_psum(pe, u - 8)
                            for k in range(KT):
                                if i == 0 and k % 2 == 0:
                                    pe.wait_ge(lo_done, b * PIECES + k // 2 + 1)
                                if blocks[b][1] == "feat":
                                    f, th = divmod(i, 2)
                                    col, tok = slice(f * P, (f + 1) * P), slice(th * HALF, (th + 1) * HALF)
                                    last = three(pe, ps[u % 8][:], w_hi[:, b % 2, k, col], w_lo[:, b % 2, k, col],
                                                 aT_hi[:, k, tok], aT_lo[:, k, tok], k == 0, k == KT - 1)
                                else:
                                    tok = slice(i * P, (i + 1) * P)
                                    last = three(pe, ps[u % 8][:], aT_hi[:, k, tok], aT_lo[:, k, tok],
                                                 w_hi[:, b % 2, k, :], w_lo[:, b % 2, k, :], k == 0, k == KT - 1)
                            last.then_inc(mm_done, 1)

        def gate_stage():
            consts_in, wt_tr, wt_hi, wt_lo = sem("ga_consts"), sem("ga_wt_tr"), sem("ga_wt_hi"), sem("ga_wt_lo")
            masked = sem("ga_masked")
            v_in = [sem(f"ga_v_in{i}") for i in range(2)]
            u_in = [sem(f"ga_u_in{i}") for i in range(2)]
            chain, var_done, root_done, vn_done = sem("ga_chain"), sem("ga_var"), sem("ga_root"), sem("ga_vn")
            vhi_done, vlo_done, mix_done, y_done = sem("ga_vhi"), sem("ga_vlo"), sem("ga_mix"), sem("ga_y")
            tr_done, hi_done, lo_done = sem("ga_tr"), sem("ga_hi"), sem("ga_lo")
            with ExitStack() as stage:
                sb, pb = local(stage)
                wraw = sb("ga_wraw", [P, A_GROUPS, P])
                wT_hi, wT_lo = sb("ga_wT_hi", [P, A_GROUPS, P], F32R), sb("ga_wT_lo", [P, A_GROUPS, P], F32R)
                bsp = sb("ga_bsp", [P, A_GROUPS])
                g_sb, b_sb = sb("ga_g", [P, D_A]), sb("ga_b", [P, D_A])
                v_sb, u_sb = sb("ga_v", [P, 2, D_A]), sb("ga_u", [P, 2, D_A])
                v_hi, v_lo = sb("ga_v_hi", [P, 2, D_A], F32R), sb("ga_v_lo", [P, 2, D_A], F32R)
                y_sb = sb("ga_y_sb", [P, 2, D_A])
                stats, mv = sb("ga_stats", [P, 2, 6]), sb("ga_mv", [P, 2, 2])
                var, root, rstd = sb("ga_var_sb", [P, 2]), sb("ga_root_sb", [P, 2]), sb("ga_rstd", [P, 2])
                ps_w = pb("ga_ps_w", HALF)
                ps_s = [pb(f"ga_ps_s{i}", HALF) for i in range(2)]
                ps_y = [pb(f"ga_ps_y{i}", HALF) for i in range(2)]
                GA = D_A // P

                with nc.Block() as block:
                    @block.sync
                    def _(sp):
                        sp.dma_start(wraw[:], w_sp.rearrange("g i j -> i g j")).then_inc(consts_in, 16)
                        sp.dma_start(bsp[:], b_sp.rearrange("g i -> i g"), allow_slow_non_contiguous=True).then_inc(consts_in, 16)
                        sp.dma_start(g_sb[:], spread(gate_ln_g)).then_inc(consts_in, 16)
                        sp.dma_start(b_sb[:], spread(gate_ln_b)).then_inc(consts_in, 16)
                        for j in range(TT):
                            if j >= 2:
                                sp.wait_ge(vlo_done, j - 1)
                            sp.dma_start(v_sb[:, j % 2, :], v_d[j * P:(j + 1) * P, :]).then_inc(v_in[j % 2], 16)
                            if j >= 2:
                                sp.wait_ge(y_done, A_GROUPS * (j - 1))
                            sp.dma_start(u_sb[:, j % 2, :], u_d[j * P:(j + 1) * P, :]).then_inc(u_in[j % 2], 16)

                    @block.scalar
                    def _(act):
                        act.wait_ge(wt_tr, 1)
                        act.activation(wT_hi[:], ps_w[:].rearrange("p (g i) -> p g i", g=A_GROUPS), ACT.Copy).then_inc(wt_hi, 1)

                        def y_hi(j):
                            act.wait_ge(tr_done, j + 1)
                            act.activation(aT_hi[:, 0:GA, j * P:(j + 1) * P], ps_y[j % 2][:].rearrange("p (k t) -> p k t", k=GA),
                                           ACT.Copy).then_inc(hi_done, 1)

                        for j in range(TT):
                            act.wait_ge(var_done, j + 1)
                            act.activation(root[:, j % 2:j % 2 + 1], var[:, j % 2:j % 2 + 1], ACT.Sqrt).then_inc(root_done, 1)
                            act.wait_ge(vn_done, j + 1)
                            if j >= 2:
                                act.wait_ge(mix_done, j - 1)
                            act.activation(v_hi[:, j % 2, :], v_sb[:, j % 2, :], ACT.Copy).then_inc(vhi_done, 1)
                            if j >= 1:
                                y_hi(j - 1)
                        y_hi(TT - 1)

                    @block.vector
                    def _(dve):
                        links = [0]

                        def link(ins):
                            links[0] += 1
                            ins.then_inc(chain, 1)
                            dve.wait_ge(chain, links[0])

                        dve.wait_ge(wt_hi, 1)
                        dve.tensor_tensor(wT_lo[:], ps_w[:].rearrange("p (g i) -> p g i", g=A_GROUPS), wT_hi[:], ALU.subtract).then_inc(wt_lo, 1)
                        dve.wait_ge(wt_lo, 1)
                        dve.memset(wT_hi[CHUNK:P, :, 0:CHUNK].bitcast(F32), 0.0).then_inc(masked, 1)
                        dve.memset(wT_lo[CHUNK:P, :, 0:CHUNK].bitcast(F32), 0.0).then_inc(masked, 1)
                        dve.wait_ge(consts_in, 64)

                        def gate(j):
                            dve.wait_ge(mix_done, j + 1)
                            dve.wait_ge(u_in[j % 2], 16 * (j // 2 + 1))
                            if j >= 2:
                                dve.wait_ge(tr_done, j - 1)
                            for g in range(A_GROUPS):
                                col = slice(g * P, (g + 1) * P)
                                dve.scalar_tensor_tensor(y_sb[:, j % 2, col], ps_s[j % 2][:, col], bsp[:, g:g + 1],
                                                         u_sb[:, j % 2, col], ALU.add, ALU.mult).then_inc(y_done, 1)

                        def y_lo(j):
                            dve.wait_ge(hi_done, j + 1)
                            dve.tensor_tensor(aT_lo[:, 0:GA, j * P:(j + 1) * P], ps_y[j % 2][:].rearrange("p (k t) -> p k t", k=GA),
                                              aT_hi[:, 0:GA, j * P:(j + 1) * P], ALU.subtract).then_inc(lo_done, 1)

                        for j in range(TT):
                            i = j % 2
                            dve.wait_ge(v_in[i], 16 * (j // 2 + 1))
                            link(dve.bn_stats(stats[:, i, :], v_sb[:, i, :]))
                            link(dve.bn_aggr(mv[:, i, :], stats[:, i, :]))
                            dve.tensor_scalar(var[:, i:i + 1], mv[:, i, 1:2], EPS, None, ALU.add).then_inc(var_done, 1)
                            dve.wait_ge(root_done, j + 1)
                            link(dve.reciprocal(rstd[:, i:i + 1], root[:, i:i + 1]))
                            link(dve.tensor_scalar(v_sb[:, i, :], v_sb[:, i, :], mv[:, i, 0:1], rstd[:, i:i + 1], ALU.subtract, ALU.mult))
                            link(dve.tensor_tensor(v_sb[:, i, :], v_sb[:, i, :], g_sb[:], ALU.mult))
                            dve.tensor_tensor(v_sb[:, i, :], v_sb[:, i, :], b_sb[:], ALU.add).then_inc(vn_done, 1)
                            if j >= 1:
                                gate(j - 1)
                            dve.wait_ge(vhi_done, j + 1)
                            dve.tensor_tensor(v_lo[:, i, :], v_sb[:, i, :], v_hi[:, i, :], ALU.subtract).then_inc(vlo_done, 1)
                            if j >= 2:
                                y_lo(j - 2)
                        gate(TT - 1)
                        y_lo(TT - 2)
                        y_lo(TT - 1)

                    @block.tensor
                    def _(pe):
                        pe.wait_ge(consts_in, 64)
                        for g in range(A_GROUPS):
                            last = pe.transpose(ps_w[:, g * P:(g + 1) * P], wraw[:, g, :], ident[:])
                        last.then_inc(wt_tr, 1)
                        pe.wait_ge(masked, 2)

                        def y_transposes(j):
                            pe.wait_ge(y_done, A_GROUPS * (j + 1))
                            if j >= 2:
                                pe.wait_ge(lo_done, j - 1)
                            for k in range(GA):
                                last = pe.transpose(ps_y[j % 2][:, k * P:(k + 1) * P], y_sb[:, j % 2, k * P:(k + 1) * P], ident[:])
                            last.then_inc(tr_done, 1)

                        for j in range(TT):
                            if j >= 1:
                                y_transposes(j - 1)
                            pe.wait_ge(vlo_done, j + 1)
                            if j >= 2:
                                pe.wait_ge(y_done, A_GROUPS * (j - 1))
                            for g in range(A_GROUPS):
                                col = slice(g * P, (g + 1) * P)
                                last = three(pe, ps_s[j % 2][:, col], wT_hi[:, g, :], wT_lo[:, g, :],
                                             v_hi[:, j % 2, col], v_lo[:, j % 2, col], True, True)
                            last.then_inc(mix_done, 1)
                        y_transposes(TT - 1)

        def attention_stage():
            bias_in, masked = sem("at_bias_in"), sem("at_masked")
            raw_in = [sem(f"at_raw_in{i}") for i in range(2)]
            sp_hi, sp_lo, sp_lo_v = sem("at_split_hi"), sem("at_split_lo"), sem("at_split_lo_v")
            s_done, max_done, neg_done, exp_done = sem("at_s"), sem("at_max"), sem("at_neg"), sem("at_exp")
            rec_done, norm_done = sem("at_rec"), sem("at_norm")
            tr_done, p_hi_done, p_lo_done, pv_done = sem("at_tr"), sem("at_p_hi"), sem("at_p_lo"), sem("at_pv")
            y_hi_done, y_lo_done = sem("at_y_hi"), sem("at_y_lo")
            QF = D_B // P
            NU = TT * B_HEADS
            units = [divmod(u, B_HEADS) for u in range(NU)]
            G0 = D_A // P

            def keys(n):
                nk = min(SPAN, (n + 1) * P)
                return (n + 1) * P - nk, nk, 1 if nk <= HALF else 2

            def backwards(row, parts):
                (step, count), (one, n) = row.ap
                w = n // parts
                return bass.AP(row.tensor, row.offset + (n - 1) * one, [[step, count], [-one * w, parts], [-one, w]])

            with ExitStack() as stage:
                sb, pb = local(stage)
                bias = sb("at_bias", [P, B_HEADS, SPAN])
                raw = sb("at_raw", [P, 2, D])
                q_hi, q_lo = sb("at_q_hi", [P, QF, T], F32R), sb("at_q_lo", [P, QF, T], F32R)
                k_hi, k_lo = sb("at_k_hi", [P, QF, T], F32R), sb("at_k_lo", [P, QF, T], F32R)
                v_hi, v_lo = sb("at_v_hi", [P, TT, D_B], F32R), sb("at_v_lo", [P, TT, D_B], F32R)
                prob = sb("at_prob", [P, 3, SPAN])
                pT_hi, pT_lo = sb("at_pT_hi", [P, 2, SPAN], F32R), sb("at_pT_lo", [P, 2, SPAN], F32R)
                top_s, neg, rsum, rinv = sb("at_top", [P, 2]), sb("at_neg_sb", [P, 2]), sb("at_rsum", [P, 4]), sb("at_rinv", [P, 2])
                ps_s = [pb(f"at_ps_s{i}", D) for i in range(2)]
                ps_t = pb("at_ps_t", D)
                ps_o = [pb(f"at_ps_o{i}", HALF) for i in range(2)]
                pieces = []
                for f in range(QF):
                    pieces.append((qb_d[f * P:(f + 1) * P, :], q_hi[:, f, :], q_lo[:, f, :]))
                    pieces.append((kb_d[f * P:(f + 1) * P, :], k_hi[:, f, :], k_lo[:, f, :]))
                for f in range(TT // 2):
                    pieces.append((vb_d[2 * f * P:2 * (f + 1) * P, :].rearrange("(a p) n -> p a n", p=P),
                                   v_hi[:, 2 * f:2 * f + 2, :], v_lo[:, 2 * f:2 * f + 2, :]))
                QK = 2 * QF

                def raw_of(n):
                    r = raw[:, n % 2, :]
                    return r if n < QK else r.rearrange("p (a n) -> p a n", a=2)

                def aT_cols(t, pair, half):
                    n, f = divmod(pair, QF)
                    return t[half * B_HD:(half + 1) * B_HD, G0 + f, n * P:(n + 1) * P]

                def out_cols(pair, half):
                    return ps_o[pair % 2][0:B_HD, half * P:(half + 1) * P]

                with nc.Block() as block:
                    @block.sync
                    def _(sp):
                        for n, (src, _, _) in enumerate(pieces):
                            if n >= QK + 2:
                                sp.wait_ge(sp_lo_v, n - QK - 1)
                            elif n >= 2:
                                sp.wait_ge(sp_lo, n - 1)
                            sp.dma_start(raw_of(n), src).then_inc(raw_in[n % 2], 16)
                            if n == 1:
                                sp.dma_start(bias[:], bass.AP(ext_d.tensor, ext_d.offset,
                                                              [[1, P], [EXT, B_HEADS], [1, SPAN]])).then_inc(bias_in, 16)

                    @block.gpsimd
                    def _(pool):
                        pool.wait_ge(bias_in, 16)
                        pool.memset(bias[0:CHUNK, :, 0:CHUNK], MASKED).then_inc(masked, 1)
                        pool.memset(bias[CHUNK:P, :, SPAN - CHUNK:SPAN], MASKED).then_inc(masked, 1)
                        pool.wait_ge(masked, 2)
                        for n in range(QK, len(pieces)):
                            pool.wait_ge(sp_hi, n + 1)
                            pool.tensor_tensor(pieces[n][2], raw_of(n), pieces[n][1], ALU.subtract).then_inc(sp_lo_v, 1)

                    @block.scalar
                    def _(act):
                        def split(n):
                            act.wait_ge(raw_in[n % 2], 16 * (n // 2 + 1))
                            act.activation(pieces[n][1], raw_of(n), ACT.Copy).then_inc(sp_hi, 1)

                        for n in range(QK + 1):
                            split(n)
                        for u in range(NU + 3):
                            if QK + 1 + u < len(pieces):
                                split(QK + 1 + u)
                            if 2 <= u < NU + 2:
                                w = u - 2
                                nk = keys(units[w][0])[1]
                                act.wait_ge(tr_done, w + 1)
                                if w >= 2:
                                    act.wait_ge(pv_done, w - 1)
                                act.activation(pT_hi[:, w % 2, 0:nk], ps_t[:, 0:nk], ACT.Copy).then_inc(p_hi_done, 1)
                            if u < NU:
                                nk = keys(units[u][0])[1]
                                act.wait_ge(neg_done, u + 1)
                                if u >= 4:
                                    act.wait_ge(rec_done, u - 3)
                                act.activation(prob[:, u % 3, 0:nk], prob[:, u % 3, 0:nk], ACT.Exp, bias=neg[:, u % 2:u % 2 + 1],
                                               accum_out=rsum[:, u % 4:u % 4 + 1]).then_inc(exp_done, 1)
                            if u >= 4 and u % 2 == 0:
                                pair = (u - 4) // 2
                                act.wait_ge(pv_done, 2 * pair + 2)
                                for half in range(2):
                                    act.activation(aT_cols(aT_hi, pair, half), out_cols(pair, half), ACT.Copy).then_inc(y_hi_done, 1)

                    @block.vector
                    def _(dve):
                        for n in range(QK):
                            dve.wait_ge(sp_hi, n + 1)
                            dve.tensor_tensor(pieces[n][2], raw_of(n), pieces[n][1], ALU.subtract).then_inc(sp_lo, 1)
                        dve.wait_ge(masked, 2)
                        for u in range(NU + 3):
                            if u < NU:
                                n, hd = units[u]
                                _, nk, parts = keys(n)
                                dve.wait_ge(s_done, u + 1)
                                if u >= 3:
                                    dve.wait_ge(tr_done, u - 2)
                                src = ps_s[u % 2][:].rearrange("p (a n) -> p a n", a=2)[:, 0:parts, 0:nk // parts]
                                dst = prob[:, u % 3, 0:nk].rearrange("p (a n) -> p a n", a=parts)
                                dve.tensor_tensor_reduce(out=dst, in0=src, in1=backwards(bias[:, hd, 0:nk], parts),
                                                         scale=1.0, scalar=LOWEST, op0=ALU.add, op1=ALU.max,
                                                         accum_out=top_s[:, u % 2:u % 2 + 1]).then_inc(max_done, 1)
                                dve.wait_ge(max_done, u + 1)
                                dve.tensor_scalar(neg[:, u % 2:u % 2 + 1], top_s[:, u % 2:u % 2 + 1], -1.0, None, ALU.mult).then_inc(neg_done, 1)
                            if 1 <= u < NU + 1:
                                w = u - 1
                                nk = keys(units[w][0])[1]
                                dve.wait_ge(exp_done, w + 1)
                                dve.reciprocal(rinv[:, w % 2:w % 2 + 1], rsum[:, w % 4:w % 4 + 1]).then_inc(rec_done, 1)
                                dve.wait_ge(rec_done, w + 1)
                                dve.tensor_scalar(prob[:, w % 3, 0:nk], prob[:, w % 3, 0:nk], rinv[:, w % 2:w % 2 + 1], None,
                                                  ALU.mult).then_inc(norm_done, 1)
                            if 2 <= u < NU + 2:
                                w = u - 2
                                nk = keys(units[w][0])[1]
                                dve.wait_ge(p_hi_done, w + 1)
                                dve.tensor_tensor(pT_lo[:, w % 2, 0:nk], ps_t[:, 0:nk], pT_hi[:, w % 2, 0:nk], ALU.subtract).then_inc(p_lo_done, 1)
                            if u >= 4 and u % 2 == 0:
                                pair = (u - 4) // 2
                                dve.wait_ge(y_hi_done, 2 * pair + 2)
                                for half in range(2):
                                    dve.tensor_tensor(aT_cols(aT_lo, pair, half), out_cols(pair, half), aT_cols(aT_hi, pair, half),
                                                      ALU.subtract).then_inc(y_lo_done, 1)

                    @block.tensor
                    def _(pe):
                        def scores(u):
                            n, hd = units[u]
                            k0, nk, parts = keys(n)
                            if n == 0 and hd % 2 == 0:
                                pe.wait_ge(sp_lo, 2 * (hd // 2) + 2)
                            if u >= 2:
                                pe.wait_ge(max_done, u - 1)
                            rows, f, tok = slice((hd % 2) * B_HD, (hd % 2 + 1) * B_HD), hd // 2, slice(n * P, (n + 1) * P)
                            w = nk // parts
                            for c in range(parts):
                                last = three(pe, ps_s[u % 2][:, c * HALF:c * HALF + w], q_hi[rows, f, tok], q_lo[rows, f, tok],
                                             k_hi[rows, f, k0 + c * w:k0 + (c + 1) * w], k_lo[rows, f, k0 + c * w:k0 + (c + 1) * w],
                                             True, True)
                            last.then_inc(s_done, 1)

                        def transposes(u):
                            nk = keys(units[u][0])[1]
                            pe.wait_ge(norm_done, u + 1)
                            if u >= 1:
                                pe.wait_ge(p_lo_done, u)
                            for c in range(0, nk, P):
                                last = pe.transpose(ps_t[:, c:c + P], prob[:, u % 3, c:c + P], ident[:])
                            last.then_inc(tr_done, 1)

                        def values(u):
                            n, hd = units[u]
                            k0, nk, _ = keys(n)
                            pair = u // 2
                            pe.wait_ge(p_lo_done, u + 1)
                            if pair >= 2:
                                pe.wait_ge(y_lo_done, 2 * pair - 2)
                            if hd == 0:
                                pe.wait_ge(sp_lo_v, n // 2 + 1)
                            col = slice(hd * B_HD, (hd + 1) * B_HD)
                            for c in range(0, nk, P):
                                kt = (k0 + c) // P
                                last = three(pe, out_cols(pair, hd % 2), v_hi[:, kt, col], v_lo[:, kt, col],
                                             pT_hi[:, u % 2, c:c + P], pT_lo[:, u % 2, c:c + P], c == 0, c + P == nk)
                            last.then_inc(pv_done, 1)

                        for u in range(NU + 3):
                            if u < NU:
                                scores(u)
                            if 2 <= u < NU + 2:
                                transposes(u - 2)
                            if u >= 3:
                                values(u - 3)

        def memory_stage(mk_hi, mk_lo, mv_hi, mv_lo):
            mem_in, mt_tr, mt_hi, mt_lo = sem("me_in"), sem("me_tr"), sem("me_thi"), sem("me_tlo")
            raw_in = [sem(f"me_raw_in{i}") for i in range(4)]
            hi_done, lo_done, mm_done, out_hi, out_lo = sem("me_hi"), sem("me_lo"), sem("me_mm"), sem("me_out_hi"), sem("me_out_lo")
            PIECES = 4
            weights = [(w_xk, 0), (w_xk, 1), (w_xv, 0), (w_xv, 1)]
            units = [(b, i) for b in range(4) for i in range(4 if b < 2 else MT)]
            ends = [4, 8, 8 + MT, 8 + 2 * MT]
            with ExitStack() as stage:
                sb, pb = local(stage)
                mraw = sb("me_mraw", [P, MT, D])
                mT_hi, mT_lo = sb("me_mT_hi", [P, KT, MEM], F32R), sb("me_mT_lo", [P, KT, MEM], F32R)
                raw = sb("me_raw", [P, 4, 2, HALF])
                w_hi, w_lo = sb("me_whi", [P, 2, KT, HALF], F32R), sb("me_wlo", [P, 2, KT, HALF], F32R)
                ps_t = pb("me_ps_t", MT * D)
                ps = [pb(f"me_ps{i}", HALF) for i in range(4)]

                def target(u, mk, mv):
                    b, i = units[u]
                    if b < 2:
                        return mk[:, b * 4 + i, :], ps[u % 4][:, 0:MEM]
                    return mv[:, i, (b - 2) * HALF:(b - 1) * HALF], ps[u % 4][:]

                with nc.Block() as block:
                    @block.sync
                    def _(sp):
                        sp.dma_start(mraw[:], mem.rearrange("(a p) d -> p a d", p=P)).then_inc(mem_in, 16)
                        for n in range(4 * PIECES):
                            b, q = divmod(n, PIECES)
                            w, c = weights[b]
                            if n >= 4:
                                sp.wait_ge(lo_done, n - 3)
                            src = w[2 * q * P:2 * (q + 1) * P, c * HALF:(c + 1) * HALF].rearrange("(a p) n -> p a n", p=P)
                            sp.dma_start(raw[:, n % 4, :, :], src).then_inc(raw_in[n % 4], 16)

                    @block.gpsimd
                    def _(pool):
                        for n in range(4 * PIECES):
                            b, q = divmod(n, PIECES)
                            pool.wait_ge(hi_done, n + 1)
                            pool.tensor_tensor(w_lo[:, b % 2, 2 * q:2 * q + 2, :], raw[:, n % 4, :, :],
                                               w_hi[:, b % 2, 2 * q:2 * q + 2, :], ALU.subtract).then_inc(lo_done, 1)

                    @block.scalar
                    def _(act):
                        act.wait_ge(mt_tr, 1)
                        for a in range(MT):
                            act.activation(mT_hi[:, :, a * P:(a + 1) * P], ps_t[:, a * D:(a + 1) * D].rearrange("p (k m) -> p k m", k=KT),
                                           ACT.Copy).then_inc(mt_hi, 1)
                        n = 0
                        for u, (b, i) in enumerate(units):
                            while n < min(4 * PIECES, (b + 2) * PIECES):
                                nb, q = divmod(n, PIECES)
                                act.wait_ge(raw_in[n % 4], 16 * (n // 4 + 1))
                                if nb >= 2:
                                    act.wait_ge(mm_done, ends[nb - 2])
                                act.activation(w_hi[:, nb % 2, 2 * q:2 * q + 2, :], raw[:, n % 4, :, :], ACT.Copy).then_inc(hi_done, 1)
                                n += 1
                            act.wait_ge(mm_done, u + 1)
                            to, src = target(u, mk_hi, mv_hi)
                            act.activation(to, src, ACT.Copy).then_inc(out_hi, 1)

                    @block.vector
                    def _(dve):
                        for a in range(MT):
                            dve.wait_ge(mt_hi, a + 1)
                            dve.tensor_tensor(mT_lo[:, :, a * P:(a + 1) * P], ps_t[:, a * D:(a + 1) * D].rearrange("p (k m) -> p k m", k=KT),
                                              mT_hi[:, :, a * P:(a + 1) * P], ALU.subtract).then_inc(mt_lo, 1)
                        for u in range(len(units)):
                            dve.wait_ge(out_hi, u + 1)
                            hi, src = target(u, mk_hi, mv_hi)
                            lo, _ = target(u, mk_lo, mv_lo)
                            dve.tensor_tensor(lo, src, hi, ALU.subtract).then_inc(out_lo, 1)

                    @block.tensor
                    def _(pe):
                        pe.wait_ge(mem_in, 16)
                        for a in range(MT):
                            for k in range(KT):
                                last = pe.transpose(ps_t[:, a * D + k * P:a * D + (k + 1) * P], mraw[:, a, k * P:(k + 1) * P], ident[:])
                        last.then_inc(mt_tr, 1)
                        pe.wait_ge(mt_lo, MT)
                        for u, (b, i) in enumerate(units):
                            if u >= 4:
                                pe.wait_ge(out_lo, u - 3)
                            for k in range(KT):
                                if i == 0 and k % 2 == 0:
                                    pe.wait_ge(lo_done, b * PIECES + k // 2 + 1)
                                at = slice(i * P, (i + 1) * P)
                                if b < 2:
                                    last = three(pe, ps[u % 4][:, 0:MEM], w_hi[:, b % 2, k, at], w_lo[:, b % 2, k, at],
                                                 mT_hi[:, k, :], mT_lo[:, k, :], k == 0, k == KT - 1)
                                else:
                                    last = three(pe, ps[u % 4][:], mT_hi[:, k, at], mT_lo[:, k, at],
                                                 w_hi[:, b % 2, k, :], w_lo[:, b % 2, k, :], k == 0, k == KT - 1)
                            last.then_inc(mm_done, 1)

        def cross_stage(mk_hi, mk_lo, mv_hi, mv_lo):
            q_in = [sem(f"xa_q_in{i}") for i in range(2)]
            q_hi_done, q_lo_done, s_done = sem("xa_q_hi"), sem("xa_q_lo"), sem("xa_s")
            max_done, neg_done, exp_done = sem("xa_max"), sem("xa_neg"), sem("xa_exp")
            tr_done, p_hi_done, p_lo_done, pv_done = sem("xa_tr"), sem("xa_p_hi"), sem("xa_p_lo"), sem("xa_pv")
            rec_done, o_done, ot_done, o_hi_done, o_lo_done = sem("xa_rec"), sem("xa_o"), sem("xa_ot"), sem("xa_o_hi"), sem("xa_o_lo")
            SCALE = float(X_HD) ** -0.5
            HC = X_HD // P
            with ExitStack() as stage:
                sb, pb = local(stage)
                q_raw = sb("xa_q_raw", [P, 2, KT, P])
                q_hi, q_lo = sb("xa_q_hi_sb", [P, 2, KT, P], F32R), sb("xa_q_lo_sb", [P, 2, KT, P], F32R)
                prob = sb("xa_prob", [P, 2, X_HEADS, MEM])
                pT_hi, pT_lo = sb("xa_pT_hi", [P, 2, X_HEADS * MT, P], F32R), sb("xa_pT_lo", [P, 2, X_HEADS * MT, P], F32R)
                topm, neg = sb("xa_top", [P, 2, X_HEADS]), sb("xa_neg_sb", [P, 2, X_HEADS])
                rsum, rinv = sb("xa_rsum", [P, 2, X_HEADS]), sb("xa_rinv", [P, 2, X_HEADS])
                o_sb = sb("xa_o_sb", [P, 2, X_HEADS, X_HD])
                ps_s, ps_t, ps_o, ps_ot = pb("xa_ps_s", D), pb("xa_ps_t", D), pb("xa_ps_o", D), pb("xa_ps_ot", D)

                with nc.Block() as block:
                    @block.sync
                    def _(sp):
                        for j in range(TT):
                            if j >= 2:
                                sp.wait_ge(q_lo_done, j - 1)
                            sp.dma_start(q_raw[:, j % 2, :, :], xq_d[:, j * P:(j + 1) * P].rearrange("(k p) t -> p k t", p=P)).then_inc(q_in[j % 2], 16)

                    @block.scalar
                    def _(act):
                        def query_hi(j):
                            act.wait_ge(q_in[j % 2], 16 * (j // 2 + 1))
                            if j >= 2:
                                act.wait_ge(s_done, j - 1)
                            act.activation(q_hi[:, j % 2, :, :], q_raw[:, j % 2, :, :], ACT.Copy).then_inc(q_hi_done, 1)

                        def prob_hi(j):
                            act.wait_ge(tr_done, j + 1)
                            if j >= 2:
                                act.wait_ge(pv_done, j - 1)
                            act.activation(pT_hi[:, j % 2, :, :], ps_t[:].rearrange("p (k t) -> p k t", t=P), ACT.Copy).then_inc(p_hi_done, 1)

                        def out_hi(j):
                            act.wait_ge(ot_done, j + 1)
                            act.activation(aT_hi[:, :, j * P:(j + 1) * P], ps_ot[:].rearrange("p (k t) -> p k t", t=P), ACT.Copy).then_inc(o_hi_done, 1)

                        query_hi(0)
                        query_hi(1)
                        for j in range(TT):
                            act.wait_ge(neg_done, j + 1)
                            if j >= 2:
                                act.wait_ge(tr_done, j - 1)
                                act.wait_ge(rec_done, j - 1)
                            for hd in range(X_HEADS):
                                act.activation(prob[:, j % 2, hd, :], ps_s[:, hd * MEM:(hd + 1) * MEM], ACT.Exp, scale=SCALE,
                                               bias=neg[:, j % 2, hd:hd + 1], accum_out=rsum[:, j % 2, hd:hd + 1]).then_inc(exp_done, 1)
                            prob_hi(j)
                            if j + 2 < TT:
                                query_hi(j + 2)
                            if j >= 1:
                                out_hi(j - 1)
                        out_hi(TT - 1)

                    @block.vector
                    def _(dve):
                        def query_lo(j):
                            dve.wait_ge(q_hi_done, j + 1)
                            dve.tensor_tensor(q_lo[:, j % 2, :, :], q_raw[:, j % 2, :, :], q_hi[:, j % 2, :, :], ALU.subtract).then_inc(q_lo_done, 1)

                        def out_lo(j):
                            dve.wait_ge(o_hi_done, j + 1)
                            dve.tensor_tensor(aT_lo[:, :, j * P:(j + 1) * P], ps_ot[:].rearrange("p (k t) -> p k t", t=P),
                                              aT_hi[:, :, j * P:(j + 1) * P], ALU.subtract).then_inc(o_lo_done, 1)

                        def top(j):
                            dve.wait_ge(s_done, j + 1)
                            dve.tensor_reduce(topm[:, j % 2, :], ps_s[:].rearrange("p (h m) -> p h m", h=X_HEADS), AX.X, ALU.max).then_inc(max_done, 1)
                            dve.wait_ge(max_done, j + 1)
                            dve.tensor_scalar(neg[:, j % 2, :], topm[:, j % 2, :], -SCALE, None, ALU.mult).then_inc(neg_done, 1)

                        query_lo(0)
                        query_lo(1)
                        top(0)
                        for j in range(TT):
                            i = j % 2
                            dve.wait_ge(p_hi_done, j + 1)
                            dve.tensor_tensor(pT_lo[:, i, :, :], ps_t[:].rearrange("p (k t) -> p k t", t=P), pT_hi[:, i, :, :], ALU.subtract).then_inc(p_lo_done, 1)
                            if j + 1 < TT:
                                top(j + 1)
                            if j + 2 < TT:
                                query_lo(j + 2)
                            if j >= 1:
                                out_lo(j - 1)
                            dve.reciprocal(rinv[:, i, :], rsum[:, i, :]).then_inc(rec_done, 1)
                            dve.wait_ge(rec_done, j + 1)
                            dve.wait_ge(pv_done, j + 1)
                            dve.tensor_tensor(o_sb[:, i, :, :], ps_o[:].rearrange("p (h d) -> p h d", h=X_HEADS),
                                              rinv[:, i, :].unsqueeze(2).broadcast_to([P, X_HEADS, X_HD]), ALU.mult).then_inc(o_done, 1)
                        out_lo(TT - 1)

                    @block.tensor
                    def _(pe):
                        def scores(j):
                            pe.wait_ge(q_lo_done, j + 1)
                            if j >= 1:
                                pe.wait_ge(exp_done, X_HEADS * j)
                            for hd in range(X_HEADS):
                                for c in range(HC):
                                    f = hd * HC + c
                                    last = three(pe, ps_s[:, hd * MEM:(hd + 1) * MEM], q_hi[:, j % 2, f, :], q_lo[:, j % 2, f, :],
                                                 mk_hi[:, f, :], mk_lo[:, f, :], c == 0, c == HC - 1)
                            last.then_inc(s_done, 1)

                        def out_transposes(j):
                            pe.wait_ge(o_done, j + 1)
                            if j >= 1:
                                pe.wait_ge(o_lo_done, j)
                            o = o_sb[:, j % 2, :, :].rearrange("p h d -> p (h d)")
                            for k in range(KT):
                                last = pe.transpose(ps_ot[:, k * P:(k + 1) * P], o[:, k * P:(k + 1) * P], ident[:])
                            last.then_inc(ot_done, 1)

                        scores(0)
                        for j in range(TT):
                            pe.wait_ge(exp_done, X_HEADS * (j + 1))
                            if j >= 1:
                                pe.wait_ge(p_lo_done, j)
                            for hd in range(X_HEADS):
                                for c in range(MT):
                                    at = (hd * MT + c) * P
                                    last = pe.transpose(ps_t[:, at:at + P], prob[:, j % 2, hd, c * P:(c + 1) * P], ident[:])
                            last.then_inc(tr_done, 1)
                            if j + 1 < TT:
                                scores(j + 1)
                            if j >= 1:
                                out_transposes(j - 1)
                            pe.wait_ge(p_lo_done, j + 1)
                            if j >= 1:
                                pe.wait_ge(o_done, j)
                            for hd in range(X_HEADS):
                                for c in range(MT):
                                    last = three(pe, ps_o[:, hd * X_HD:(hd + 1) * X_HD], pT_hi[:, j % 2, hd * MT + c, :], pT_lo[:, j % 2, hd * MT + c, :],
                                                 mv_hi[:, c, hd * X_HD:(hd + 1) * X_HD], mv_lo[:, c, hd * X_HD:(hd + 1) * X_HD], c == 0, c == MT - 1)
                            last.then_inc(pv_done, 1)
                        out_transposes(TT - 1)

        def key_score_stage():
            sk_in, sk_tr, sk_hi, sk_lo = sem("ks_sk_in"), sem("ks_sk_tr"), sem("ks_sk_hi"), sem("ks_sk_lo")
            raw_in = [sem(f"ks_raw_in{i}") for i in range(4)]
            hi_done, lo_done = sem("ks_hi"), sem("ks_lo")
            q_done, q_hi_done, q_lo_done = sem("ks_q"), sem("ks_q_hi"), sem("ks_q_lo")
            s_done, s_out = sem("ks_s"), sem("ks_s_out")
            stored = [sem(f"ks_stored{i}") for i in range(2)]
            HP, PIECES, NB = 2 * PH, 4, 4
            s_view = s_d.rearrange("(j h) t (q k) -> h q t j k", h=PH, q=2)
            with ExitStack() as stage:
                sb, pb = local(stage)
                sraw = sb("ks_sraw", [P, HP, P])
                sk_hi_sb, sk_lo_sb = sb("ks_skT_hi", [P, HP, P], F32R), sb("ks_skT_lo", [P, HP, P], F32R)
                raw = sb("ks_raw", [P, 4, 2, HALF])
                w_hi, w_lo = sb("ks_whi", [P, 2, KT, HALF], F32R), sb("ks_wlo", [P, 2, KT, HALF], F32R)
                q_hi, q_lo = sb("ks_qhi", [P, 2, T], F32R), sb("ks_qlo", [P, 2, T], F32R)
                res = sb("ks_res", [P, 2, TT, KEYS])
                ps_q = [pb(f"ks_ps_q{i}", HALF) for i in range(4)]
                ps_s = [pb(f"ks_ps_s{i}", D) for i in range(2)]
                with nc.Block() as block:
                    @block.sync
                    def _(sp):
                        def load(n):
                            b, q = divmod(n, PIECES)
                            if n >= 4:
                                sp.wait_ge(lo_done, n - 3)
                            src = w_pq[2 * q * P:2 * (q + 1) * P, b * HALF:(b + 1) * HALF].rearrange("(a p) n -> p a n", p=P)
                            sp.dma_start(raw[:, n % 4, :, :], src).then_inc(raw_in[n % 4], 16)

                        for n in range(PIECES):
                            load(n)
                        sp.dma_start(sraw[:], sub_keys.rearrange("h q k d -> k (h q) d")).then_inc(sk_in, 16)
                        for hp in range(HP + 1):
                            if hp // 4 + 1 < NB:
                                load(PIECES + hp)
                            if hp >= 1:
                                sp.wait_ge(s_out, hp)
                                sp.dma_start(s_view[(hp - 1) // 2, (hp - 1) % 2], res[:, (hp - 1) % 2, :, :]).then_inc(stored[(hp - 1) % 2], 16)
                        for i in range(2):
                            sp.wait_ge(stored[i], 16 * (HP // 2))

                    @block.gpsimd
                    def _(pool):
                        for n in range(NB * PIECES):
                            b, q = divmod(n, PIECES)
                            pool.wait_ge(hi_done, n + 1)
                            pool.tensor_tensor(w_lo[:, b % 2, 2 * q:2 * q + 2, :], raw[:, n % 4, :, :],
                                               w_hi[:, b % 2, 2 * q:2 * q + 2, :], ALU.subtract).then_inc(lo_done, 1)

                    @block.scalar
                    def _(act):
                        def split(n):
                            b, q = divmod(n, PIECES)
                            act.wait_ge(raw_in[n % 4], 16 * (n // 4 + 1))
                            if b >= 2:
                                act.wait_ge(q_done, 8 * (b - 1))
                            act.activation(w_hi[:, b % 2, 2 * q:2 * q + 2, :], raw[:, n % 4, :, :], ACT.Copy).then_inc(hi_done, 1)

                        for n in range(PIECES):
                            split(n)
                        for c in range(2):
                            act.wait_ge(sk_tr, c + 1)
                            act.activation(sk_hi_sb[:, 8 * c:8 * c + 8, :], ps_s[c][:].rearrange("p (k t) -> p k t", t=P), ACT.Copy).then_inc(sk_hi, 1)
                        for hp in range(HP):
                            if hp // 4 + 1 < NB:
                                split(PIECES + hp)
                            for th in range(2):
                                act.wait_ge(q_done, 2 * hp + th + 1)
                                if hp >= 2:
                                    act.wait_ge(s_done, hp - 1)
                                act.activation(q_hi[:, hp % 2, th * HALF:(th + 1) * HALF], ps_q[(2 * hp + th) % 4][:], ACT.Copy).then_inc(q_hi_done, 1)

                    @block.vector
                    def _(dve):
                        for c in range(2):
                            dve.wait_ge(sk_hi, c + 1)
                            dve.tensor_tensor(sk_lo_sb[:, 8 * c:8 * c + 8, :], ps_s[c][:].rearrange("p (k t) -> p k t", t=P),
                                              sk_hi_sb[:, 8 * c:8 * c + 8, :], ALU.subtract).then_inc(sk_lo, 1)

                        def scores_out(hp):
                            dve.wait_ge(s_done, hp + 1)
                            if hp >= 2:
                                dve.wait_ge(stored[hp % 2], 16 * (hp // 2))
                            dve.tensor_copy(res[:, hp % 2, :, :], ps_s[hp % 2][:].rearrange("p (k t) -> p k t", t=P)).then_inc(s_out, 1)

                        for hp in range(HP):
                            for th in range(2):
                                dve.wait_ge(q_hi_done, 2 * hp + th + 1)
                                dve.tensor_tensor(q_lo[:, hp % 2, th * HALF:(th + 1) * HALF], ps_q[(2 * hp + th) % 4][:],
                                                  q_hi[:, hp % 2, th * HALF:(th + 1) * HALF], ALU.subtract).then_inc(q_lo_done, 1)
                            if hp >= 1:
                                scores_out(hp - 1)
                        scores_out(HP - 1)

                    @block.tensor
                    def _(pe):
                        pe.wait_ge(sk_in, 16)
                        for hp in range(HP):
                            last = pe.transpose(ps_s[hp // 8][:, (hp % 8) * P:(hp % 8 + 1) * P], sraw[:, hp, :], ident[:])
                            if hp % 8 == 7:
                                last.then_inc(sk_tr, 1)

                        def scores(hp):
                            pe.wait_ge(q_lo_done, 2 * hp + 2)
                            if hp < 2:
                                pe.wait_ge(sk_lo, 2)
                            else:
                                pe.wait_ge(s_out, hp - 1)
                            for j in range(TT):
                                tok = slice(j * P, (j + 1) * P)
                                last = three(pe, ps_s[hp % 2][:, tok], q_hi[:, hp % 2, tok], q_lo[:, hp % 2, tok],
                                             sk_hi_sb[:, hp, :], sk_lo_sb[:, hp, :], True, True)
                            last.then_inc(s_done, 1)

                        for hp in range(HP):
                            b, f = divmod(hp, 4)
                            for th in range(2):
                                u = 2 * hp + th
                                if u >= 4:
                                    pe.wait_ge(q_lo_done, u - 3)
                                for k in range(KT):
                                    if f == 0 and th == 0 and k % 2 == 0:
                                        pe.wait_ge(lo_done, b * PIECES + k // 2 + 1)
                                    col, tok = slice(f * P, (f + 1) * P), slice(th * HALF, (th + 1) * HALF)
                                    last = three(pe, ps_q[u % 4][:], w_hi[:, b % 2, k, col], w_lo[:, b % 2, k, col],
                                                 aT_hi[:, k, tok], aT_lo[:, k, tok], k == 0, k == KT - 1)
                                last.then_inc(q_done, 1)
                            if hp >= 1:
                                scores(hp - 1)
                        scores(HP - 1)

        def expert_in_stage():
            ROUTE_STEPS, ROUTE_E = 32, 2
            GATE_STEPS, GATE_E = 16, 4
            HALF_E = ROUTE_STEPS * ROUTE_E
            ETILES = HALF_E + GATE_STEPS * GATE_E
            u_rows = expert_u.rearrange("(p e) d -> e p d", e=P)

            raw_in = [sem(f"ei_raw_in{i}") for i in range(2)]
            tr_done, uT_hi_done, uT_lo_done = sem("ei_tr"), sem("ei_uT_hi"), sem("ei_uT_lo")
            mm_done = sem("ei_mm")
            gelu_done = [sem(f"ei_gelu{i}") for i in range(2)]
            act_stored = [sem(f"ei_act_stored{i}") for i in range(2)]
            iota_done, rank = sem("ei_iota"), sem("ei_rank")
            s_in = [sem(f"ei_s_in{i}") for i in range(2)]
            top_done, exp_done = sem("ei_top"), sem("ei_exp")
            route_done, rt_done, rt_out = sem("ei_route"), sem("ei_rt"), sem("ei_rt_out")
            rt_stored = [sem(f"ei_rt_stored{i}") for i in range(2)]
            col_in = [sem(f"ei_col_in{i}") for i in range(2)]
            hot = sem("ei_hot")
            hot_done = [sem(f"ei_hot_done{i}") for i in range(2)]
            last_done = [sem(f"ei_last_done{i}") for i in range(2)]
            g_done = [[sem(f"ei_g_done{i}{g}") for g in range(2)] for i in range(2)]
            g_out = [sem(f"ei_g_out{i}") for i in range(2)]
            g_stored = [sem(f"ei_g_stored{i}") for i in range(2)]
            BATCH, GROUP = 8, 4
            BATCHES = GBLK // BATCH

            def route_step(it, s):
                return it * ROUTE_E + s, s, it + 0, s

            def gate_step(it, s):
                return it * GATE_E + (HALF_E + s), s % 2, it * (GATE_E // 2) + (HALF_E // 2 + s // 2), s

            with ExitStack() as stage:
                sb, pb = local(stage)
                u_raw = sb("ei_u_raw", [P, 2, D])
                uT_hi, uT_lo = sb("ei_uT_hi_sb", [P, 2, KT, P], F32R), sb("ei_uT_lo_sb", [P, 2, KT, P], F32R)
                act_sb = sb("ei_act", [P, 2, T])
                iota = sb("ei_iota_sb", [P, P])
                s_sb = sb("ei_s", [P, 2, 2, KEYS])
                s_left = sb("ei_s_left", [P, 2, KEYS])
                kv = sb("ei_kv", [P, 2, TOPK])
                ki = sb("ei_ki", [P, 2, TOPK], U32)
                kf = sb("ei_kf", [P, 2, TOPK])
                pair, pair_left = sb("ei_pair", [P, TOPK, TOPK]), sb("ei_pair_left", [P, TOPK, TOPK])
                gv, gi = sb("ei_gv", [P, 2, TOPK]), sb("ei_gi", [P, TOPK], U32)
                gpos, gpf = sb("ei_gpos", [P, 2, TOPK], U32), sb("ei_gpf", [P, 2, TOPK])
                pick = sb("ei_pick", [P, 2, TOPK, TOPK])
                gneg, gexp = sb("ei_gneg", [P, 2]), sb("ei_gexp", [P, 2, TOPK])
                gsum, ginv = sb("ei_gsum", [P, 2]), sb("ei_ginv", [P, 2])
                route = sb("ei_route_sb", [P, 2, TOPK, 3])
                routeT = sb("ei_routeT", [3 * TOPK, 2, P])
                col = sb("ei_col", [P, 2, 3, GBLK])
                w_rest = sb("ei_w_rest", [P, 2, GBLK])
                w_part = [sb(f"ei_w_part{c}", [P, 2, GBLK], BF16) for c in range(3)]
                hot1, hot2 = sb("ei_hot1", [P, 2, BATCH, P], BF16), sb("ei_hot2", [P, 2, BATCH, P], BF16)
                hw = [sb(f"ei_hw{c}", [P, 2, BATCH, P], BF16) for c in range(3)]
                gate_sb = sb("ei_gate", [P, 2, P, GBLK])
                ps_t = pb("ei_ps_t", D)
                ps_h = [pb(f"ei_ps_h{i}", T) for i in range(2)]
                ps_x = [pb(f"ei_ps_x{i}", HALF) for i in range(2)]
                route_cols = route_d.rearrange("(j h) (k q) t -> j (h k) q t", h=PH, q=3)
                RANKS = 24
                HOTS = 4 + 3 * BATCHES

                with nc.Block() as block:
                    @block.sync
                    def _(sp):
                        def load_expert(step):
                            e, i, _, _ = step
                            sp.wait_ge(tr_done, e + 1)
                            sp.dma_start(u_raw[:, i, :], u_rows[e + 2, :, :]).then_inc(raw_in[i], 16)

                        def store_act(step):
                            e, i, n, _ = step
                            sp.wait_ge(gelu_done[i], n + 1)
                            sp.dma_start(act_d[e, :, :], act_sb[:, i, :]).then_inc(act_stored[i], 16)

                        def load_scores(u, i):
                            sp.dma_start(s_sb[:, i, :, :], s_d[u].rearrange("t (q k) -> t q k", q=2)).then_inc(s_in[i], 16)

                        def store_route(u, i):
                            sp.wait_ge(rt_out, u + 1)
                            sp.dma_start(route_d[u, :, :], routeT[:, i, :]).then_inc(rt_stored[i], 16)

                        def load_col(tile, off, b):
                            src = route_cols[tile][:, :, bass.ds(off, GBLK)]
                            sp.dma_start(col[:, b, :, :], src).then_inc(col_in[b], 16)

                        def store_gate(it, b):
                            sp.wait_ge(g_out[1], (it * 2 + (b + 1)) * BATCHES)
                            sp.dma_start(gate_d[it * 2 + b], gate_sb[:, b, :, :]).then_inc(g_stored[b], 16)

                        for i in range(2):
                            sp.dma_start(u_raw[:, i, :], u_rows[i, :, :]).then_inc(raw_in[i], 16)
                            load_scores(i, i)

                        def route_body(it, more):
                            for s in range(ROUTE_E):
                                step = route_step(it, s)
                                load_expert(step)
                                if more:
                                    sp.wait_ge(rank, (step[0] + 1) * RANKS)
                                    load_scores(step[0] + 2, s)
                                store_route(step[0], s)
                                store_act(step)

                        with sp.Fori(0, ROUTE_STEPS - 1) as it:
                            route_body(it, True)
                        route_body(ROUTE_STEPS - 1, False)
                        for i in range(2):
                            sp.wait_ge(rt_stored[i], 16 * (UNITS // 2))
                        load_col(0, 0, 0)
                        load_col(0, GBLK, 1)

                        def gate_body(it, more):
                            for s in range(GATE_E):
                                step = gate_step(it, s)
                                if more or s < GATE_E - 2:
                                    load_expert(step)
                                if s % 2 == 1:
                                    store_gate(it, s // 2)
                                    if more:
                                        load_col((it + 1) // 2, ((it + 1) % 2) * (2 * GBLK) + s // 2 * GBLK, s // 2)
                                store_act(step)

                        with sp.Fori(0, GATE_STEPS - 1) as it:
                            gate_body(it, True)
                        gate_body(GATE_STEPS - 1, False)
                        for i in range(2):
                            sp.wait_ge(act_stored[i], 16 * (ETILES // 2))
                            sp.wait_ge(g_stored[i], 16 * GATE_STEPS)

                    @block.gpsimd
                    def _(pool):
                        pool.iota(iota[:], [[1, P]], base=0, channel_multiplier=0,
                                  allow_small_or_imprecise_dtypes=True).then_inc(iota_done, 1)

                        with pool.Fori(0, GATE_STEPS) as it:
                            for b in range(2):
                                for m in range(BATCHES):
                                    i, t0 = m % 2, m * BATCH
                                    part = w_part[2][:, b, t0:t0 + BATCH].unsqueeze(2).broadcast_to([P, BATCH, P])
                                    pool.wait_ge(hot, it * (2 * HOTS) + (b * HOTS + 4 + 3 * m + 1))
                                    pool.wait_ge(g_done[i][1], it * BATCHES + (b * (BATCHES // 2) + m // 2))
                                    pool.tensor_tensor(hw[2][:, i, :, :], hot2[:, i, :, :], part, ALU.mult).then_inc(last_done[i], 1)

                    @block.scalar
                    def _(act):
                        def next_hi(step):
                            e, i, _, _ = step
                            act.wait_ge(tr_done, e + 2)
                            act.wait_ge(mm_done, e)
                            act.activation(uT_hi[:, 1 - i, :, :], ps_t[:].rearrange("p (k t) -> p k t", t=P), ACT.Copy).then_inc(uT_hi_done, 1)

                        def gelu(step):
                            e, i, n, _ = step
                            act.wait_ge(mm_done, e + 1)
                            act.wait_ge(act_stored[i], n * 16)
                            act.activation(act_sb[:, i, :], ps_h[i][:], ACT.Gelu).then_inc(gelu_done[i], 1)

                        act.wait_ge(tr_done, 1)
                        act.activation(uT_hi[:, 0, :, :], ps_t[:].rearrange("p (k t) -> p k t", t=P), ACT.Copy).then_inc(uT_hi_done, 1)

                        with act.Fori(0, ROUTE_STEPS) as it:
                            for s in range(ROUTE_E):
                                step = route_step(it, s)
                                u, i, n, _ = step
                                next_hi(step)
                                act.wait_ge(top_done, u + 1)
                                act.activation(gexp[:, i, :], gv[:, i, :], ACT.Exp, bias=gneg[:, i:i + 1],
                                               accum_out=gsum[:, i:i + 1]).then_inc(exp_done, 1)
                                gelu(step)
                                act.wait_ge(rt_done, u + 1)
                                act.wait_ge(rt_stored[i], n * 16)
                                act.activation(routeT[:, i, :], ps_x[i][0:3 * TOPK, 0:P], ACT.Copy).then_inc(rt_out, 1)

                        def gates_out(it, s, m, gh):
                            b = s // 2
                            act.wait_ge(g_done[m % 2][gh], it * BATCHES + (b * (BATCHES // 2) + m // 2 + 1))
                            if m == 0 and gh == 0:
                                act.wait_ge(g_stored[b], it * 16)
                            t0 = m * BATCH + gh * GROUP
                            act.activation(gate_sb[:, b, :, t0:t0 + GROUP].rearrange("p i t -> p t i"),
                                           ps_x[gh][:].rearrange("p (t i) -> p t i", i=P), ACT.Copy).then_inc(g_out[gh], 1)

                        def gate_body(it, more):
                            for s in range(GATE_E):
                                step = gate_step(it, s)
                                if more or s < GATE_E - 1:
                                    next_hi(step)
                                for q in range(4):
                                    gates_out(it, s, 2 * (s % 2) + q // 2, q % 2)
                                gelu(step)

                        with act.Fori(0, GATE_STEPS - 1) as it:
                            gate_body(it, True)
                        gate_body(GATE_STEPS - 1, False)

                    @block.vector
                    def _(dve):
                        def next_lo(step):
                            e, i, _, _ = step
                            dve.wait_ge(uT_hi_done, e + 2)
                            dve.tensor_tensor(uT_lo[:, 1 - i, :, :], ps_t[:].rearrange("p (k t) -> p k t", t=P), uT_hi[:, 1 - i, :, :],
                                              ALU.subtract).then_inc(uT_lo_done, 1)

                        count_reg = dve.alloc_register("ei_count")

                        def wait_apart(signal, count):
                            dve.reg_mov(count_reg, count)
                            dve.wait_ge(iota_done, 1)
                            dve.wait_ge(signal, count_reg)

                        def rank_unit(step):
                            u, i, n, _ = step
                            links = [0]

                            def link(ins, wait=True):
                                links[0] += 1
                                ins.then_inc(rank, 1)
                                if wait:
                                    wait_apart(rank, u * RANKS + links[0])

                            wait_apart(s_in[i], n * 16 + 16)
                            for q in range(2):
                                src = s_sb[:, i, q, :]
                                link(dve.max(kv[:, q, 0:8], src))
                                link(dve.match_replace(out=s_left[:, q, :], in_to_replace=kv[:, q, 0:8], in_values=src, imm_value=LOWEST), False)
                                link(dve.max_index(ki[:, q, 0:8], kv[:, q, 0:8], src))
                                link(dve.max(kv[:, q, 8:16], s_left[:, q, :]))
                                link(dve.max_index(ki[:, q, 8:16], kv[:, q, 8:16], s_left[:, q, :]), q == 1)
                            link(dve.tensor_copy(kf[:], ki[:]), False)
                            link(dve.tensor_tensor(pair[:], kv[:, 0, :].unsqueeze(2).broadcast_to([P, TOPK, TOPK]),
                                                   kv[:, 1, :].unsqueeze(1).broadcast_to([P, TOPK, TOPK]), ALU.add))
                            flat, left = pair[:].rearrange("p a b -> p (a b)"), pair_left[:].rearrange("p a b -> p (a b)")
                            link(dve.max(gv[:, i, 0:8], flat))
                            link(dve.match_replace(out=left, in_to_replace=gv[:, i, 0:8], in_values=flat, imm_value=LOWEST), False)
                            link(dve.max_index(gi[:, 0:8], gv[:, i, 0:8], flat))
                            link(dve.max(gv[:, i, 8:16], left))
                            link(dve.max_index(gi[:, 8:16], gv[:, i, 8:16], left))
                            dve.tensor_scalar(gneg[:, i:i + 1], gv[:, i, 0:1], -1.0, None, ALU.mult).then_inc(top_done, 1)
                            link(dve.tensor_scalar(gpos[:, 0, :], gi[:], 4, None, ALU.logical_shift_right), False)
                            link(dve.tensor_scalar(gpos[:, 1, :], gi[:], TOPK - 1, None, ALU.bitwise_and))
                            link(dve.tensor_copy(gpf[:], gpos[:]))
                            link(dve.tensor_tensor(pick[:], gpf[:].unsqueeze(3).broadcast_to([P, 2, TOPK, TOPK]),
                                                   iota[:, 0:TOPK].unsqueeze(1).unsqueeze(1).broadcast_to([P, 2, TOPK, TOPK]), ALU.is_equal))
                            link(dve.tensor_tensor(pick[:], pick[:], kf[:].unsqueeze(2).broadcast_to([P, 2, TOPK, TOPK]), ALU.mult))
                            dve.wait_ge(rt_done, it_floor(u, i))
                            link(dve.tensor_reduce(route[:, i, :, 1:3].rearrange("p k q -> p q k"), pick[:], AX.X, ALU.add), False)
                            return link

                        def it_floor(u, i):
                            return u - i

                        def weigh_unit(step, link):
                            u, i, _, _ = step
                            dve.wait_ge(exp_done, u + 1)
                            link(dve.reciprocal(ginv[:, i:i + 1], gsum[:, i:i + 1]))
                            dve.tensor_scalar(route[:, i, :, 0], gexp[:, i, :], ginv[:, i:i + 1], None, ALU.mult).then_inc(route_done, 1)

                        dve.wait_ge(uT_hi_done, 1)
                        dve.tensor_tensor(uT_lo[:, 0, :, :], ps_t[:].rearrange("p (k t) -> p k t", t=P), uT_hi[:, 0, :, :],
                                          ALU.subtract).then_inc(uT_lo_done, 1)
                        dve.wait_ge(iota_done, 1)
                        with dve.Fori(0, ROUTE_STEPS) as it:
                            for s in range(ROUTE_E):
                                step = route_step(it, s)
                                link = rank_unit(step)
                                next_lo(step)
                                weigh_unit(step, link)

                        def batch(it, b, m):
                            i, t0 = m % 2, m * BATCH
                            before = it * BATCHES + (b * (BATCHES // 2) + m // 2)
                            base = it * (2 * HOTS) + (b * HOTS + 4 + 3 * m)
                            keys = iota[:].unsqueeze(1).broadcast_to([P, BATCH, P])

                            def per_token(t):
                                return t.unsqueeze(2).broadcast_to([P, BATCH, P])

                            dve.wait_ge(g_done[i][1], before)
                            dve.tensor_tensor(hot2[:, i, :, :], keys, per_token(col[:, b, 2, t0:t0 + BATCH]), ALU.is_equal).then_inc(hot, 1)
                            dve.tensor_tensor(hot1[:, i, :, :], keys, per_token(col[:, b, 1, t0:t0 + BATCH]), ALU.is_equal).then_inc(hot, 1)
                            dve.wait_ge(hot, base + 1)
                            dve.tensor_tensor(hw[0][:, i, :, :], hot2[:, i, :, :], per_token(w_part[0][:, b, t0:t0 + BATCH]), ALU.mult).then_inc(hot, 1)
                            dve.tensor_tensor(hw[1][:, i, :, :], hot2[:, i, :, :], per_token(w_part[1][:, b, t0:t0 + BATCH]), ALU.mult).then_inc(hot_done[i], 1)

                        def gate_body(it, more):
                            for s in range(GATE_E):
                                step = gate_step(it, s)
                                b = s // 2
                                if s % 2 == 0:
                                    dve.wait_ge(col_in[b], it * 16 + 16)
                                    split = it * (2 * HOTS) + b * HOTS
                                    dve.tensor_copy(w_part[0][:, b, :], col[:, b, 0, :]).then_inc(hot, 1)
                                    dve.wait_ge(hot, split + 1)
                                    dve.tensor_tensor(w_rest[:, b, :], col[:, b, 0, :], w_part[0][:, b, :], ALU.subtract).then_inc(hot, 1)
                                    dve.wait_ge(hot, split + 2)
                                    dve.tensor_copy(w_part[1][:, b, :], w_rest[:, b, :]).then_inc(hot, 1)
                                    dve.wait_ge(hot, split + 3)
                                    dve.tensor_tensor(w_part[2][:, b, :], w_rest[:, b, :], w_part[1][:, b, :], ALU.subtract).then_inc(hot, 1)
                                batch(it, b, 2 * (s % 2))
                                if more or s < GATE_E - 1:
                                    next_lo(step)
                                batch(it, b, 2 * (s % 2) + 1)

                        with dve.Fori(0, GATE_STEPS - 1) as it:
                            gate_body(it, True)
                        gate_body(GATE_STEPS - 1, False)

                    @block.tensor
                    def _(pe):
                        def transposes(i):
                            for k in range(KT):
                                last = pe.transpose(ps_t[:, k * P:(k + 1) * P], u_raw[:, i, k * P:(k + 1) * P], ident[:])
                            last.then_inc(tr_done, 1)

                        def next_transposes(step):
                            e, i, n, _ = step
                            pe.wait_ge(raw_in[1 - i], (n + i) * 16 + 16)
                            pe.wait_ge(uT_lo_done, e + 1)
                            transposes(1 - i)

                        def product(step, between):
                            e, i, n, _ = step
                            pe.wait_ge(uT_lo_done, e + 1)
                            pe.wait_ge(gelu_done[i], n)
                            q = 0
                            for c in range(2):
                                tok = slice(c * HALF, (c + 1) * HALF)
                                for k in range(KT):
                                    last = three(pe, ps_h[i][:, tok], uT_hi[:, i, k, :], uT_lo[:, i, k, :],
                                                 aT_hi[:, k, tok], aT_lo[:, k, tok], k == 0, k == KT - 1)
                                    if k == KT - 1 and c == 1:
                                        last.then_inc(mm_done, 1)
                                    if k % (KT // 2) == KT // 2 - 1:
                                        between(q)
                                        q += 1

                        pe.wait_ge(raw_in[0], 16)
                        transposes(0)

                        with pe.Fori(0, ROUTE_STEPS) as it:
                            for s in range(ROUTE_E):
                                step = route_step(it, s)
                                u, i, _, _ = step
                                next_transposes(step)
                                product(step, lambda q: None)
                                pe.wait_ge(raw_in[0], 16)
                                pe.wait_ge(route_done, u + 1)
                                pe.wait_ge(rt_out, u - i)
                                pe.transpose(ps_x[i][0:3 * TOPK, 0:P], route[:, i, :, :].rearrange("p k q -> p (k q)"), ident[:]).then_inc(rt_done, 1)
                        pe.wait_ge(rt_out, UNITS)

                        def gates(it, s, m, gh):
                            b, i = s // 2, m % 2
                            pe.wait_ge(hot_done[i], it * BATCHES + (b * (BATCHES // 2) + m // 2 + 1))
                            pe.wait_ge(last_done[i], it * BATCHES + (b * (BATCHES // 2) + m // 2 + 1))
                            pe.wait_ge(g_out[gh], it * (2 * BATCHES) + (b * BATCHES + m))
                            for t in range(GROUP):
                                at, tk = slice(t * P, (t + 1) * P), gh * GROUP + t
                                for c in range(3):
                                    last = pe.matmul(ps_x[gh][:, at], hot1[:, i, tk, :], hw[c][:, i, tk, :], start=c == 0, stop=c == 2)
                            last.then_inc(g_done[i][gh], 1)

                        def gate_body(it, more):
                            for s in range(GATE_E):
                                step = gate_step(it, s)
                                if more or s < GATE_E - 1:
                                    next_transposes(step)
                                product(step, lambda q: gates(it, s, 2 * (s % 2) + q // 2, q % 2))

                        with pe.Fori(0, GATE_STEPS - 1) as it:
                            gate_body(it, True)
                        gate_body(GATE_STEPS - 1, False)

        def expert_out_stage(gain, bias, resid, dest):
            GE = 4
            GROUPS = P // GE
            v_rows = expert_v.rearrange("(p e) d -> e p d", e=P)
            a_in = [sem(f"eo_a_in{i}") for i in range(2)]
            v_in = [sem(f"eo_v_in{i}") for i in range(2)]
            g_in = sem("eo_g_in")
            prod, a_hi_done, a_lo_done = sem("eo_prod"), sem("eo_a_hi"), sem("eo_a_lo")
            v_hi_done, v_lo_done = sem("eo_v_hi"), sem("eo_v_lo")
            mm_done = [sem(f"eo_mm{i}") for i in range(4)]
            added = [sem(f"eo_added{i}") for i in range(4)]
            row_in = [sem(f"eo_row_in{i}") for i in range(2)]
            sum_done, stored = sem("eo_sum"), sem("eo_stored")
            with ExitStack() as stage:
                sb, pb = local(stage)
                ln = RowNorm("eo_ln", sb, gain, bias)
                acc = sb("eo_acc", [P, TT, D])
                a_raw, v_raw = sb("eo_a_raw", [P, 2, T]), sb("eo_v_raw", [P, 2, D])
                row = v_raw
                g_raw = sb("eo_g_raw", [P, T // GBLK, GE, GBLK])
                a_hi, a_lo = sb("eo_a_hi_sb", [P, 2, GE, T], F32R), sb("eo_a_lo_sb", [P, 2, GE, T], F32R)
                v_hi, v_lo = sb("eo_v_hi_sb", [P, 2, GE, D], F32R), sb("eo_v_lo_sb", [P, 2, GE, D], F32R)
                ps = [pb(f"eo_ps{i}", D) for i in range(4)]

                with nc.Block() as block:
                    @block.sync
                    def _(sp):
                        def load_gates(q):
                            sp.wait_ge(prod, q * GE)
                            sp.dma_start(g_raw[:], gate_d[:, :, bass.ds(q * GE, GE), :].rearrange("n p e t -> p n e t")).then_inc(g_in, 16)

                        def store_row(j):
                            sp.wait_ge(ln.ln_done, j + 1)
                            sp.dma_start(dest[j * P:(j + 1) * P, :], acc[:, j, :]).then_inc(stored, 16)

                        def load_group(q, gates_at=2):
                            for j in range(GE):
                                e, i = q * GE + j, j % 2
                                if j == gates_at:
                                    load_gates(q)
                                if j >= 2:
                                    sp.wait_ge(a_lo_done, e - 1)
                                    sp.wait_ge(v_lo_done, e - 1)
                                else:
                                    sp.wait_ge(a_lo_done, e - j)
                                    sp.wait_ge(v_lo_done, e - j)
                                sp.dma_start(a_raw[:, i, :], act_d[e, :, :]).then_inc(a_in[i], 16)
                                sp.dma_start(v_raw[:, i, :], v_rows[e, :, :]).then_inc(v_in[i], 16)

                        load_group(0, gates_at=0)
                        load_group(1)
                        with sp.Fori(1, GROUPS // 2) as it:
                            for b in range(2):
                                load_group(it * 2 + b)
                        ln.load(sp)
                        sp.wait_ge(v_lo_done, P)
                        for j in range(TT):
                            if j >= 2:
                                sp.wait_ge(sum_done, j - 1)
                            sp.dma_start(row[:, j % 2, :], resid[j * P:(j + 1) * P, :]).then_inc(row_in[j % 2], 16)
                            if j >= 2:
                                store_row(j - 2)
                        store_row(TT - 2)
                        store_row(TT - 1)
                        sp.wait_ge(stored, 16 * TT)

                    @block.gpsimd
                    def _(pool):
                        with pool.Fori(0, GROUPS // 2) as it:
                            for b in range(2):
                                for j in range(GE):
                                    pool.wait_ge(v_hi_done, it * (2 * GE) + (b * GE + j + 1))
                                    pool.tensor_tensor(v_lo[:, b, j, :], v_raw[:, j % 2, :], v_hi[:, b, j, :], ALU.subtract).then_inc(v_lo_done, 1)
                        for j in range(TT):
                            ln.plus_bias(pool, j, acc[:, j, :])

                    @block.scalar
                    def _(act):
                        def split_group(it, b):
                            for j in range(GE):
                                e = it * (2 * GE) + (b * GE + j)
                                act.wait_ge(v_in[j % 2], it * (GE * 16) + (b * (GE // 2) + j // 2 + 1) * 16)
                                act.activation(v_hi[:, b, j, :], v_raw[:, j % 2, :], ACT.Copy).then_inc(v_hi_done, 1)
                                act.wait_ge(prod, e + 1)
                                act.activation(a_hi[:, b, j, :], a_raw[:, j % 2, :], ACT.Copy).then_inc(a_hi_done, 1)

                        split_group(0, 0)
                        with act.Fori(0, GROUPS // 2 - 1) as it:
                            act.wait_ge(mm_done[3], it * 4)
                            split_group(it, 1)
                            act.wait_ge(mm_done[3], it * 4 + 2)
                            split_group(it + 1, 0)
                        act.wait_ge(mm_done[3], (GROUPS // 2 - 1) * 4)
                        split_group(GROUPS // 2 - 1, 1)
                        for j in range(TT):
                            ln.square_root(act, j)
                            ln.normalise(act, j, acc[:, j, :])

                    @block.vector
                    def _(dve):
                        def multiply(it, b, j):
                            dve.wait_ge(a_in[j % 2], it * (GE * 16) + (b * (GE // 2) + j // 2 + 1) * 16)
                            if j == 0:
                                dve.wait_ge(g_in, it * 32 + (b + 1) * 16)
                            a = a_raw[:, j % 2, :].rearrange("p (n t) -> p n t", t=GBLK)
                            dve.tensor_tensor(a, a, g_raw[:, :, j, :], ALU.mult).then_inc(prod, 1)

                        def product_lo(it, b, j):
                            dve.wait_ge(a_hi_done, it * (2 * GE) + (b * GE + j + 1))
                            dve.tensor_tensor(a_lo[:, b, j, :], a_raw[:, j % 2, :], a_hi[:, b, j, :], ALU.subtract).then_inc(a_lo_done, 1)

                        def add(it, b, t, first=False):
                            n = it * 4 + (b * 2 + t // 4)
                            dve.wait_ge(mm_done[t % 4], n + 1)
                            if first:
                                dve.tensor_copy(acc[:, t, :], ps[t % 4][:]).then_inc(added[t % 4], 1)
                            else:
                                dve.tensor_tensor(acc[:, t, :], acc[:, t, :], ps[t % 4][:], ALU.add).then_inc(added[t % 4], 1)

                        for j in range(GE):
                            multiply(0, 0, j)
                            product_lo(0, 0, j)

                        def group_step(it, b, first=False):
                            ni, nb = (it, 1) if b == 0 else (it + 1, 0)
                            for j in range(GE):
                                multiply(ni, nb, j)
                                add(it, b, 2 * j, first)
                                product_lo(ni, nb, j)
                                add(it, b, 2 * j + 1, first)

                        group_step(0, 0, first=True)
                        group_step(0, 1)
                        with dve.Fori(1, GROUPS // 2 - 1) as it:
                            group_step(it, 0)
                            group_step(it, 1)
                        group_step(GROUPS // 2 - 1, 0)
                        for j in range(TT):
                            add(GROUPS // 2 - 1, 1, j)
                            dve.wait_ge(added[j % 4], GROUPS * 2 - 1 + j // 4)
                            dve.wait_ge(row_in[j % 2], 16 * (j // 2 + 1))
                            dve.scalar_tensor_tensor(acc[:, j, :], row[:, j % 2, :], ALPHA, acc[:, j, :], ALU.mult, ALU.add).then_inc(sum_done, 1)
                            dve.wait_ge(sum_done, j + 1)
                            ln.statistics(dve, j, acc[:, j, :])
                            if j >= 1:
                                ln.times_gain(dve, j - 1, acc[:, j - 1, :])
                            ln.scale(dve, j)
                        ln.times_gain(dve, TT - 1, acc[:, TT - 1, :])

                    @block.tensor
                    def _(pe):
                        with pe.Fori(0, GROUPS // 2) as it:
                            for b in range(2):
                                for t in range(TT):
                                    if t == 0:
                                        pe.wait_ge(a_lo_done, it * (2 * GE) + (b + 1) * GE)
                                        pe.wait_ge(v_lo_done, it * (2 * GE) + (b + 1) * GE)
                                    pe.wait_ge(added[t % 4], it * 4 + (b * 2 + t // 4))
                                    tok = slice(t * P, (t + 1) * P)
                                    for c in range(2):
                                        colc = slice(c * HALF, (c + 1) * HALF)
                                        for j in range(GE):
                                            last = three(pe, ps[t % 4][:, colc], a_hi[:, b, j, tok], a_lo[:, b, j, tok],
                                                         v_hi[:, b, j, colc], v_lo[:, b, j, colc], j == 0, j == GE - 1)
                                    last.then_inc(mm_done[t % 4], 1)

        norm_stage("n0", ln_in_g, ln_in_b, x, h0_d)
        free_sems()
        project_stage("pin", w_in, [(u_d, "gelu", 1.0), (v_d, "gelu", 1.0), (qb_d, "feat", float(B_HD) ** -0.5),
                                    (kb_d, "feat", 1.0), (vb_d, "tok", 1.0)])
        gate_stage()
        free_sems()
        attention_stage()
        free_sems()
        norm_stage("n1", ln1_g, ln1_b, h0_d, h1_d, weight=w_out)
        with ExitStack() as memory:
            msb, _ = local(memory)
            mk_hi, mk_lo = msb("mk_hi", [P, KT, MEM], F32R), msb("mk_lo", [P, KT, MEM], F32R)
            mv_hi, mv_lo = msb("mv_hi", [P, MT, D], F32R), msb("mv_lo", [P, MT, D], F32R)
            memory_stage(mk_hi, mk_lo, mv_hi, mv_lo)
            free_sems()
            project_stage("pxq", w_xq, [(xq_d[0:HALF, :], "feat", 1.0), (xq_d[HALF:D, :], "feat", 1.0)])
            cross_stage(mk_hi, mk_lo, mv_hi, mv_lo)
        free_sems()
        norm_stage("n2", ln2_g, ln2_b, h1_d, h2_d, weight=w_xo)
        free_sems()
        key_score_stage()
        free_sems()
        expert_in_stage()
        act_stack.close()
        free_sems()
        expert_out_stage(ln3_g, ln3_b, h2_d, out)


_INS = ["x", "mem", "ln_in_g", "ln_in_b", "w_in", "gate_ln_g", "gate_ln_b", "w_sp", "b_sp", "rel_bias", "w_out",
        "ln1_g", "ln1_b", "w_xq", "w_xk", "w_xv", "w_xo", "ln2_g", "ln2_b", "w_pq", "sub_keys", "expert_u",
        "expert_v", "ln3_g", "ln3_b"]


def kernel(**inputs):
    import numpy as _np
    import concourse.bacc as _bacc
    from concourse import mybir as _mybir
    from concourse.bass_utils import run_bass_kernel_spmd as _run

    nc = _bacc.Bacc("TRN2", target_bir_lowering=False, num_devices=1)
    arrays, args = {}, []
    for name in _INS:
        a = _np.asarray(inputs[name])
        if name != "ln_in_g" and name != "ln_in_b":
            a = a[0]
        a = _np.ascontiguousarray(a)
        arrays[f"in_{name}"] = a
        args.append(nc.dram_tensor(f"in_{name}", a.shape, _mybir.dt.from_np(a.dtype), kind="ExternalInput").ap())
    out = nc.dram_tensor("out_0", (T, D), F32, kind="ExternalOutput").ap()
    layer_program(nc, *args, out)
    r = _run(nc, [arrays], core_ids=[0])
    return r.results[0]["out_0"].reshape(1, T, D)
```

```python
from contextlib import ExitStack

import concourse.bass as bass
from concourse import mybir

F32 = mybir.dt.float32
F32R = mybir.dt.float32r
BF16 = mybir.dt.bfloat16
U32 = mybir.dt.uint32
ACT = mybir.ActivationFunctionType
ALU = mybir.AluOpType
AX = mybir.AxisListType

P = 128
D = 1024
T = 1024
KT = D // P
TT = T // P
HALF = 512
D_A = D // 2
D_B = D - D_A
A_GROUPS = 4
CHUNK = 64
B_HEADS = 8
B_HD = D_B // B_HEADS
BAND = 8 * CHUNK
SPAN = BAND + P
REL = 128
EXT = SPAN + P
MEM = 256
MT = MEM // P
X_HEADS = 4
X_HD = D // X_HEADS
PH = 8
KEYS = 128
TOPK = 16
UNITS = TT * PH
GBLK = 32
ALPHA = 2.0 ** 0.25
EPS = 1e-5
MASKED = -1e30
LOWEST = -3.4e38


def layer_program(nc, x, mem, ln_in_g, ln_in_b, w_in, gate_ln_g, gate_ln_b, w_sp, b_sp, rel_bias, w_out,
                  ln1_g, ln1_b, w_xq, w_xk, w_xv, w_xo, ln2_g, ln2_b, w_pq, sub_keys, expert_u,
                  expert_v, ln3_g, ln3_b, out):
    top = ExitStack()

    def dram(name, shape):
        return nc.dram_tensor(name, shape, F32, kind="Internal").ap()

    h0_d = dram("h0_d", [T, D])
    h1_d = dram("h1_d", [T, D])
    h2_d = dram("h2_d", [T, D])
    u_d = dram("u_d", [T, D_A])
    v_d = dram("v_d", [T, D_A])
    vb_d = dram("vb_d", [T, D_B])
    qb_d = dram("qb_d", [D_B, T])
    kb_d = dram("kb_d", [D_B, T])
    ext_d = dram("ext_d", [B_HEADS, EXT])
    xq_d = dram("xq_d", [D, T])
    s_d = dram("s_d", [UNITS, P, 2 * KEYS])
    route_d = dram("route_d", [UNITS, TOPK * 3, P])
    act_d = dram("act_d", [P, P, T])
    gate_d = dram("gate_d", [T // GBLK, P, P, GBLK])

    stage_sems = []

    def sem(name):
        stage_sems.append(nc.alloc_semaphore(name=name))
        return stage_sems[-1]

    def free_sems():
        nc.clear_and_free_semaphores(stage_sems)
        nc.all_engine_barrier()
        stage_sems.clear()

    def local(stage):
        def sb(name, shape, dt=F32):
            return stage.enter_context(nc.sbuf_tensor(name, shape, dt))

        def pb(name, cols):
            return stage.enter_context(nc.psum_tensor(name, [P, cols], F32))
        return sb, pb

    def spread(vec):
        return bass.AP(vec.tensor, vec.offset, [[0, P], [1, vec.shape[-1]]])

    def three(pe, ps, l_hi, l_lo, r_hi, r_lo, first, last):
        pe.matmul(ps, l_hi, r_hi, start=first, stop=False)
        pe.matmul(ps, l_hi, r_lo, start=False, stop=False)
        return pe.matmul(ps, l_lo, r_hi, start=False, stop=last)

    with top:
        act_stack = ExitStack()
        asb, _ = local(act_stack)
        ident = asb("ident", [P, P])
        aT_hi = asb("aT_hi", [P, KT, T], F32R)
        aT_lo = asb("aT_lo", [P, KT, T], F32R)

        ident_done, ext_in, ext_built, ext_out = sem("ident_done"), sem("ext_in"), sem("ext_built"), sem("ext_out")
        with ExitStack() as stage:
            sb, pb = local(stage)
            ext = sb("ext", [B_HEADS, EXT])
            rel = sb("rel", [B_HEADS, 2 * REL + 1])
            with nc.Block() as block:
                @block.gpsimd
                def _(pool):
                    pool.memset(ident[:], 0.0).then_inc(ident_done, 1)
                    pool.wait_ge(ident_done, 1)
                    pool.affine_select(out=ident[:], in_=ident[:], compare_op=ALU.not_equal, fill=1.0, base=0,
                                       pattern=[[-1, P]], channel_multiplier=1).then_inc(ident_done, 1)

                @block.sync
                def _(sp):
                    sp.dma_start(rel[:], rel_bias).then_inc(ext_in, 16)
                    sp.wait_ge(ext_built, 2)
                    sp.dma_start(ext_d, ext[:]).then_inc(ext_out, 16)
                    sp.wait_ge(ext_out, 16)

                @block.vector
                def _(dve):
                    near = EXT - BAND - 1
                    dve.wait_ge(ext_in, 16)
                    dve.tensor_copy(ext[:, 0:near], rel[:, 2 * REL - near:2 * REL]).then_inc(ext_built, 1)
                    dve.tensor_copy(ext[:, near:EXT], rel[:, 2 * REL:2 * REL + 1].broadcast_to([B_HEADS, EXT - near])).then_inc(ext_built, 1)

        class RowNorm:

            def __init__(self, tag, sb, gain, bias):
                self.gain, self.bias = gain, bias
                self.gb_in, self.chain, self.var_done = sem(f"{tag}_gb_in"), sem(f"{tag}_chain"), sem(f"{tag}_var")
                self.root_done, self.scale_done = sem(f"{tag}_root"), sem(f"{tag}_scale")
                self.unit_done, self.gain_done, self.ln_done = sem(f"{tag}_unit"), sem(f"{tag}_gain"), sem(f"{tag}_ln")
                self.g_sb, self.b_sb = sb(f"{tag}_g", [P, D]), sb(f"{tag}_b", [P, D])
                self.stats, self.mv = sb(f"{tag}_stats", [P, 2, 2, 6]), sb(f"{tag}_mv", [P, 2, 2])
                self.var, self.root = sb(f"{tag}_var_sb", [P, 2]), sb(f"{tag}_root_sb", [P, 2])
                self.rstd, self.shift = sb(f"{tag}_rstd", [P, 2]), sb(f"{tag}_shift", [P, 2])
                self.links = 0

            def load(self, sp):
                sp.dma_start(self.g_sb[:], spread(self.gain)).then_inc(self.gb_in, 16)
                sp.dma_start(self.b_sb[:], spread(self.bias)).then_inc(self.gb_in, 16)

            def link(self, dve, ins):
                self.links += 1
                ins.then_inc(self.chain, 1)
                dve.wait_ge(self.chain, self.links)

            def statistics(self, dve, j, x):
                i = j % 2
                for c in range(2):
                    self.link(dve, dve.bn_stats(self.stats[:, i, c, :], x[:, c * HALF:(c + 1) * HALF]))
                self.link(dve, dve.bn_aggr(self.mv[:, i, :], self.stats[:, i, :, :].rearrange("p a b -> p (a b)")))
                dve.tensor_scalar(self.var[:, i:i + 1], self.mv[:, i, 1:2], EPS, None, ALU.add).then_inc(self.var_done, 1)

            def square_root(self, act, j):
                i = j % 2
                act.wait_ge(self.var_done, j + 1)
                act.activation(self.root[:, i:i + 1], self.var[:, i:i + 1], ACT.Sqrt).then_inc(self.root_done, 1)

            def scale(self, dve, j):
                i = j % 2
                dve.wait_ge(self.root_done, j + 1)
                if j >= 2:
                    dve.wait_ge(self.unit_done, j - 1)
                self.link(dve, dve.reciprocal(self.rstd[:, i:i + 1], self.root[:, i:i + 1]))
                dve.tensor_scalar(self.shift[:, i:i + 1], self.mv[:, i, 0:1], self.rstd[:, i:i + 1], -1.0,
                                  ALU.mult, ALU.mult).then_inc(self.scale_done, 1)

            def normalise(self, act, j, x):
                i = j % 2
                act.wait_ge(self.scale_done, j + 1)
                act.activation(x, x, ACT.Identity, scale=self.rstd[:, i:i + 1], bias=self.shift[:, i:i + 1]).then_inc(self.unit_done, 1)

            def times_gain(self, dve, j, x):
                if j == 0:
                    dve.wait_ge(self.gb_in, 32)
                dve.wait_ge(self.unit_done, j + 1)
                dve.tensor_tensor(x, x, self.g_sb[:], ALU.mult).then_inc(self.gain_done, 1)

            def plus_bias(self, pool, j, x):
                if j == 0:
                    pool.wait_ge(self.gb_in, 32)
                pool.wait_ge(self.gain_done, j + 1)
                pool.tensor_tensor(x, x, self.b_sb[:], ALU.add).then_inc(self.ln_done, 1)

        def norm_stage(tag, gain, bias, resid, dest, weight=None):
            ROWS = TT if weight is None else 4
            TR = 4 if weight is None else 2
            LAG = TR - 1 if weight is None else TR
            w_raw_in = [sem(f"{tag}_w_raw_in{i}") for i in range(4)]
            w_hi_done = sem(f"{tag}_w_hi")
            w_lo_done = [sem(f"{tag}_w_lo{i}") for i in range(2)]
            row_in = [sem(f"{tag}_row_in{i}") for i in range(ROWS)]
            stored = [sem(f"{tag}_stored{i}") for i in range(ROWS)]
            mm_done, sum_done = sem(f"{tag}_mm"), sem(f"{tag}_sum")
            tr_done, hi_done, lo_done = sem(f"{tag}_tr"), sem(f"{tag}_hi"), sem(f"{tag}_lo")
            with ExitStack() as stage:
                sb, pb = local(stage)
                ln = RowNorm(tag, sb, gain, bias)
                row = sb(f"{tag}_row", [P, ROWS, D])
                if weight is not None:
                    w_raw = sb(f"{tag}_w_raw", [P, 4, D])
                    w_hi, w_lo = sb(f"{tag}_whi", [P, KT, D], F32R), sb(f"{tag}_wlo", [P, KT, D], F32R)
                    ps_mm = [pb(f"{tag}_ps_mm{i}", D) for i in range(2)]
                ps_tr = [pb(f"{tag}_ps_tr{i}", D) for i in range(TR)]

                def x(j):
                    return row[:, j % ROWS, :]

                with nc.Block() as block:
                    @block.sync
                    def _(sp):
                        def load_row(j):
                            sp.dma_start(x(j), resid[j * P:(j + 1) * P, :]).then_inc(row_in[j % ROWS], 16)

                        if weight is not None:
                            for k in range(KT):
                                if k >= 4:
                                    sp.wait_ge(w_lo_done[k % 2], k // 2 - 1)
                                sp.dma_start(w_raw[:, k % 4, :], weight[k * P:(k + 1) * P, :]).then_inc(w_raw_in[k % 4], 16)
                        for j in range(ROWS):
                            load_row(j)
                            if j == 1:
                                ln.load(sp)
                        for j in range(TT):
                            sp.wait_ge(ln.ln_done, j + 1)
                            sp.dma_start(dest[j * P:(j + 1) * P, :], x(j)).then_inc(stored[j % ROWS], 16)
                            if 1 <= j and j - 1 + ROWS < TT:
                                sp.wait_ge(stored[(j - 1) % ROWS], 16 * ((j - 1) // ROWS + 1))
                                sp.wait_ge(tr_done, j)
                                load_row(j - 1 + ROWS)
                        for i in range(ROWS):
                            sp.wait_ge(stored[i], 16 * (TT // ROWS))

                    @block.gpsimd
                    def _(pool):
                        if weight is not None:
                            for k in range(1, KT, 2):
                                pool.wait_ge(w_hi_done, k + 1)
                                pool.tensor_tensor(w_lo[:, k, :], w_raw[:, k % 4, :], w_hi[:, k, :], ALU.subtract).then_inc(w_lo_done[1], 1)
                        for j in range(TT):
                            ln.plus_bias(pool, j, x(j))

                    @block.scalar
                    def _(act):
                        if weight is not None:
                            for k in range(KT):
                                act.wait_ge(w_raw_in[k % 4], 16 * (k // 4 + 1))
                                act.activation(w_hi[:, k, :], w_raw[:, k % 4, :], ACT.Copy).then_inc(w_hi_done, 1)

                        def transposed_hi(j):
                            act.wait_ge(tr_done, j + 1)
                            act.activation(aT_hi[:, :, j * P:(j + 1) * P], ps_tr[j % TR][:].rearrange("p (k t) -> p k t", k=KT),
                                           ACT.Copy).then_inc(hi_done, 1)

                        for j in range(TT):
                            ln.square_root(act, j)
                            ln.normalise(act, j, x(j))
                            if j >= LAG:
                                transposed_hi(j - LAG)
                        for j in range(TT - LAG, TT):
                            transposed_hi(j)

                    @block.vector
                    def _(dve):
                        def transposed_lo(j):
                            dve.wait_ge(hi_done, j + 1)
                            dve.tensor_tensor(aT_lo[:, :, j * P:(j + 1) * P], ps_tr[j % TR][:].rearrange("p (k t) -> p k t", k=KT),
                                              aT_hi[:, :, j * P:(j + 1) * P], ALU.subtract).then_inc(lo_done, 1)

                        if weight is not None:
                            for k in range(0, KT, 2):
                                dve.wait_ge(w_hi_done, k + 1)
                                dve.tensor_tensor(w_lo[:, k, :], w_raw[:, k % 4, :], w_hi[:, k, :], ALU.subtract).then_inc(w_lo_done[0], 1)
                        for j in range(TT):
                            dve.wait_ge(row_in[j % ROWS], 16 * (j // ROWS + 1))
                            if weight is not None:
                                dve.wait_ge(mm_done, j + 1)
                                dve.scalar_tensor_tensor(x(j), x(j), ALPHA, ps_mm[j % 2][:], ALU.mult, ALU.add).then_inc(sum_done, 1)
                                dve.wait_ge(sum_done, j + 1)
                            ln.statistics(dve, j, x(j))
                            if j >= 1 and weight is None:
                                ln.times_gain(dve, j - 1, x(j - 1))
                            ln.scale(dve, j)
                            if weight is not None:
                                ln.times_gain(dve, j, x(j))
                            if j >= LAG:
                                transposed_lo(j - LAG)
                        if weight is None:
                            ln.times_gain(dve, TT - 1, x(TT - 1))
                        for j in range(TT - LAG, TT):
                            transposed_lo(j)

                    @block.tensor
                    def _(pe):
                        def transposes(j):
                            pe.wait_ge(ln.ln_done, j + 1)
                            if j >= TR:
                                pe.wait_ge(lo_done, j - TR + 1)
                            for k in range(KT):
                                last = pe.transpose(ps_tr[j % TR][:, k * P:(k + 1) * P], x(j)[:, k * P:(k + 1) * P], ident[:])
                            last.then_inc(tr_done, 1)

                        for j in range(TT):
                            if weight is not None:
                                if j >= 2:
                                    pe.wait_ge(sum_done, j - 1)
                                tok = slice(j * P, (j + 1) * P)
                                for k in range(KT):
                                    if j == 0:
                                        pe.wait_ge(w_lo_done[k % 2], k // 2 + 1)
                                    for c in range(2):
                                        col = slice(c * HALF, (c + 1) * HALF)
                                        last = three(pe, ps_mm[j % 2][:, col], aT_hi[:, k, tok], aT_lo[:, k, tok],
                                                     w_hi[:, k, col], w_lo[:, k, col], k == 0, k == KT - 1)
                                last.then_inc(mm_done, 1)
                            if j >= 1:
                                transposes(j - 1)
                        transposes(TT - 1)

        class Gating:
            FIRST, EVERY, SETUP = 16, 3, 8

            def __init__(self, sb, pb, sources):
                self.sources = sources
                self.consts_in, self.wt_tr, self.wt_hi, self.wt_lo = sem("ga_consts"), sem("ga_wt_tr"), sem("ga_wt_hi"), sem("ga_wt_lo")
                self.masked = sem("ga_masked")
                self.v_in = [sem(f"ga_v_in{i}") for i in range(2)]
                self.u_in = [sem(f"ga_u_in{i}") for i in range(2)]
                self.chain, self.var_done, self.root_done, self.vn_done = sem("ga_chain"), sem("ga_var"), sem("ga_root"), sem("ga_vn")
                self.vhi_done, self.vlo_done, self.mix_done, self.y_done = sem("ga_vhi"), sem("ga_vlo"), sem("ga_mix"), sem("ga_y")
                self.tr_done, self.hi_done, self.lo_done = sem("ga_tr"), sem("ga_hi"), sem("ga_lo")
                self.wraw = sb("ga_wraw", [P, A_GROUPS, P])
                self.wT_hi, self.wT_lo = sb("ga_wT_hi", [P, A_GROUPS, P], F32R), sb("ga_wT_lo", [P, A_GROUPS, P], F32R)
                self.bsp = sb("ga_bsp", [P, A_GROUPS])
                self.g_sb, self.b_sb = sb("ga_g", [P, D_A]), sb("ga_b", [P, D_A])
                self.v_sb, self.u_sb = sb("ga_v", [P, 2, D_A]), sb("ga_u", [P, 2, D_A])
                self.v_hi, self.v_lo = sb("ga_v_hi", [P, 2, D_A], F32R), sb("ga_v_lo", [P, 2, D_A], F32R)
                self.y_sb = sb("ga_y_sb", [P, TT, D_A])
                self.stats, self.mv = sb("ga_stats", [P, 2, 6]), sb("ga_mv", [P, 2, 2])
                self.var, self.root, self.rstd = sb("ga_var_sb", [P, 2]), sb("ga_root_sb", [P, 2]), sb("ga_rstd", [P, 2])
                self.ps_s = [pb(f"ga_ps_s{i}", HALF) for i in range(2)]
                self.ps_y = [pb(f"ga_ps_y{i}", HALF) for i in range(2)]
                self.links = 0

            def tile(self, u, delay):
                j, off = divmod(u - self.FIRST - delay, self.EVERY)
                return j if off == 0 and 0 <= j < TT else None

            def link(self, dve, ins):
                self.links += 1
                ins.then_inc(self.chain, 1)
                dve.wait_ge(self.chain, self.links)

            def sync_step(self, sp, u):
                if u == 0:
                    sp.dma_start(self.wraw[:], w_sp.rearrange("g i j -> i g j")).then_inc(self.consts_in, 16)
                    sp.dma_start(self.bsp[:], b_sp.rearrange("g i -> i g"), allow_slow_non_contiguous=True).then_inc(self.consts_in, 16)
                    sp.dma_start(self.g_sb[:], spread(gate_ln_g)).then_inc(self.consts_in, 16)
                    sp.dma_start(self.b_sb[:], spread(gate_ln_b)).then_inc(self.consts_in, 16)
                j = self.tile(u, 0)
                if j is None:
                    return
                if j == 0:
                    for stored, count in self.sources:
                        sp.wait_ge(stored, count)
                if j >= 2:
                    sp.wait_ge(self.vlo_done, j - 1)
                sp.dma_start(self.v_sb[:, j % 2, :], v_d[j * P:(j + 1) * P, :]).then_inc(self.v_in[j % 2], 16)
                if j >= 2:
                    sp.wait_ge(self.y_done, A_GROUPS * (j - 1))
                sp.dma_start(self.u_sb[:, j % 2, :], u_d[j * P:(j + 1) * P, :]).then_inc(self.u_in[j % 2], 16)

            def scalar_step(self, act, u):
                if u == self.SETUP:
                    act.wait_ge(self.wt_tr, 1)
                    act.activation(self.wT_hi[:], self.ps_y[0][:].rearrange("p (g i) -> p g i", g=A_GROUPS), ACT.Copy).then_inc(self.wt_hi, 1)
                j = self.tile(u, 1)
                if j is None:
                    return
                act.wait_ge(self.var_done, j + 1)
                act.activation(self.root[:, j % 2:j % 2 + 1], self.var[:, j % 2:j % 2 + 1], ACT.Sqrt).then_inc(self.root_done, 1)
                act.wait_ge(self.vn_done, j + 1)
                if j >= 2:
                    act.wait_ge(self.mix_done, j - 1)
                act.activation(self.v_hi[:, j % 2, :], self.v_sb[:, j % 2, :], ACT.Copy).then_inc(self.vhi_done, 1)

            def vector_step(self, dve, u):
                if u == self.SETUP:
                    dve.wait_ge(self.wt_hi, 1)
                    dve.tensor_tensor(self.wT_lo[:], self.ps_y[0][:].rearrange("p (g i) -> p g i", g=A_GROUPS), self.wT_hi[:],
                                      ALU.subtract).then_inc(self.wt_lo, 1)
                    dve.wait_ge(self.wt_lo, 1)
                    dve.memset(self.wT_hi[CHUNK:P, :, 0:CHUNK].bitcast(F32), 0.0).then_inc(self.masked, 1)
                    dve.memset(self.wT_lo[CHUNK:P, :, 0:CHUNK].bitcast(F32), 0.0).then_inc(self.masked, 1)
                    dve.wait_ge(self.consts_in, 64)
                j = self.tile(u, 1)
                if j is not None:
                    i = j % 2
                    v = self.v_sb[:, i, :]
                    dve.wait_ge(self.v_in[i], 16 * (j // 2 + 1))
                    self.link(dve, dve.bn_stats(self.stats[:, i, :], v))
                    self.link(dve, dve.bn_aggr(self.mv[:, i, :], self.stats[:, i, :]))
                    dve.tensor_scalar(self.var[:, i:i + 1], self.mv[:, i, 1:2], EPS, None, ALU.add).then_inc(self.var_done, 1)
                    dve.wait_ge(self.root_done, j + 1)
                    self.link(dve, dve.reciprocal(self.rstd[:, i:i + 1], self.root[:, i:i + 1]))
                    self.link(dve, dve.tensor_scalar(v, v, self.mv[:, i, 0:1], self.rstd[:, i:i + 1], ALU.subtract, ALU.mult))
                    self.link(dve, dve.tensor_tensor(v, v, self.g_sb[:], ALU.mult))
                    dve.tensor_tensor(v, v, self.b_sb[:], ALU.add).then_inc(self.vn_done, 1)
                    dve.wait_ge(self.vhi_done, j + 1)
                    dve.tensor_tensor(self.v_lo[:, i, :], v, self.v_hi[:, i, :], ALU.subtract).then_inc(self.vlo_done, 1)
                j = self.tile(u, 3)
                if j is not None:
                    dve.wait_ge(self.mix_done, j + 1)
                    dve.wait_ge(self.u_in[j % 2], 16 * (j // 2 + 1))
                    for g in range(A_GROUPS):
                        col = slice(g * P, (g + 1) * P)
                        dve.scalar_tensor_tensor(self.y_sb[:, j, col], self.ps_s[j % 2][:, col], self.bsp[:, g:g + 1],
                                                 self.u_sb[:, j % 2, col], ALU.add, ALU.mult).then_inc(self.y_done, 1)

            def tensor_step(self, pe, u):
                if u == self.SETUP:
                    pe.wait_ge(self.consts_in, 64)
                    for g in range(A_GROUPS):
                        last = pe.transpose(self.ps_y[0][:, g * P:(g + 1) * P], self.wraw[:, g, :], ident[:])
                    last.then_inc(self.wt_tr, 1)
                j = self.tile(u, 3)
                if j is None:
                    return
                if j == 0:
                    pe.wait_ge(self.masked, 2)
                pe.wait_ge(self.vlo_done, j + 1)
                if j >= 2:
                    pe.wait_ge(self.y_done, A_GROUPS * (j - 1))
                for g in range(A_GROUPS):
                    col = slice(g * P, (g + 1) * P)
                    last = three(pe, self.ps_s[j % 2][:, col], self.wT_hi[:, g, :], self.wT_lo[:, g, :],
                                 self.v_hi[:, j % 2, col], self.v_lo[:, j % 2, col], True, True)
                last.then_inc(self.mix_done, 1)

            def bank(self, j):
                return self.ps_y[j % 2][:].rearrange("p (k t) -> p k t", k=A_GROUPS)

            def part(self, aT, j):
                return aT[:, 0:A_GROUPS, j * P:(j + 1) * P]

            def finish_tensor(self, pe):
                for j in range(TT):
                    pe.wait_ge(self.y_done, A_GROUPS * (j + 1))
                    if j >= 2:
                        pe.wait_ge(self.lo_done, j - 1)
                    for k in range(A_GROUPS):
                        last = pe.transpose(self.ps_y[j % 2][:, k * P:(k + 1) * P], self.y_sb[:, j, k * P:(k + 1) * P], ident[:])
                    last.then_inc(self.tr_done, 1)

            def finish_scalar(self, act):
                for j in range(TT):
                    act.wait_ge(self.tr_done, j + 1)
                    act.activation(self.part(aT_hi, j), self.bank(j), ACT.Copy).then_inc(self.hi_done, 1)

            def finish_vector(self, dve):
                for j in range(TT):
                    dve.wait_ge(self.hi_done, j + 1)
                    dve.tensor_tensor(self.part(aT_lo, j), self.bank(j), self.part(aT_hi, j), ALU.subtract).then_inc(self.lo_done, 1)

        def project_stage(tag, weight, blocks, gated=False):
            raw_in = [sem(f"{tag}_raw_in{i}") for i in range(4)]
            hi_done, mm_done = sem(f"{tag}_hi"), sem(f"{tag}_mm")
            lo_done = [sem(f"{tag}_lo{i}") for i in range(2)]
            act_out, dve_out = sem(f"{tag}_act_out"), sem(f"{tag}_dve_out")
            stored = [sem(f"{tag}_stored{i}") for i in range(4)]
            NB, PIECES, PER = len(blocks), 4, 8
            units = [(b, i) for b in range(NB) for i in range(PER)]

            def by_act(u):
                return blocks[units[u][0]][1] == "gelu"

            def count(u):
                return sum(by_act(n) == by_act(u) for n in range(u + 1))

            def out_of_psum(eng, u):
                eng.wait_ge(act_out if by_act(u) else dve_out, count(u))

            with ExitStack() as stage:
                sb, pb = local(stage)
                raw = sb(f"{tag}_raw", [P, 4, 2, HALF])
                w_hi, w_lo = sb(f"{tag}_whi", [P, 2, KT, HALF], F32R), sb(f"{tag}_wlo", [P, 2, KT, HALF], F32R)
                res = sb(f"{tag}_res", [P, 4, HALF])
                gate = Gating(sb, pb, [(done, 16 * (Gating.FIRST // 4)) for done in stored]) if gated else None
                BANKS = 4 if gated else 8
                ps = [pb(f"{tag}_ps{i}", HALF) for i in range(BANKS)]
                after = range(len(units), len(units) + 3)
                with nc.Block() as block:
                    @block.sync
                    def _(sp):
                        def load(n):
                            b, q = divmod(n, PIECES)
                            if n >= 4:
                                sp.wait_ge(lo_done[n % 2], n // 2 - 1)
                            src = weight[2 * q * P:2 * (q + 1) * P, b * HALF:(b + 1) * HALF].rearrange("(a p) n -> p a n", p=P)
                            sp.dma_start(raw[:, n % 4, :, :], src).then_inc(raw_in[n % 4], 16)

                        for n in range(PIECES):
                            load(n)
                        for u, (b, i) in enumerate(units):
                            if b + 1 < NB and i % 2 == 0:
                                load((b + 1) * PIECES + i // 2)
                            if gated:
                                gate.sync_step(sp, u)
                            dest, kind, _ = blocks[b]
                            if kind == "feat":
                                f, th = divmod(i, 2)
                                to = dest[f * P:(f + 1) * P, th * HALF:(th + 1) * HALF]
                            else:
                                to = dest[i * P:(i + 1) * P, :]
                            out_of_psum(sp, u)
                            sp.dma_start(to, res[:, u % 4, :]).then_inc(stored[u % 4], 16)
                        for i in range(4):
                            sp.wait_ge(stored[i], 16 * (len(units) // 4))

                    @block.gpsimd
                    def _(pool):
                        for n in range(0, NB * PIECES, 2):
                            b, q = divmod(n, PIECES)
                            pool.wait_ge(hi_done, n + 1)
                            pool.tensor_tensor(w_lo[:, b % 2, 2 * q:2 * q + 2, :], raw[:, n % 4, :, :],
                                               w_hi[:, b % 2, 2 * q:2 * q + 2, :], ALU.subtract).then_inc(lo_done[0], 1)

                    @block.scalar
                    def _(act):
                        def split(n):
                            b, q = divmod(n, PIECES)
                            act.wait_ge(raw_in[n % 4], 16 * (n // 4 + 1))
                            if b >= 2:
                                act.wait_ge(mm_done, (b - 1) * PER)
                            act.activation(w_hi[:, b % 2, 2 * q:2 * q + 2, :], raw[:, n % 4, :, :], ACT.Copy).then_inc(hi_done, 1)

                        for n in range(PIECES):
                            split(n)
                        for u, (b, i) in enumerate(units):
                            if b + 1 < NB and i % 2 == 0:
                                split((b + 1) * PIECES + i // 2)
                            if by_act(u):
                                act.wait_ge(mm_done, u + 1)
                                if u >= 4:
                                    act.wait_ge(stored[u % 4], 16 * (u // 4))
                                act.activation(res[:, u % 4, :], ps[u % BANKS][:], ACT.Gelu).then_inc(act_out, 1)
                            if gated:
                                gate.scalar_step(act, u)
                        if gated:
                            for u in after:
                                gate.scalar_step(act, u)
                            gate.finish_scalar(act)

                    @block.vector
                    def _(dve):
                        def split_lo(n):
                            b, q = divmod(n, PIECES)
                            dve.wait_ge(hi_done, n + 1)
                            dve.tensor_tensor(w_lo[:, b % 2, 2 * q:2 * q + 2, :], raw[:, n % 4, :, :],
                                              w_hi[:, b % 2, 2 * q:2 * q + 2, :], ALU.subtract).then_inc(lo_done[1], 1)

                        split_lo(1)
                        split_lo(3)
                        for u, (b, i) in enumerate(units):
                            if b + 1 < NB and i % 4 == 2:
                                split_lo((b + 1) * PIECES + i // 2)
                            if not by_act(u):
                                dve.wait_ge(mm_done, u + 1)
                                if u >= 4:
                                    dve.wait_ge(stored[u % 4], 16 * (u // 4))
                                dve.tensor_scalar(res[:, u % 4, :], ps[u % BANKS][:], blocks[b][2], None, ALU.mult).then_inc(dve_out, 1)
                            if gated:
                                gate.vector_step(dve, u)
                        if gated:
                            for u in after:
                                gate.vector_step(dve, u)
                            gate.finish_vector(dve)

                    @block.tensor
                    def _(pe):
                        for u, (b, i) in enumerate(units):
                            if gated:
                                gate.tensor_step(pe, u)
                            if u >= BANKS:
                                out_of_psum(pe, u - BANKS)
                            for k in range(KT):
                                if i == 0 and k % 2 == 0:
                                    pe.wait_ge(lo_done[k // 2 % 2], (b * PIECES + k // 2) // 2 + 1)
                                if blocks[b][1] == "feat":
                                    f, th = divmod(i, 2)
                                    col, tok = slice(f * P, (f + 1) * P), slice(th * HALF, (th + 1) * HALF)
                                    last = three(pe, ps[u % BANKS][:], w_hi[:, b % 2, k, col], w_lo[:, b % 2, k, col],
                                                 aT_hi[:, k, tok], aT_lo[:, k, tok], k == 0, k == KT - 1)
                                else:
                                    tok = slice(i * P, (i + 1) * P)
                                    last = three(pe, ps[u % BANKS][:], aT_hi[:, k, tok], aT_lo[:, k, tok],
                                                 w_hi[:, b % 2, k, :], w_lo[:, b % 2, k, :], k == 0, k == KT - 1)
                            last.then_inc(mm_done, 1)
                        if gated:
                            for u in after:
                                gate.tensor_step(pe, u)
                            gate.finish_tensor(pe)

        def attention_stage():
            bias_in, masked = sem("at_bias_in"), sem("at_masked")
            raw_in = [sem(f"at_raw_in{i}") for i in range(2)]
            sp_hi, sp_lo, sp_lo_v = sem("at_split_hi"), sem("at_split_lo"), sem("at_split_lo_v")
            s_done, max_done, neg_done, exp_done = sem("at_s"), sem("at_max"), sem("at_neg"), sem("at_exp")
            rec_done, norm_done = sem("at_rec"), sem("at_norm")
            tr_done, p_hi_done, p_lo_done, pv_done = sem("at_tr"), sem("at_p_hi"), sem("at_p_lo"), sem("at_pv")
            y_hi_done, y_lo_done = sem("at_y_hi"), sem("at_y_lo")
            QF = D_B // P
            NU = TT * B_HEADS
            units = [divmod(u, B_HEADS) for u in range(NU)]
            G0 = D_A // P

            def keys(n):
                nk = min(SPAN, (n + 1) * P)
                return (n + 1) * P - nk, nk, 1 if nk <= HALF else 2

            def backwards(row, parts):
                (step, count), (one, n) = row.ap
                w = n // parts
                return bass.AP(row.tensor, row.offset + (n - 1) * one, [[step, count], [-one * w, parts], [-one, w]])

            with ExitStack() as stage:
                sb, pb = local(stage)
                bias = sb("at_bias", [P, B_HEADS, SPAN])
                raw = sb("at_raw", [P, 2, D])
                q_hi, q_lo = sb("at_q_hi", [P, QF, T], F32R), sb("at_q_lo", [P, QF, T], F32R)
                k_hi, k_lo = sb("at_k_hi", [P, QF, T], F32R), sb("at_k_lo", [P, QF, T], F32R)
                v_hi, v_lo = sb("at_v_hi", [P, TT, D_B], F32R), sb("at_v_lo", [P, TT, D_B], F32R)
                prob = sb("at_prob", [P, 3, SPAN])
                pT_hi, pT_lo = sb("at_pT_hi", [P, 2, SPAN], F32R), sb("at_pT_lo", [P, 2, SPAN], F32R)
                top_s, neg, rsum, rinv = sb("at_top", [P, 2]), sb("at_neg_sb", [P, 2]), sb("at_rsum", [P, 4]), sb("at_rinv", [P, 2])
                ps_s = [pb(f"at_ps_s{i}", D) for i in range(2)]
                ps_t = pb("at_ps_t", D)
                ps_o = [pb(f"at_ps_o{i}", HALF) for i in range(2)]
                pieces = []
                for f in range(QF):
                    pieces.append((qb_d[f * P:(f + 1) * P, :], q_hi[:, f, :], q_lo[:, f, :]))
                    pieces.append((kb_d[f * P:(f + 1) * P, :], k_hi[:, f, :], k_lo[:, f, :]))
                for f in range(TT // 2):
                    pieces.append((vb_d[2 * f * P:2 * (f + 1) * P, :].rearrange("(a p) n -> p a n", p=P),
                                   v_hi[:, 2 * f:2 * f + 2, :], v_lo[:, 2 * f:2 * f + 2, :]))
                QK = 2 * QF

                def raw_of(n):
                    r = raw[:, n % 2, :]
                    return r if n < QK else r.rearrange("p (a n) -> p a n", a=2)

                def aT_cols(t, pair, half):
                    n, f = divmod(pair, QF)
                    return t[half * B_HD:(half + 1) * B_HD, G0 + f, n * P:(n + 1) * P]

                def out_cols(pair, half):
                    return ps_o[pair % 2][0:B_HD, half * P:(half + 1) * P]

                with nc.Block() as block:
                    @block.sync
                    def _(sp):
                        for n, (src, _, _) in enumerate(pieces):
                            if n >= QK + 2:
                                sp.wait_ge(sp_lo_v, n - QK - 1)
                            elif n >= 2:
                                sp.wait_ge(sp_lo, n - 1)
                            sp.dma_start(raw_of(n), src).then_inc(raw_in[n % 2], 16)
                            if n == 1:
                                sp.dma_start(bias[:], bass.AP(ext_d.tensor, ext_d.offset,
                                                              [[1, P], [EXT, B_HEADS], [1, SPAN]])).then_inc(bias_in, 16)

                    @block.gpsimd
                    def _(pool):
                        pool.wait_ge(bias_in, 16)
                        pool.memset(bias[0:CHUNK, :, 0:CHUNK], MASKED).then_inc(masked, 1)
                        pool.memset(bias[CHUNK:P, :, SPAN - CHUNK:SPAN], MASKED).then_inc(masked, 1)
                        pool.wait_ge(masked, 2)
                        for n in range(QK, len(pieces)):
                            pool.wait_ge(sp_hi, n + 1)
                            pool.tensor_tensor(pieces[n][2], raw_of(n), pieces[n][1], ALU.subtract).then_inc(sp_lo_v, 1)

                    @block.scalar
                    def _(act):
                        def split(n):
                            act.wait_ge(raw_in[n % 2], 16 * (n // 2 + 1))
                            act.activation(pieces[n][1], raw_of(n), ACT.Copy).then_inc(sp_hi, 1)

                        split(0)
                        split(1)
                        for u in range(NU + 3):
                            if 2 <= u < NU + 2:
                                w = u - 2
                                nk = keys(units[w][0])[1]
                                act.wait_ge(tr_done, w + 1)
                                if w >= 2:
                                    act.wait_ge(pv_done, w - 1)
                                act.activation(pT_hi[:, w % 2, 0:nk], ps_t[:, 0:nk], ACT.Copy).then_inc(p_hi_done, 1)
                            if u < NU:
                                nk = keys(units[u][0])[1]
                                act.wait_ge(neg_done, u + 1)
                                if u >= 4:
                                    act.wait_ge(rec_done, u - 3)
                                act.activation(prob[:, u % 3, 0:nk], prob[:, u % 3, 0:nk], ACT.Exp, bias=neg[:, u % 2:u % 2 + 1],
                                               accum_out=rsum[:, u % 4:u % 4 + 1]).then_inc(exp_done, 1)
                            for n in range(2 * u + 2, min(2 * u + 4, len(pieces))):
                                split(n)
                            if u >= 4 and u % 2 == 0:
                                pair = (u - 4) // 2
                                act.wait_ge(pv_done, 2 * pair + 2)
                                for half in range(2):
                                    act.activation(aT_cols(aT_hi, pair, half), out_cols(pair, half), ACT.Copy).then_inc(y_hi_done, 1)

                    @block.vector
                    def _(dve):
                        def split(n):
                            dve.wait_ge(sp_hi, n + 1)
                            dve.tensor_tensor(pieces[n][2], raw_of(n), pieces[n][1], ALU.subtract).then_inc(sp_lo, 1)

                        split(0)
                        split(1)
                        dve.wait_ge(masked, 2)
                        for u in range(NU + 3):
                            if u < NU:
                                n, hd = units[u]
                                _, nk, parts = keys(n)
                                dve.wait_ge(s_done, u + 1)
                                if u >= 3:
                                    dve.wait_ge(tr_done, u - 2)
                                src = ps_s[u % 2][:].rearrange("p (a n) -> p a n", a=2)[:, 0:parts, 0:nk // parts]
                                dst = prob[:, u % 3, 0:nk].rearrange("p (a n) -> p a n", a=parts)
                                dve.tensor_tensor_reduce(out=dst, in0=src, in1=backwards(bias[:, hd, 0:nk], parts),
                                                         scale=1.0, scalar=LOWEST, op0=ALU.add, op1=ALU.max,
                                                         accum_out=top_s[:, u % 2:u % 2 + 1]).then_inc(max_done, 1)
                                dve.wait_ge(max_done, u + 1)
                                dve.tensor_scalar(neg[:, u % 2:u % 2 + 1], top_s[:, u % 2:u % 2 + 1], -1.0, None, ALU.mult).then_inc(neg_done, 1)
                            for n in range(2 * u + 2, min(2 * u + 4, QK)):
                                split(n)
                            if 1 <= u < NU + 1:
                                w = u - 1
                                nk = keys(units[w][0])[1]
                                dve.wait_ge(exp_done, w + 1)
                                dve.reciprocal(rinv[:, w % 2:w % 2 + 1], rsum[:, w % 4:w % 4 + 1]).then_inc(rec_done, 1)
                                dve.wait_ge(rec_done, w + 1)
                                dve.tensor_scalar(prob[:, w % 3, 0:nk], prob[:, w % 3, 0:nk], rinv[:, w % 2:w % 2 + 1], None,
                                                  ALU.mult).then_inc(norm_done, 1)
                            if 2 <= u < NU + 2:
                                w = u - 2
                                nk = keys(units[w][0])[1]
                                dve.wait_ge(p_hi_done, w + 1)
                                dve.tensor_tensor(pT_lo[:, w % 2, 0:nk], ps_t[:, 0:nk], pT_hi[:, w % 2, 0:nk], ALU.subtract).then_inc(p_lo_done, 1)
                            if u >= 4 and u % 2 == 0:
                                pair = (u - 4) // 2
                                dve.wait_ge(y_hi_done, 2 * pair + 2)
                                for half in range(2):
                                    dve.tensor_tensor(aT_cols(aT_lo, pair, half), out_cols(pair, half), aT_cols(aT_hi, pair, half),
                                                      ALU.subtract).then_inc(y_lo_done, 1)

                    @block.tensor
                    def _(pe):
                        def scores(u):
                            n, hd = units[u]
                            k0, nk, parts = keys(n)
                            if n == 0 and hd % 2 == 0:
                                pe.wait_ge(sp_lo, 2 * (hd // 2) + 2)
                            if u >= 2:
                                pe.wait_ge(max_done, u - 1)
                            rows, f, tok = slice((hd % 2) * B_HD, (hd % 2 + 1) * B_HD), hd // 2, slice(n * P, (n + 1) * P)
                            w = nk // parts
                            for c in range(parts):
                                last = three(pe, ps_s[u % 2][:, c * HALF:c * HALF + w], q_hi[rows, f, tok], q_lo[rows, f, tok],
                                             k_hi[rows, f, k0 + c * w:k0 + (c + 1) * w], k_lo[rows, f, k0 + c * w:k0 + (c + 1) * w],
                                             True, True)
                            last.then_inc(s_done, 1)

                        def transposes(u):
                            nk = keys(units[u][0])[1]
                            pe.wait_ge(norm_done, u + 1)
                            if u >= 1:
                                pe.wait_ge(p_lo_done, u)
                            for c in range(0, nk, P):
                                last = pe.transpose(ps_t[:, c:c + P], prob[:, u % 3, c:c + P], ident[:])
                            last.then_inc(tr_done, 1)

                        def values(u):
                            n, hd = units[u]
                            k0, nk, _ = keys(n)
                            pair = u // 2
                            pe.wait_ge(p_lo_done, u + 1)
                            if pair >= 2:
                                pe.wait_ge(y_lo_done, 2 * pair - 2)
                            if hd == 0:
                                pe.wait_ge(sp_lo_v, n // 2 + 1)
                            col = slice(hd * B_HD, (hd + 1) * B_HD)
                            for c in range(0, nk, P):
                                kt = (k0 + c) // P
                                last = three(pe, out_cols(pair, hd % 2), v_hi[:, kt, col], v_lo[:, kt, col],
                                             pT_hi[:, u % 2, c:c + P], pT_lo[:, u % 2, c:c + P], c == 0, c + P == nk)
                            last.then_inc(pv_done, 1)

                        for u in range(NU + 3):
                            if u < NU:
                                scores(u)
                            if 2 <= u < NU + 2:
                                transposes(u - 2)
                            if u >= 3:
                                values(u - 3)

        def memory_stage(mk_hi, mk_lo, mv_hi, mv_lo):
            mem_in, mt_tr, mt_hi, mt_lo = sem("me_in"), sem("me_tr"), sem("me_thi"), sem("me_tlo")
            raw_in = [sem(f"me_raw_in{i}") for i in range(4)]
            hi_done, lo_done, mm_done, out_hi, out_lo = sem("me_hi"), sem("me_lo"), sem("me_mm"), sem("me_out_hi"), sem("me_out_lo")
            PIECES = 4
            weights = [(w_xk, 0), (w_xk, 1), (w_xv, 0), (w_xv, 1)]
            units = [(b, i) for b in range(4) for i in range(4 if b < 2 else MT)]
            ends = [4, 8, 8 + MT, 8 + 2 * MT]
            with ExitStack() as stage:
                sb, pb = local(stage)
                mraw = sb("me_mraw", [P, MT, D])
                mT_hi, mT_lo = sb("me_mT_hi", [P, KT, MEM], F32R), sb("me_mT_lo", [P, KT, MEM], F32R)
                raw = sb("me_raw", [P, 4, 2, HALF])
                w_hi, w_lo = sb("me_whi", [P, 2, KT, HALF], F32R), sb("me_wlo", [P, 2, KT, HALF], F32R)
                ps_t = pb("me_ps_t", MT * D)
                ps = [pb(f"me_ps{i}", HALF) for i in range(4)]

                def target(u, mk, mv):
                    b, i = units[u]
                    if b < 2:
                        return mk[:, b * 4 + i, :], ps[u % 4][:, 0:MEM]
                    return mv[:, i, (b - 2) * HALF:(b - 1) * HALF], ps[u % 4][:]

                with nc.Block() as block:
                    @block.sync
                    def _(sp):
                        sp.dma_start(mraw[:], mem.rearrange("(a p) d -> p a d", p=P)).then_inc(mem_in, 16)
                        for n in range(4 * PIECES):
                            b, q = divmod(n, PIECES)
                            w, c = weights[b]
                            if n >= 4:
                                sp.wait_ge(lo_done, n - 3)
                            src = w[2 * q * P:2 * (q + 1) * P, c * HALF:(c + 1) * HALF].rearrange("(a p) n -> p a n", p=P)
                            sp.dma_start(raw[:, n % 4, :, :], src).then_inc(raw_in[n % 4], 16)

                    @block.gpsimd
                    def _(pool):
                        for n in range(4 * PIECES):
                            b, q = divmod(n, PIECES)
                            pool.wait_ge(hi_done, n + 1)
                            pool.tensor_tensor(w_lo[:, b % 2, 2 * q:2 * q + 2, :], raw[:, n % 4, :, :],
                                               w_hi[:, b % 2, 2 * q:2 * q + 2, :], ALU.subtract).then_inc(lo_done, 1)

                    @block.scalar
                    def _(act):
                        act.wait_ge(mt_tr, 1)
                        for a in range(MT):
                            act.activation(mT_hi[:, :, a * P:(a + 1) * P], ps_t[:, a * D:(a + 1) * D].rearrange("p (k m) -> p k m", k=KT),
                                           ACT.Copy).then_inc(mt_hi, 1)
                        n = 0
                        for u, (b, i) in enumerate(units):
                            while n < min(4 * PIECES, (b + 2) * PIECES):
                                nb, q = divmod(n, PIECES)
                                act.wait_ge(raw_in[n % 4], 16 * (n // 4 + 1))
                                if nb >= 2:
                                    act.wait_ge(mm_done, ends[nb - 2])
                                act.activation(w_hi[:, nb % 2, 2 * q:2 * q + 2, :], raw[:, n % 4, :, :], ACT.Copy).then_inc(hi_done, 1)
                                n += 1
                            act.wait_ge(mm_done, u + 1)
                            to, src = target(u, mk_hi, mv_hi)
                            act.activation(to, src, ACT.Copy).then_inc(out_hi, 1)

                    @block.vector
                    def _(dve):
                        for a in range(MT):
                            dve.wait_ge(mt_hi, a + 1)
                            dve.tensor_tensor(mT_lo[:, :, a * P:(a + 1) * P], ps_t[:, a * D:(a + 1) * D].rearrange("p (k m) -> p k m", k=KT),
                                              mT_hi[:, :, a * P:(a + 1) * P], ALU.subtract).then_inc(mt_lo, 1)
                        for u in range(len(units)):
                            dve.wait_ge(out_hi, u + 1)
                            hi, src = target(u, mk_hi, mv_hi)
                            lo, _ = target(u, mk_lo, mv_lo)
                            dve.tensor_tensor(lo, src, hi, ALU.subtract).then_inc(out_lo, 1)

                    @block.tensor
                    def _(pe):
                        pe.wait_ge(mem_in, 16)
                        for a in range(MT):
                            for k in range(KT):
                                last = pe.transpose(ps_t[:, a * D + k * P:a * D + (k + 1) * P], mraw[:, a, k * P:(k + 1) * P], ident[:])
                        last.then_inc(mt_tr, 1)
                        pe.wait_ge(mt_lo, MT)
                        for u, (b, i) in enumerate(units):
                            if u >= 4:
                                pe.wait_ge(out_lo, u - 3)
                            for k in range(KT):
                                if i == 0 and k % 2 == 0:
                                    pe.wait_ge(lo_done, b * PIECES + k // 2 + 1)
                                at = slice(i * P, (i + 1) * P)
                                if b < 2:
                                    last = three(pe, ps[u % 4][:, 0:MEM], w_hi[:, b % 2, k, at], w_lo[:, b % 2, k, at],
                                                 mT_hi[:, k, :], mT_lo[:, k, :], k == 0, k == KT - 1)
                                else:
                                    last = three(pe, ps[u % 4][:], mT_hi[:, k, at], mT_lo[:, k, at],
                                                 w_hi[:, b % 2, k, :], w_lo[:, b % 2, k, :], k == 0, k == KT - 1)
                            last.then_inc(mm_done, 1)

        def cross_stage(mk_hi, mk_lo, mv_hi, mv_lo):
            q_in = [sem(f"xa_q_in{i}") for i in range(2)]
            q_hi_done, q_lo_done, s_done = sem("xa_q_hi"), sem("xa_q_lo"), sem("xa_s")
            max_done, neg_done, exp_done = sem("xa_max"), sem("xa_neg"), sem("xa_exp")
            tr_done, p_hi_done, p_lo_done, pv_done = sem("xa_tr"), sem("xa_p_hi"), sem("xa_p_lo"), sem("xa_pv")
            rec_done, o_done, ot_done, o_hi_done, o_lo_done = sem("xa_rec"), sem("xa_o"), sem("xa_ot"), sem("xa_o_hi"), sem("xa_o_lo")
            SCALE = float(X_HD) ** -0.5
            HC = X_HD // P
            with ExitStack() as stage:
                sb, pb = local(stage)
                q_raw = sb("xa_q_raw", [P, 2, KT, P])
                q_hi, q_lo = sb("xa_q_hi_sb", [P, 2, KT, P], F32R), sb("xa_q_lo_sb", [P, 2, KT, P], F32R)
                prob = sb("xa_prob", [P, 2, X_HEADS, MEM])
                pT_hi, pT_lo = sb("xa_pT_hi", [P, 2, X_HEADS * MT, P], F32R), sb("xa_pT_lo", [P, 2, X_HEADS * MT, P], F32R)
                topm, neg = sb("xa_top", [P, 2, X_HEADS]), sb("xa_neg_sb", [P, 2, X_HEADS])
                rsum, rinv = sb("xa_rsum", [P, 2, X_HEADS]), sb("xa_rinv", [P, 2, X_HEADS])
                o_sb = sb("xa_o_sb", [P, 2, X_HEADS, X_HD])
                ps_s, ps_t, ps_o, ps_ot = pb("xa_ps_s", D), pb("xa_ps_t", D), pb("xa_ps_o", D), pb("xa_ps_ot", D)

                with nc.Block() as block:
                    @block.sync
                    def _(sp):
                        for j in range(TT):
                            if j >= 2:
                                sp.wait_ge(q_lo_done, j - 1)
                            sp.dma_start(q_raw[:, j % 2, :, :], xq_d[:, j * P:(j + 1) * P].rearrange("(k p) t -> p k t", p=P)).then_inc(q_in[j % 2], 16)

                    @block.scalar
                    def _(act):
                        def query_hi(j):
                            act.wait_ge(q_in[j % 2], 16 * (j // 2 + 1))
                            if j >= 2:
                                act.wait_ge(s_done, j - 1)
                            act.activation(q_hi[:, j % 2, :, :], q_raw[:, j % 2, :, :], ACT.Copy).then_inc(q_hi_done, 1)

                        def prob_hi(j):
                            act.wait_ge(tr_done, j + 1)
                            if j >= 2:
                                act.wait_ge(pv_done, j - 1)
                            act.activation(pT_hi[:, j % 2, :, :], ps_t[:].rearrange("p (k t) -> p k t", t=P), ACT.Copy).then_inc(p_hi_done, 1)

                        def out_hi(j):
                            act.wait_ge(ot_done, j + 1)
                            act.activation(aT_hi[:, :, j * P:(j + 1) * P], ps_ot[:].rearrange("p (k t) -> p k t", t=P), ACT.Copy).then_inc(o_hi_done, 1)

                        query_hi(0)
                        query_hi(1)
                        for j in range(TT):
                            act.wait_ge(neg_done, j + 1)
                            if j >= 2:
                                act.wait_ge(tr_done, j - 1)
                                act.wait_ge(rec_done, j - 1)
                            for hd in range(X_HEADS):
                                act.activation(prob[:, j % 2, hd, :], ps_s[:, hd * MEM:(hd + 1) * MEM], ACT.Exp, scale=SCALE,
                                               bias=neg[:, j % 2, hd:hd + 1], accum_out=rsum[:, j % 2, hd:hd + 1]).then_inc(exp_done, 1)
                            prob_hi(j)
                            if j + 2 < TT:
                                query_hi(j + 2)
                            if j >= 1:
                                out_hi(j - 1)
                        out_hi(TT - 1)

                    @block.vector
                    def _(dve):
                        def query_lo(j):
                            dve.wait_ge(q_hi_done, j + 1)
                            dve.tensor_tensor(q_lo[:, j % 2, :, :], q_raw[:, j % 2, :, :], q_hi[:, j % 2, :, :], ALU.subtract).then_inc(q_lo_done, 1)

                        def out_lo(j):
                            dve.wait_ge(o_hi_done, j + 1)
                            dve.tensor_tensor(aT_lo[:, :, j * P:(j + 1) * P], ps_ot[:].rearrange("p (k t) -> p k t", t=P),
                                              aT_hi[:, :, j * P:(j + 1) * P], ALU.subtract).then_inc(o_lo_done, 1)

                        def top(j):
                            dve.wait_ge(s_done, j + 1)
                            dve.tensor_reduce(topm[:, j % 2, :], ps_s[:].rearrange("p (h m) -> p h m", h=X_HEADS), AX.X, ALU.max).then_inc(max_done, 1)
                            dve.wait_ge(max_done, j + 1)
                            dve.tensor_scalar(neg[:, j % 2, :], topm[:, j % 2, :], -SCALE, None, ALU.mult).then_inc(neg_done, 1)

                        query_lo(0)
                        query_lo(1)
                        top(0)
                        for j in range(TT):
                            i = j % 2
                            dve.wait_ge(p_hi_done, j + 1)
                            dve.tensor_tensor(pT_lo[:, i, :, :], ps_t[:].rearrange("p (k t) -> p k t", t=P), pT_hi[:, i, :, :], ALU.subtract).then_inc(p_lo_done, 1)
                            if j + 1 < TT:
                                top(j + 1)
                            if j + 2 < TT:
                                query_lo(j + 2)
                            if j >= 1:
                                out_lo(j - 1)
                            dve.reciprocal(rinv[:, i, :], rsum[:, i, :]).then_inc(rec_done, 1)
                            dve.wait_ge(rec_done, j + 1)
                            dve.wait_ge(pv_done, j + 1)
                            dve.tensor_tensor(o_sb[:, i, :, :], ps_o[:].rearrange("p (h d) -> p h d", h=X_HEADS),
                                              rinv[:, i, :].unsqueeze(2).broadcast_to([P, X_HEADS, X_HD]), ALU.mult).then_inc(o_done, 1)
                        out_lo(TT - 1)

                    @block.tensor
                    def _(pe):
                        def scores(j):
                            pe.wait_ge(q_lo_done, j + 1)
                            if j >= 1:
                                pe.wait_ge(exp_done, X_HEADS * j)
                            for hd in range(X_HEADS):
                                for c in range(HC):
                                    f = hd * HC + c
                                    last = three(pe, ps_s[:, hd * MEM:(hd + 1) * MEM], q_hi[:, j % 2, f, :], q_lo[:, j % 2, f, :],
                                                 mk_hi[:, f, :], mk_lo[:, f, :], c == 0, c == HC - 1)
                            last.then_inc(s_done, 1)

                        def out_transposes(j):
                            pe.wait_ge(o_done, j + 1)
                            if j >= 1:
                                pe.wait_ge(o_lo_done, j)
                            o = o_sb[:, j % 2, :, :].rearrange("p h d -> p (h d)")
                            for k in range(KT):
                                last = pe.transpose(ps_ot[:, k * P:(k + 1) * P], o[:, k * P:(k + 1) * P], ident[:])
                            last.then_inc(ot_done, 1)

                        scores(0)
                        for j in range(TT):
                            pe.wait_ge(exp_done, X_HEADS * (j + 1))
                            if j >= 1:
                                pe.wait_ge(p_lo_done, j)
                            for hd in range(X_HEADS):
                                for c in range(MT):
                                    at = (hd * MT + c) * P
                                    last = pe.transpose(ps_t[:, at:at + P], prob[:, j % 2, hd, c * P:(c + 1) * P], ident[:])
                            last.then_inc(tr_done, 1)
                            if j + 1 < TT:
                                scores(j + 1)
                            if j >= 1:
                                out_transposes(j - 1)
                            pe.wait_ge(p_lo_done, j + 1)
                            if j >= 1:
                                pe.wait_ge(o_done, j)
                            for hd in range(X_HEADS):
                                for c in range(MT):
                                    last = three(pe, ps_o[:, hd * X_HD:(hd + 1) * X_HD], pT_hi[:, j % 2, hd * MT + c, :], pT_lo[:, j % 2, hd * MT + c, :],
                                                 mv_hi[:, c, hd * X_HD:(hd + 1) * X_HD], mv_lo[:, c, hd * X_HD:(hd + 1) * X_HD], c == 0, c == MT - 1)
                            last.then_inc(pv_done, 1)
                        out_transposes(TT - 1)

        def key_score_stage():
            sk_in, sk_tr, sk_hi, sk_lo = sem("ks_sk_in"), sem("ks_sk_tr"), sem("ks_sk_hi"), sem("ks_sk_lo")
            raw_in = [sem(f"ks_raw_in{i}") for i in range(4)]
            hi_done = sem("ks_hi")
            lo_done = [sem(f"ks_lo{i}") for i in range(2)]
            q_done, q_hi_done, q_lo_done = sem("ks_q"), sem("ks_q_hi"), sem("ks_q_lo")
            s_done, s_out = sem("ks_s"), sem("ks_s_out")
            stored = [sem(f"ks_stored{i}") for i in range(2)]
            HP, PIECES, NB = 2 * PH, 4, 4
            s_view = s_d.rearrange("(j h) t (q k) -> h q t j k", h=PH, q=2)
            with ExitStack() as stage:
                sb, pb = local(stage)
                sraw = sb("ks_sraw", [P, HP, P])
                sk_hi_sb, sk_lo_sb = sb("ks_skT_hi", [P, HP, P], F32R), sb("ks_skT_lo", [P, HP, P], F32R)
                raw = sb("ks_raw", [P, 4, 2, HALF])
                w_hi, w_lo = sb("ks_whi", [P, 2, KT, HALF], F32R), sb("ks_wlo", [P, 2, KT, HALF], F32R)
                q_hi, q_lo = sb("ks_qhi", [P, 2, T], F32R), sb("ks_qlo", [P, 2, T], F32R)
                res = sb("ks_res", [P, 2, TT, KEYS])
                ps_q = [pb(f"ks_ps_q{i}", HALF) for i in range(4)]
                ps_s = [pb(f"ks_ps_s{i}", D) for i in range(2)]
                with nc.Block() as block:
                    @block.sync
                    def _(sp):
                        def load(n):
                            b, q = divmod(n, PIECES)
                            if n >= 4:
                                sp.wait_ge(lo_done[n % 2], n // 2 - 1)
                            src = w_pq[2 * q * P:2 * (q + 1) * P, b * HALF:(b + 1) * HALF].rearrange("(a p) n -> p a n", p=P)
                            sp.dma_start(raw[:, n % 4, :, :], src).then_inc(raw_in[n % 4], 16)

                        for n in range(PIECES):
                            load(n)
                        sp.dma_start(sraw[:], sub_keys.rearrange("h q k d -> k (h q) d")).then_inc(sk_in, 16)
                        for hp in range(HP + 1):
                            if hp // 4 + 1 < NB:
                                load(PIECES + hp)
                            if hp >= 1:
                                sp.wait_ge(s_out, hp)
                                sp.dma_start(s_view[(hp - 1) // 2, (hp - 1) % 2], res[:, (hp - 1) % 2, :, :]).then_inc(stored[(hp - 1) % 2], 16)
                        for i in range(2):
                            sp.wait_ge(stored[i], 16 * (HP // 2))

                    @block.gpsimd
                    def _(pool):
                        for n in range(0, NB * PIECES, 2):
                            b, q = divmod(n, PIECES)
                            pool.wait_ge(hi_done, n + 1)
                            pool.tensor_tensor(w_lo[:, b % 2, 2 * q:2 * q + 2, :], raw[:, n % 4, :, :],
                                               w_hi[:, b % 2, 2 * q:2 * q + 2, :], ALU.subtract).then_inc(lo_done[0], 1)

                    @block.scalar
                    def _(act):
                        def split(n):
                            b, q = divmod(n, PIECES)
                            act.wait_ge(raw_in[n % 4], 16 * (n // 4 + 1))
                            if b >= 2:
                                act.wait_ge(q_done, 8 * (b - 1))
                            act.activation(w_hi[:, b % 2, 2 * q:2 * q + 2, :], raw[:, n % 4, :, :], ACT.Copy).then_inc(hi_done, 1)

                        for n in range(PIECES):
                            split(n)
                        for c in range(2):
                            act.wait_ge(sk_tr, c + 1)
                            act.activation(sk_hi_sb[:, 8 * c:8 * c + 8, :], ps_s[c][:].rearrange("p (k t) -> p k t", t=P), ACT.Copy).then_inc(sk_hi, 1)
                        for hp in range(HP):
                            if hp // 4 + 1 < NB:
                                split(PIECES + hp)
                            for th in range(2):
                                act.wait_ge(q_done, 2 * hp + th + 1)
                                if hp >= 2:
                                    act.wait_ge(s_done, hp - 1)
                                act.activation(q_hi[:, hp % 2, th * HALF:(th + 1) * HALF], ps_q[(2 * hp + th) % 4][:], ACT.Copy).then_inc(q_hi_done, 1)

                    @block.vector
                    def _(dve):
                        def split_lo(n):
                            b, q = divmod(n, PIECES)
                            dve.wait_ge(hi_done, n + 1)
                            dve.tensor_tensor(w_lo[:, b % 2, 2 * q:2 * q + 2, :], raw[:, n % 4, :, :],
                                              w_hi[:, b % 2, 2 * q:2 * q + 2, :], ALU.subtract).then_inc(lo_done[1], 1)

                        split_lo(1)
                        split_lo(3)
                        for c in range(2):
                            dve.wait_ge(sk_hi, c + 1)
                            dve.tensor_tensor(sk_lo_sb[:, 8 * c:8 * c + 8, :], ps_s[c][:].rearrange("p (k t) -> p k t", t=P),
                                              sk_hi_sb[:, 8 * c:8 * c + 8, :], ALU.subtract).then_inc(sk_lo, 1)

                        def scores_out(hp):
                            dve.wait_ge(s_done, hp + 1)
                            if hp >= 2:
                                dve.wait_ge(stored[hp % 2], 16 * (hp // 2))
                            dve.tensor_copy(res[:, hp % 2, :, :], ps_s[hp % 2][:].rearrange("p (k t) -> p k t", t=P)).then_inc(s_out, 1)

                        for hp in range(HP):
                            if hp % 2 == 1 and hp // 4 + 1 < NB:
                                split_lo(PIECES + hp)
                            for th in range(2):
                                dve.wait_ge(q_hi_done, 2 * hp + th + 1)
                                dve.tensor_tensor(q_lo[:, hp % 2, th * HALF:(th + 1) * HALF], ps_q[(2 * hp + th) % 4][:],
                                                  q_hi[:, hp % 2, th * HALF:(th + 1) * HALF], ALU.subtract).then_inc(q_lo_done, 1)
                            if hp >= 1:
                                scores_out(hp - 1)
                        scores_out(HP - 1)

                    @block.tensor
                    def _(pe):
                        pe.wait_ge(sk_in, 16)
                        for hp in range(HP):
                            last = pe.transpose(ps_s[hp // 8][:, (hp % 8) * P:(hp % 8 + 1) * P], sraw[:, hp, :], ident[:])
                            if hp % 8 == 7:
                                last.then_inc(sk_tr, 1)

                        def scores(hp):
                            pe.wait_ge(q_lo_done, 2 * hp + 2)
                            if hp < 2:
                                pe.wait_ge(sk_lo, 2)
                            else:
                                pe.wait_ge(s_out, hp - 1)
                            for j in range(TT):
                                tok = slice(j * P, (j + 1) * P)
                                last = three(pe, ps_s[hp % 2][:, tok], q_hi[:, hp % 2, tok], q_lo[:, hp % 2, tok],
                                             sk_hi_sb[:, hp, :], sk_lo_sb[:, hp, :], True, True)
                            last.then_inc(s_done, 1)

                        for hp in range(HP):
                            b, f = divmod(hp, 4)
                            for th in range(2):
                                u = 2 * hp + th
                                if u >= 4:
                                    pe.wait_ge(q_lo_done, u - 3)
                                for k in range(KT):
                                    if f == 0 and th == 0 and k % 2 == 0:
                                        pe.wait_ge(lo_done[k // 2 % 2], (b * PIECES + k // 2) // 2 + 1)
                                    col, tok = slice(f * P, (f + 1) * P), slice(th * HALF, (th + 1) * HALF)
                                    last = three(pe, ps_q[u % 4][:], w_hi[:, b % 2, k, col], w_lo[:, b % 2, k, col],
                                                 aT_hi[:, k, tok], aT_lo[:, k, tok], k == 0, k == KT - 1)
                                last.then_inc(q_done, 1)
                            if hp >= 1:
                                scores(hp - 1)
                        scores(HP - 1)

        def expert_in_stage():
            ROUTE_STEPS, ROUTE_E = 32, 2
            GATE_STEPS, GATE_E = 16, 4
            HALF_E = ROUTE_STEPS * ROUTE_E
            ETILES = HALF_E + GATE_STEPS * GATE_E
            u_rows = expert_u.rearrange("(p e) d -> e p d", e=P)

            raw_in = [sem(f"ei_raw_in{i}") for i in range(2)]
            tr_done, uT_hi_done, uT_lo_done = sem("ei_tr"), sem("ei_uT_hi"), sem("ei_uT_lo")
            mm_done = sem("ei_mm")
            gelu_done = [sem(f"ei_gelu{i}") for i in range(2)]
            act_stored = [sem(f"ei_act_stored{i}") for i in range(2)]
            iota_done, rank = sem("ei_iota"), sem("ei_rank")
            s_in = [sem(f"ei_s_in{i}") for i in range(2)]
            top_done, exp_done = sem("ei_top"), sem("ei_exp")
            route_done, rt_done, rt_out = sem("ei_route"), sem("ei_rt"), sem("ei_rt_out")
            rt_stored = [sem(f"ei_rt_stored{i}") for i in range(2)]
            col_in = [sem(f"ei_col_in{i}") for i in range(2)]
            hot = sem("ei_hot")
            hot_done = [sem(f"ei_hot_done{i}") for i in range(2)]
            last_done = [sem(f"ei_last_done{i}") for i in range(2)]
            g_done = [[sem(f"ei_g_done{i}{g}") for g in range(2)] for i in range(2)]
            g_out = [sem(f"ei_g_out{i}") for i in range(2)]
            g_stored = [sem(f"ei_g_stored{i}") for i in range(2)]
            BATCH, GROUP = 8, 4
            BATCHES = GBLK // BATCH

            def route_step(it, s):
                return it * ROUTE_E + s, s, it, s

            def gate_step(it, s):
                return it * GATE_E + (HALF_E + s), s % 2, it * (GATE_E // 2) + (HALF_E // 2 + s // 2), s

            with ExitStack() as stage:
                sb, pb = local(stage)
                u_raw = sb("ei_u_raw", [P, 2, D])
                uT_hi, uT_lo = sb("ei_uT_hi_sb", [P, 2, KT, P], F32R), sb("ei_uT_lo_sb", [P, 2, KT, P], F32R)
                act_sb = sb("ei_act", [P, 2, T])
                iota = sb("ei_iota_sb", [P, P])
                s_sb = sb("ei_s", [P, 2, 2, KEYS])
                s_left = sb("ei_s_left", [P, 2, KEYS])
                kv = sb("ei_kv", [P, 2, TOPK])
                ki = sb("ei_ki", [P, 2, TOPK], U32)
                kf = sb("ei_kf", [P, 2, TOPK])
                pair, pair_left = sb("ei_pair", [P, TOPK, TOPK]), sb("ei_pair_left", [P, TOPK, TOPK])
                gv, gi = sb("ei_gv", [P, 2, TOPK]), sb("ei_gi", [P, TOPK], U32)
                gpos, gpf = sb("ei_gpos", [P, 2, TOPK], U32), sb("ei_gpf", [P, 2, TOPK])
                pick = sb("ei_pick", [P, 2, TOPK, TOPK])
                gneg, gexp = sb("ei_gneg", [P, 2]), sb("ei_gexp", [P, 2, TOPK])
                gsum, ginv = sb("ei_gsum", [P, 2]), sb("ei_ginv", [P, 2])
                route = sb("ei_route_sb", [P, 2, TOPK, 3])
                routeT = sb("ei_routeT", [3 * TOPK, 2, P])
                col = sb("ei_col", [P, 2, 3, GBLK])
                w_rest = sb("ei_w_rest", [P, 2, GBLK])
                w_part = [sb(f"ei_w_part{c}", [P, 2, GBLK], BF16) for c in range(3)]
                hot1, hot2 = sb("ei_hot1", [P, 2, BATCH, P], BF16), sb("ei_hot2", [P, 2, BATCH, P], BF16)
                hw = [sb(f"ei_hw{c}", [P, 2, BATCH, P], BF16) for c in range(3)]
                gate_sb = sb("ei_gate", [P, 2, P, GBLK])
                ps_t = pb("ei_ps_t", D)
                ps_h = [pb(f"ei_ps_h{i}", T) for i in range(2)]
                ps_x = [pb(f"ei_ps_x{i}", HALF) for i in range(2)]
                route_cols = route_d.rearrange("(j h) (k q) t -> j (h k) q t", h=PH, q=3)
                RANKS = 24
                HOTS = 4 + 3 * BATCHES

                with nc.Block() as block:
                    @block.sync
                    def _(sp):
                        def load_expert(step):
                            e, i, _, _ = step
                            sp.wait_ge(tr_done, e + 1)
                            sp.dma_start(u_raw[:, i, :], u_rows[e + 2, :, :]).then_inc(raw_in[i], 16)

                        def store_act(step):
                            e, i, n, _ = step
                            sp.wait_ge(gelu_done[i], n + 1)
                            sp.dma_start(act_d[e, :, :], act_sb[:, i, :]).then_inc(act_stored[i], 16)

                        def load_scores(u, i):
                            sp.dma_start(s_sb[:, i, :, :], s_d[u].rearrange("t (q k) -> t q k", q=2)).then_inc(s_in[i], 16)

                        def store_route(u, i):
                            sp.wait_ge(rt_out, u + 1)
                            sp.dma_start(route_d[u, :, :], routeT[:, i, :]).then_inc(rt_stored[i], 16)

                        def load_col(tile, off, b):
                            src = route_cols[tile][:, :, bass.ds(off, GBLK)]
                            sp.dma_start(col[:, b, :, :], src).then_inc(col_in[b], 16)

                        def store_gate(it, b):
                            sp.wait_ge(g_out[1], (it * 2 + (b + 1)) * BATCHES)
                            sp.dma_start(gate_d[it * 2 + b], gate_sb[:, b, :, :]).then_inc(g_stored[b], 16)

                        for i in range(2):
                            sp.dma_start(u_raw[:, i, :], u_rows[i, :, :]).then_inc(raw_in[i], 16)
                            load_scores(i, i)

                        def route_body(it, more):
                            for s in range(ROUTE_E):
                                step = route_step(it, s)
                                load_expert(step)
                                if more:
                                    sp.wait_ge(rank, (step[0] + 1) * RANKS)
                                    load_scores(step[0] + 2, s)
                                store_route(step[0], s)
                                store_act(step)

                        with sp.Fori(0, ROUTE_STEPS - 1) as it:
                            route_body(it, True)
                        route_body(ROUTE_STEPS - 1, False)
                        for i in range(2):
                            sp.wait_ge(rt_stored[i], 16 * (UNITS // 2))
                        load_col(0, 0, 0)
                        load_col(0, GBLK, 1)

                        def gate_body(it, more):
                            for s in range(GATE_E):
                                step = gate_step(it, s)
                                if more or s < GATE_E - 2:
                                    load_expert(step)
                                if s % 2 == 1:
                                    store_gate(it, s // 2)
                                    if more:
                                        load_col((it + 1) // 2, ((it + 1) % 2) * (2 * GBLK) + s // 2 * GBLK, s // 2)
                                store_act(step)

                        with sp.Fori(0, GATE_STEPS - 1) as it:
                            gate_body(it, True)
                        gate_body(GATE_STEPS - 1, False)
                        for i in range(2):
                            sp.wait_ge(act_stored[i], 16 * (ETILES // 2))
                            sp.wait_ge(g_stored[i], 16 * GATE_STEPS)

                    @block.gpsimd
                    def _(pool):
                        pool.iota(iota[:], [[1, P]], base=0, channel_multiplier=0,
                                  allow_small_or_imprecise_dtypes=True).then_inc(iota_done, 1)

                        def last_parts(it):
                            for b in range(2):
                                for m in range(BATCHES):
                                    i, t0 = m % 2, m * BATCH
                                    part = w_part[2][:, b, t0:t0 + BATCH].unsqueeze(2).broadcast_to([P, BATCH, P])
                                    pool.wait_ge(hot, it * (2 * HOTS) + (b * HOTS + 4 + 3 * m + 1))
                                    pool.wait_ge(g_done[i][1], it * BATCHES + (b * (BATCHES // 2) + m // 2))
                                    pool.tensor_tensor(hw[2][:, i, :, :], hot2[:, i, :, :], part, ALU.mult).then_inc(last_done[i], 1)

                        last_parts(0)
                        with pool.Fori(1, GATE_STEPS) as it:
                            last_parts(it)

                    @block.scalar
                    def _(act):
                        def next_hi(step):
                            e, i, _, _ = step
                            act.wait_ge(tr_done, e + 2)
                            act.wait_ge(mm_done, e)
                            act.activation(uT_hi[:, 1 - i, :, :], ps_t[:].rearrange("p (k t) -> p k t", t=P), ACT.Copy).then_inc(uT_hi_done, 1)

                        def gelu(step):
                            e, i, n, _ = step
                            act.wait_ge(mm_done, e + 1)
                            act.wait_ge(act_stored[i], n * 16)
                            act.activation(act_sb[:, i, :], ps_h[i][:], ACT.Gelu).then_inc(gelu_done[i], 1)

                        act.wait_ge(tr_done, 1)
                        act.activation(uT_hi[:, 0, :, :], ps_t[:].rearrange("p (k t) -> p k t", t=P), ACT.Copy).then_inc(uT_hi_done, 1)

                        def route_body(it):
                            for s in range(ROUTE_E):
                                step = route_step(it, s)
                                u, i, n, _ = step
                                next_hi(step)
                                act.wait_ge(top_done, u + 1)
                                act.activation(gexp[:, i, :], gv[:, i, :], ACT.Exp, bias=gneg[:, i:i + 1],
                                               accum_out=gsum[:, i:i + 1]).then_inc(exp_done, 1)
                                gelu(step)
                                act.wait_ge(rt_done, u + 1)
                                act.wait_ge(rt_stored[i], n * 16)
                                act.activation(routeT[:, i, :], ps_x[i][0:3 * TOPK, 0:P], ACT.Copy).then_inc(rt_out, 1)

                        route_body(0)
                        with act.Fori(1, ROUTE_STEPS) as it:
                            route_body(it)

                        def gates_out(it, s, m, gh):
                            b = s // 2
                            act.wait_ge(g_done[m % 2][gh], it * BATCHES + (b * (BATCHES // 2) + m // 2 + 1))
                            if m == 0 and gh == 0:
                                act.wait_ge(g_stored[b], it * 16)
                            t0 = m * BATCH + gh * GROUP
                            act.activation(gate_sb[:, b, :, t0:t0 + GROUP].rearrange("p i t -> p t i"),
                                           ps_x[gh][:].rearrange("p (t i) -> p t i", i=P), ACT.Copy).then_inc(g_out[gh], 1)

                        def gate_body(it, more):
                            for s in range(GATE_E):
                                step = gate_step(it, s)
                                if more or s < GATE_E - 1:
                                    next_hi(step)
                                for q in range(4):
                                    gates_out(it, s, 2 * (s % 2) + q // 2, q % 2)
                                gelu(step)

                        gate_body(0, True)
                        with act.Fori(1, GATE_STEPS - 1) as it:
                            gate_body(it, True)
                        gate_body(GATE_STEPS - 1, False)

                    @block.vector
                    def _(dve):
                        def next_lo(step):
                            e, i, _, _ = step
                            dve.wait_ge(uT_hi_done, e + 2)
                            dve.tensor_tensor(uT_lo[:, 1 - i, :, :], ps_t[:].rearrange("p (k t) -> p k t", t=P), uT_hi[:, 1 - i, :, :],
                                              ALU.subtract).then_inc(uT_lo_done, 1)

                        count_reg = dve.alloc_register("ei_count")

                        def wait_apart(signal, count):
                            dve.reg_mov(count_reg, count)
                            dve.wait_ge(iota_done, 1)
                            dve.wait_ge(signal, count_reg)

                        def rank_unit(step):
                            u, i, n, _ = step
                            links = [0]

                            def link(ins, wait=True):
                                links[0] += 1
                                ins.then_inc(rank, 1)
                                if wait:
                                    wait_apart(rank, u * RANKS + links[0])

                            wait_apart(s_in[i], n * 16 + 16)
                            for q in range(2):
                                src = s_sb[:, i, q, :]
                                link(dve.max(kv[:, q, 0:8], src))
                                link(dve.match_replace(out=s_left[:, q, :], in_to_replace=kv[:, q, 0:8], in_values=src, imm_value=LOWEST), False)
                                link(dve.max_index(ki[:, q, 0:8], kv[:, q, 0:8], src))
                                link(dve.max(kv[:, q, 8:16], s_left[:, q, :]))
                                link(dve.max_index(ki[:, q, 8:16], kv[:, q, 8:16], s_left[:, q, :]), q == 1)
                            link(dve.tensor_copy(kf[:], ki[:]), False)
                            link(dve.tensor_tensor(pair[:], kv[:, 0, :].unsqueeze(2).broadcast_to([P, TOPK, TOPK]),
                                                   kv[:, 1, :].unsqueeze(1).broadcast_to([P, TOPK, TOPK]), ALU.add))
                            flat, left = pair[:].rearrange("p a b -> p (a b)"), pair_left[:].rearrange("p a b -> p (a b)")
                            link(dve.max(gv[:, i, 0:8], flat))
                            link(dve.match_replace(out=left, in_to_replace=gv[:, i, 0:8], in_values=flat, imm_value=LOWEST), False)
                            link(dve.max_index(gi[:, 0:8], gv[:, i, 0:8], flat))
                            link(dve.max(gv[:, i, 8:16], left))
                            link(dve.max_index(gi[:, 8:16], gv[:, i, 8:16], left))
                            dve.tensor_scalar(gneg[:, i:i + 1], gv[:, i, 0:1], -1.0, None, ALU.mult).then_inc(top_done, 1)
                            link(dve.tensor_scalar(gpos[:, 0, :], gi[:], 4, None, ALU.logical_shift_right), False)
                            link(dve.tensor_scalar(gpos[:, 1, :], gi[:], TOPK - 1, None, ALU.bitwise_and))
                            link(dve.tensor_copy(gpf[:], gpos[:]))
                            link(dve.tensor_tensor(pick[:], gpf[:].unsqueeze(3).broadcast_to([P, 2, TOPK, TOPK]),
                                                   iota[:, 0:TOPK].unsqueeze(1).unsqueeze(1).broadcast_to([P, 2, TOPK, TOPK]), ALU.is_equal))
                            link(dve.tensor_tensor(pick[:], pick[:], kf[:].unsqueeze(2).broadcast_to([P, 2, TOPK, TOPK]), ALU.mult))
                            dve.wait_ge(rt_done, u - i)
                            link(dve.tensor_reduce(route[:, i, :, 1:3].rearrange("p k q -> p q k"), pick[:], AX.X, ALU.add), False)
                            return link

                        def weigh_unit(step, link):
                            u, i, _, _ = step
                            dve.wait_ge(exp_done, u + 1)
                            link(dve.reciprocal(ginv[:, i:i + 1], gsum[:, i:i + 1]))
                            dve.tensor_scalar(route[:, i, :, 0], gexp[:, i, :], ginv[:, i:i + 1], None, ALU.mult).then_inc(route_done, 1)

                        dve.wait_ge(uT_hi_done, 1)
                        dve.tensor_tensor(uT_lo[:, 0, :, :], ps_t[:].rearrange("p (k t) -> p k t", t=P), uT_hi[:, 0, :, :],
                                          ALU.subtract).then_inc(uT_lo_done, 1)
                        dve.wait_ge(iota_done, 1)
                        def route_body(it):
                            for s in range(ROUTE_E):
                                step = route_step(it, s)
                                link = rank_unit(step)
                                next_lo(step)
                                weigh_unit(step, link)

                        route_body(0)
                        with dve.Fori(1, ROUTE_STEPS) as it:
                            route_body(it)

                        def batch(it, b, m):
                            i, t0 = m % 2, m * BATCH
                            before = it * BATCHES + (b * (BATCHES // 2) + m // 2)
                            base = it * (2 * HOTS) + (b * HOTS + 4 + 3 * m)
                            keys = iota[:].unsqueeze(1).broadcast_to([P, BATCH, P])

                            def per_token(t):
                                return t.unsqueeze(2).broadcast_to([P, BATCH, P])

                            dve.wait_ge(g_done[i][1], before)
                            dve.tensor_tensor(hot2[:, i, :, :], keys, per_token(col[:, b, 2, t0:t0 + BATCH]), ALU.is_equal).then_inc(hot, 1)
                            dve.tensor_tensor(hot1[:, i, :, :], keys, per_token(col[:, b, 1, t0:t0 + BATCH]), ALU.is_equal).then_inc(hot, 1)
                            dve.wait_ge(hot, base + 1)
                            dve.tensor_tensor(hw[0][:, i, :, :], hot2[:, i, :, :], per_token(w_part[0][:, b, t0:t0 + BATCH]), ALU.mult).then_inc(hot, 1)
                            dve.tensor_tensor(hw[1][:, i, :, :], hot2[:, i, :, :], per_token(w_part[1][:, b, t0:t0 + BATCH]), ALU.mult).then_inc(hot_done[i], 1)

                        def gate_body(it, more):
                            for s in range(GATE_E):
                                step = gate_step(it, s)
                                b = s // 2
                                if s % 2 == 0:
                                    dve.wait_ge(col_in[b], it * 16 + 16)
                                    split = it * (2 * HOTS) + b * HOTS
                                    dve.tensor_copy(w_part[0][:, b, :], col[:, b, 0, :]).then_inc(hot, 1)
                                    dve.wait_ge(hot, split + 1)
                                    dve.tensor_tensor(w_rest[:, b, :], col[:, b, 0, :], w_part[0][:, b, :], ALU.subtract).then_inc(hot, 1)
                                    dve.wait_ge(hot, split + 2)
                                    dve.tensor_copy(w_part[1][:, b, :], w_rest[:, b, :]).then_inc(hot, 1)
                                    dve.wait_ge(hot, split + 3)
                                    dve.tensor_tensor(w_part[2][:, b, :], w_rest[:, b, :], w_part[1][:, b, :], ALU.subtract).then_inc(hot, 1)
                                batch(it, b, 2 * (s % 2))
                                if more or s < GATE_E - 1:
                                    next_lo(step)
                                batch(it, b, 2 * (s % 2) + 1)

                        gate_body(0, True)
                        with dve.Fori(1, GATE_STEPS - 1) as it:
                            gate_body(it, True)
                        gate_body(GATE_STEPS - 1, False)

                    @block.tensor
                    def _(pe):
                        def transposes(i):
                            for k in range(KT):
                                last = pe.transpose(ps_t[:, k * P:(k + 1) * P], u_raw[:, i, k * P:(k + 1) * P], ident[:])
                            last.then_inc(tr_done, 1)

                        def next_transposes(step):
                            e, i, n, _ = step
                            pe.wait_ge(raw_in[1 - i], (n + i) * 16 + 16)
                            pe.wait_ge(uT_lo_done, e + 1)
                            transposes(1 - i)

                        def product(step, between):
                            e, i, n, _ = step
                            pe.wait_ge(uT_lo_done, e + 1)
                            pe.wait_ge(gelu_done[i], n)
                            q = 0
                            for c in range(2):
                                tok = slice(c * HALF, (c + 1) * HALF)
                                for k in range(KT):
                                    last = three(pe, ps_h[i][:, tok], uT_hi[:, i, k, :], uT_lo[:, i, k, :],
                                                 aT_hi[:, k, tok], aT_lo[:, k, tok], k == 0, k == KT - 1)
                                    if k == KT - 1 and c == 1:
                                        last.then_inc(mm_done, 1)
                                    if k % (KT // 2) == KT // 2 - 1:
                                        between(q)
                                        q += 1

                        pe.wait_ge(raw_in[0], 16)
                        transposes(0)

                        def route_body(it):
                            for s in range(ROUTE_E):
                                step = route_step(it, s)
                                u, i, _, _ = step
                                next_transposes(step)
                                product(step, lambda q: None)
                                pe.wait_ge(raw_in[0], 16)
                                pe.wait_ge(route_done, u + 1)
                                pe.wait_ge(rt_out, u - i)
                                pe.transpose(ps_x[i][0:3 * TOPK, 0:P], route[:, i, :, :].rearrange("p k q -> p (k q)"), ident[:]).then_inc(rt_done, 1)

                        route_body(0)
                        with pe.Fori(1, ROUTE_STEPS) as it:
                            route_body(it)
                        pe.wait_ge(rt_out, UNITS)

                        def gates(it, s, m, gh):
                            b, i = s // 2, m % 2
                            pe.wait_ge(hot_done[i], it * BATCHES + (b * (BATCHES // 2) + m // 2 + 1))
                            pe.wait_ge(last_done[i], it * BATCHES + (b * (BATCHES // 2) + m // 2 + 1))
                            pe.wait_ge(g_out[gh], it * (2 * BATCHES) + (b * BATCHES + m))
                            for t in range(GROUP):
                                at, tk = slice(t * P, (t + 1) * P), gh * GROUP + t
                                for c in range(3):
                                    last = pe.matmul(ps_x[gh][:, at], hot1[:, i, tk, :], hw[c][:, i, tk, :], start=c == 0, stop=c == 2)
                            last.then_inc(g_done[i][gh], 1)

                        def gate_body(it, more):
                            for s in range(GATE_E):
                                step = gate_step(it, s)
                                if more or s < GATE_E - 1:
                                    next_transposes(step)
                                product(step, lambda q: gates(it, s, 2 * (s % 2) + q // 2, q % 2))

                        gate_body(0, True)
                        with pe.Fori(1, GATE_STEPS - 1) as it:
                            gate_body(it, True)
                        gate_body(GATE_STEPS - 1, False)

        def expert_out_stage(gain, bias, resid, dest):
            GE = 4
            GROUPS = P // GE
            v_rows = expert_v.rearrange("(p e) d -> e p d", e=P)
            a_in = [sem(f"eo_a_in{i}") for i in range(2)]
            v_in = [sem(f"eo_v_in{i}") for i in range(2)]
            g_in = sem("eo_g_in")
            prod, a_hi_done, a_lo_done = sem("eo_prod"), sem("eo_a_hi"), sem("eo_a_lo")
            v_hi_done, v_lo_done = sem("eo_v_hi"), sem("eo_v_lo")
            mm_done = [sem(f"eo_mm{i}") for i in range(4)]
            added = [sem(f"eo_added{i}") for i in range(4)]
            row_in = [sem(f"eo_row_in{i}") for i in range(2)]
            sum_done, stored = sem("eo_sum"), sem("eo_stored")
            with ExitStack() as stage:
                sb, pb = local(stage)
                ln = RowNorm("eo_ln", sb, gain, bias)
                acc = sb("eo_acc", [P, TT, D])
                a_raw, v_raw = sb("eo_a_raw", [P, 2, T]), sb("eo_v_raw", [P, 2, D])
                row = v_raw
                g_raw = sb("eo_g_raw", [P, T // GBLK, GE, GBLK])
                a_hi, a_lo = sb("eo_a_hi_sb", [P, 2, GE, T], F32R), sb("eo_a_lo_sb", [P, 2, GE, T], F32R)
                v_hi, v_lo = sb("eo_v_hi_sb", [P, 2, GE, D], F32R), sb("eo_v_lo_sb", [P, 2, GE, D], F32R)
                ps = [pb(f"eo_ps{i}", D) for i in range(4)]

                with nc.Block() as block:
                    @block.sync
                    def _(sp):
                        def load_gates(q):
                            sp.wait_ge(prod, q * GE)
                            sp.dma_start(g_raw[:], gate_d[:, :, bass.ds(q * GE, GE), :].rearrange("n p e t -> p n e t")).then_inc(g_in, 16)

                        def store_row(j):
                            sp.wait_ge(ln.ln_done, j + 1)
                            sp.dma_start(dest[j * P:(j + 1) * P, :], acc[:, j, :]).then_inc(stored, 16)

                        def load_group(q, gates_at=2):
                            for j in range(GE):
                                e, i = q * GE + j, j % 2
                                if j == gates_at:
                                    load_gates(q)
                                if j >= 2:
                                    sp.wait_ge(a_lo_done, e - 1)
                                    sp.wait_ge(v_lo_done, e - 1)
                                else:
                                    sp.wait_ge(a_lo_done, e - j)
                                    sp.wait_ge(v_lo_done, e - j)
                                sp.dma_start(a_raw[:, i, :], act_d[e, :, :]).then_inc(a_in[i], 16)
                                sp.dma_start(v_raw[:, i, :], v_rows[e, :, :]).then_inc(v_in[i], 16)

                        load_group(0, gates_at=0)
                        load_group(1)
                        with sp.Fori(1, GROUPS // 2) as it:
                            for b in range(2):
                                load_group(it * 2 + b)
                        ln.load(sp)
                        sp.wait_ge(v_lo_done, P)
                        for j in range(TT):
                            if j >= 2:
                                sp.wait_ge(sum_done, j - 1)
                            sp.dma_start(row[:, j % 2, :], resid[j * P:(j + 1) * P, :]).then_inc(row_in[j % 2], 16)
                            if j >= 2:
                                store_row(j - 2)
                        store_row(TT - 2)
                        store_row(TT - 1)
                        sp.wait_ge(stored, 16 * TT)

                    @block.gpsimd
                    def _(pool):
                        with pool.Fori(0, GROUPS // 2) as it:
                            for b in range(2):
                                for j in range(GE):
                                    pool.wait_ge(v_hi_done, it * (2 * GE) + (b * GE + j + 1))
                                    pool.tensor_tensor(v_lo[:, b, j, :], v_raw[:, j % 2, :], v_hi[:, b, j, :], ALU.subtract).then_inc(v_lo_done, 1)
                        for j in range(TT):
                            ln.plus_bias(pool, j, acc[:, j, :])

                    @block.scalar
                    def _(act):
                        def split_group(it, b):
                            for j in range(GE):
                                e = it * (2 * GE) + (b * GE + j)
                                act.wait_ge(v_in[j % 2], it * (GE * 16) + (b * (GE // 2) + j // 2 + 1) * 16)
                                act.activation(v_hi[:, b, j, :], v_raw[:, j % 2, :], ACT.Copy).then_inc(v_hi_done, 1)
                                act.wait_ge(prod, e + 1)
                                act.activation(a_hi[:, b, j, :], a_raw[:, j % 2, :], ACT.Copy).then_inc(a_hi_done, 1)

                        split_group(0, 0)
                        def split_next(it):
                            act.wait_ge(mm_done[3], it * 4)
                            split_group(it, 1)
                            act.wait_ge(mm_done[3], it * 4 + 2)
                            split_group(it + 1, 0)

                        split_next(0)
                        with act.Fori(1, GROUPS // 2 - 1) as it:
                            split_next(it)
                        act.wait_ge(mm_done[3], (GROUPS // 2 - 1) * 4)
                        split_group(GROUPS // 2 - 1, 1)
                        for j in range(TT):
                            ln.square_root(act, j)
                            ln.normalise(act, j, acc[:, j, :])

                    @block.vector
                    def _(dve):
                        def multiply(it, b, j):
                            dve.wait_ge(a_in[j % 2], it * (GE * 16) + (b * (GE // 2) + j // 2 + 1) * 16)
                            if j == 0:
                                dve.wait_ge(g_in, it * 32 + (b + 1) * 16)
                            a = a_raw[:, j % 2, :].rearrange("p (n t) -> p n t", t=GBLK)
                            dve.tensor_tensor(a, a, g_raw[:, :, j, :], ALU.mult).then_inc(prod, 1)

                        def product_lo(it, b, j):
                            dve.wait_ge(a_hi_done, it * (2 * GE) + (b * GE + j + 1))
                            dve.tensor_tensor(a_lo[:, b, j, :], a_raw[:, j % 2, :], a_hi[:, b, j, :], ALU.subtract).then_inc(a_lo_done, 1)

                        def add(it, b, t, first=False):
                            n = it * 4 + (b * 2 + t // 4)
                            dve.wait_ge(mm_done[t % 4], n + 1)
                            if first:
                                dve.tensor_copy(acc[:, t, :], ps[t % 4][:]).then_inc(added[t % 4], 1)
                            else:
                                dve.tensor_tensor(acc[:, t, :], acc[:, t, :], ps[t % 4][:], ALU.add).then_inc(added[t % 4], 1)

                        for j in range(GE):
                            multiply(0, 0, j)
                            product_lo(0, 0, j)

                        def group_step(it, b, first=False):
                            ni, nb = (it, 1) if b == 0 else (it + 1, 0)
                            for j in range(GE):
                                multiply(ni, nb, j)
                                add(it, b, 2 * j, first)
                                product_lo(ni, nb, j)
                                add(it, b, 2 * j + 1, first)

                        group_step(0, 0, first=True)
                        group_step(0, 1)
                        with dve.Fori(1, GROUPS // 2 - 1) as it:
                            group_step(it, 0)
                            group_step(it, 1)
                        group_step(GROUPS // 2 - 1, 0)
                        for j in range(TT):
                            add(GROUPS // 2 - 1, 1, j)
                            dve.wait_ge(added[j % 4], GROUPS * 2 - 1 + j // 4)
                            dve.wait_ge(row_in[j % 2], 16 * (j // 2 + 1))
                            dve.scalar_tensor_tensor(acc[:, j, :], row[:, j % 2, :], ALPHA, acc[:, j, :], ALU.mult, ALU.add).then_inc(sum_done, 1)
                            dve.wait_ge(sum_done, j + 1)
                            ln.statistics(dve, j, acc[:, j, :])
                            if j >= 1:
                                ln.times_gain(dve, j - 1, acc[:, j - 1, :])
                            ln.scale(dve, j)
                        ln.times_gain(dve, TT - 1, acc[:, TT - 1, :])

                    @block.tensor
                    def _(pe):
                        def sum_groups(it):
                            for b in range(2):
                                for t in range(TT):
                                    if t == 0:
                                        pe.wait_ge(a_lo_done, it * (2 * GE) + (b + 1) * GE)
                                        pe.wait_ge(v_lo_done, it * (2 * GE) + (b + 1) * GE)
                                    pe.wait_ge(added[t % 4], it * 4 + (b * 2 + t // 4))
                                    tok = slice(t * P, (t + 1) * P)
                                    for c in range(2):
                                        colc = slice(c * HALF, (c + 1) * HALF)
                                        for j in range(GE):
                                            last = three(pe, ps[t % 4][:, colc], a_hi[:, b, j, tok], a_lo[:, b, j, tok],
                                                         v_hi[:, b, j, colc], v_lo[:, b, j, colc], j == 0, j == GE - 1)
                                    last.then_inc(mm_done[t % 4], 1)

                        sum_groups(0)
                        with pe.Fori(1, GROUPS // 2) as it:
                            sum_groups(it)

        norm_stage("n0", ln_in_g, ln_in_b, x, h0_d)
        free_sems()
        project_stage("pin", w_in, [(u_d, "gelu", 1.0), (v_d, "gelu", 1.0), (qb_d, "feat", float(B_HD) ** -0.5),
                                    (kb_d, "feat", 1.0), (vb_d, "tok", 1.0)], gated=True)
        free_sems()
        attention_stage()
        free_sems()
        norm_stage("n1", ln1_g, ln1_b, h0_d, h1_d, weight=w_out)
        with ExitStack() as memory:
            msb, _ = local(memory)
            mk_hi, mk_lo = msb("mk_hi", [P, KT, MEM], F32R), msb("mk_lo", [P, KT, MEM], F32R)
            mv_hi, mv_lo = msb("mv_hi", [P, MT, D], F32R), msb("mv_lo", [P, MT, D], F32R)
            memory_stage(mk_hi, mk_lo, mv_hi, mv_lo)
            free_sems()
            project_stage("pxq", w_xq, [(xq_d[0:HALF, :], "feat", 1.0), (xq_d[HALF:D, :], "feat", 1.0)])
            cross_stage(mk_hi, mk_lo, mv_hi, mv_lo)
        free_sems()
        norm_stage("n2", ln2_g, ln2_b, h1_d, h2_d, weight=w_xo)
        free_sems()
        key_score_stage()
        free_sems()
        expert_in_stage()
        act_stack.close()
        free_sems()
        expert_out_stage(ln3_g, ln3_b, h2_d, out)


_INS = ["x", "mem", "ln_in_g", "ln_in_b", "w_in", "gate_ln_g", "gate_ln_b", "w_sp", "b_sp", "rel_bias", "w_out",
        "ln1_g", "ln1_b", "w_xq", "w_xk", "w_xv", "w_xo", "ln2_g", "ln2_b", "w_pq", "sub_keys", "expert_u",
        "expert_v", "ln3_g", "ln3_b"]


def kernel(**inputs):
    import numpy as _np
    import concourse.bacc as _bacc
    from concourse import mybir as _mybir
    from concourse.bass_utils import run_bass_kernel_spmd as _run

    nc = _bacc.Bacc("TRN2", target_bir_lowering=False, num_devices=1)
    arrays, args = {}, []
    for name in _INS:
        a = _np.asarray(inputs[name])
        if name != "ln_in_g" and name != "ln_in_b":
            a = a[0]
        a = _np.ascontiguousarray(a)
        arrays[f"in_{name}"] = a
        args.append(nc.dram_tensor(f"in_{name}", a.shape, _mybir.dt.from_np(a.dtype), kind="ExternalInput").ap())
    out = nc.dram_tensor("out_0", (T, D), F32, kind="ExternalOutput").ap()
    layer_program(nc, *args, out)
    r = _run(nc, [arrays], core_ids=[0])
    return r.results[0]["out_0"].reshape(1, T, D)
```
